# Optimizing a Trainium2 kernel written in Bass

```python
import jax, jax.numpy as jnp
from jax import lax
import numpy as np
import math

D_MODEL = 2048
BATCH = 1
SEQ = 256
DEPTH = 1

D_A = D_MODEL // 2
HEAD_SIZE = 64
N_HEADS_A = D_A // HEAD_SIZE
LORA_W = 64
LORA_A = 64
D_B = D_MODEL // 2
CONV_GROUPS = 16
CONV_WIDTH = 3
N_BRANCH = 2
RMS_EPS = 1e-6
GN_EPS = 64e-5

COLS_A = 3 * D_A + LORA_W + LORA_A
OFF_ZA = COLS_A
OFF_B = OFF_ZA + D_A
OFF_GATE = OFF_B + 4 * D_B
N_IN = OFF_GATE + N_BRANCH * D_MODEL


def rms_norm(x, g):
    xf = x.astype(jnp.float32)
    y = xf * lax.rsqrt(jnp.mean(xf * xf, axis=-1, keepdims=True) + RMS_EPS)
    return (y * g.astype(jnp.float32)).astype(x.dtype)

def shift_time(u, n):
    return jnp.pad(u, ((0, 0), (n, 0), (0, 0)))[:, : u.shape[1]]

def wkv7_scan(r, decay, k, v, kk, b):
    def step(S, inp):
        r_t, w_t, k_t, v_t, kk_t, b_t = inp
        sa = jnp.einsum('bhvk,bhk->bhv', S, -kk_t)
        S = (S * w_t[:, :, None, :]
             + sa[..., None] * b_t[:, :, None, :]
             + v_t[..., None] * k_t[:, :, None, :])
        y_t = jnp.einsum('bhvk,bhk->bhv', S, r_t)
        return S, y_t
    xs = (jnp.swapaxes(r, 0, 1), jnp.swapaxes(decay, 0, 1), jnp.swapaxes(k, 0, 1),
          jnp.swapaxes(v, 0, 1), jnp.swapaxes(kk, 0, 1), jnp.swapaxes(b, 0, 1))
    bsz, _, nh, n = r.shape
    S0 = jnp.zeros((bsz, nh, n, n), jnp.float32)
    _, y = lax.scan(step, S0, xs)
    return jnp.swapaxes(y, 0, 1)

def rwkv7_mix(pa, w0, w2, a0, a2, k_k, k_a, r_k, lnx_g, lnx_b):
    bsz, t, _ = pa.shape
    pa = pa.astype(jnp.float32)
    r = pa[..., :D_A]
    k = pa[..., D_A:2 * D_A]
    v = pa[..., 2 * D_A:3 * D_A]
    xw = pa[..., 3 * D_A:3 * D_A + LORA_W]
    xa = pa[..., 3 * D_A + LORA_W:]
    f = lambda p: p.astype(jnp.float32)
    w_log = -jax.nn.softplus(-(f(w0) + jnp.tanh(xw) @ f(w2))) - 0.5
    decay = jnp.exp(-jnp.exp(w_log))
    a = jax.nn.sigmoid(f(a0) + xa @ f(a2))
    hs = (bsz, t, N_HEADS_A, HEAD_SIZE)
    kk = (k * f(k_k)).reshape(hs)
    kk = kk / jnp.maximum(jnp.sqrt(jnp.sum(kk * kk, axis=-1, keepdims=True)), 1e-12)
    k = k * (1.0 + (a - 1.0) * f(k_a))
    r_h, k_h, v_h = r.reshape(hs), k.reshape(hs), v.reshape(hs)
    b_h = kk * a.reshape(hs)
    y = wkv7_scan(r_h, decay.reshape(hs), k_h, v_h, kk, b_h)
    mu = jnp.mean(y, axis=-1, keepdims=True)
    var = jnp.mean(jnp.square(y - mu), axis=-1, keepdims=True)
    y = ((y - mu) * lax.rsqrt(var + GN_EPS)).reshape(bsz, t, D_A) * f(lnx_g) + f(lnx_b)
    bonus = jnp.sum(r_h * k_h * f(r_k), axis=-1, keepdims=True) * v_h
    return y + bonus.reshape(bsz, t, D_A)

def short_conv_mix(pb, conv_w):
    bg = pb[..., :D_B]
    cg = pb[..., D_B:2 * D_B]
    hb = pb[..., 2 * D_B:]
    u = cg * hb
    y = conv_w[0] * shift_time(u, 2) + conv_w[1] * shift_time(u, 1) + conv_w[2] * u
    return bg * y

def first_inputs(seed: int = 0) -> dict:
    key = jax.random.key(seed)
    ks = jax.random.split(key, 24)
    L, D = DEPTH, D_MODEL
    nrm = lambda k, s, sc: jax.random.normal(k, s, jnp.float32) * sc
    return {
        "x": nrm(ks[0], (BATCH, SEQ, D), 1.0),
        "c": nrm(ks[1], (BATCH, D), 1.0),
        "ada_w": nrm(ks[2], (L, D, 3 * D), 0.5 * D ** -0.5),
        "ada_b": nrm(ks[3], (L, 3 * D), 0.01),
        "pre_gain": 1.0 + nrm(ks[4], (L, D), 0.05),
        "post_gain": 1.0 + nrm(ks[5], (L, D), 0.05),
        "w_in": nrm(ks[6], (L, D, N_IN), D ** -0.5),
        "mu_shift": jax.random.uniform(ks[7], (L, COLS_A), jnp.float32),
        "w0": nrm(ks[8], (L, D_A), 1.0),
        "w2": nrm(ks[9], (L, LORA_W, D_A), 0.5 * LORA_W ** -0.5),
        "a0": nrm(ks[10], (L, D_A), 0.5),
        "a2": nrm(ks[11], (L, LORA_A, D_A), 0.5 * LORA_A ** -0.5),
        "k_k": 0.85 + nrm(ks[12], (L, D_A), 0.05),
        "k_a": 1.0 + nrm(ks[13], (L, D_A), 0.05),
        "r_k": nrm(ks[14], (L, N_HEADS_A, HEAD_SIZE), 0.1),
        "lnx_gain": 1.0 + nrm(ks[15], (L, D_A), 0.05),
        "lnx_bias": nrm(ks[16], (L, D_A), 0.01),
        "conv_w": nrm(ks[17], (L, CONV_WIDTH, D_B), CONV_WIDTH ** -0.5),
        "p_a": nrm(ks[18], (L, D_A, D), D_A ** -0.5),
        "p_b": nrm(ks[19], (L, D_B, D), D_B ** -0.5),
        "w_out": nrm(ks[20], (L, D, D), D ** -0.5),
    }

def first_block(x, c, ada_w, ada_b, pre_gain, post_gain, w_in, mu_shift, w0, w2, a0, a2,
              k_k, k_a, r_k, lnx_gain, lnx_bias, conv_w, p_a, p_b, w_out):
    D = D_MODEL
    c_act = jax.nn.silu(c)
    for l in range(DEPTH):
        mod = c_act @ ada_w[l] + ada_b[l]
        shift = mod[:, None, :D]
        scale = mod[:, None, D:2 * D]
        gate = mod[:, None, 2 * D:]
        h = rms_norm(x, pre_gain[l]) * (1.0 + scale) + shift
        proj = h @ w_in[l]
        pa = proj[..., :COLS_A]
        pa = pa + (shift_time(pa, 1) - pa) * mu_shift[l]
        z_a = proj[..., OFF_ZA:OFF_B]
        pb = proj[..., OFF_B:OFF_B + 3 * D_B]
        z_b = proj[..., OFF_B + 3 * D_B:OFF_GATE]
        g_a = proj[..., OFF_GATE:OFF_GATE + D]
        g_b = proj[..., OFF_GATE + D:]
        y_a = rwkv7_mix(pa, w0[l], w2[l], a0[l], a2[l], k_k[l], k_a[l], r_k[l],
                        lnx_gain[l], lnx_bias[l]).astype(x.dtype)
        y_a = (y_a * jax.nn.silu(z_a)) @ p_a[l]
        y_b = (short_conv_mix(pb, conv_w[l]) * jax.nn.silu(z_b)) @ p_b[l]
        m = jax.nn.sigmoid(g_a) * y_a + jax.nn.sigmoid(g_b) * y_b
        o = m @ w_out[l]
        x = x + gate * rms_norm(o, post_gain[l])
    return x


D_MIX = D_MODEL
D_HYENA = D_MIX // 2
D_ATTN = D_MIX - D_HYENA
N_DIFF_HEADS = 8
DIFF_HEAD_DIM = D_ATTN // (2 * N_DIFF_HEADS)
VAL_DIM = 2 * DIFF_HEAD_DIM
D_QK = 2 * N_DIFF_HEADS * DIFF_HEAD_DIM
D_IN = 3 * D_HYENA + 2 * D_QK + N_DIFF_HEADS * VAL_DIM
ROT_DIM = DIFF_HEAD_DIM // 4
ROPE_THETA = 500000.0
Q_BLOCK = 128
HYENA_ORDER = 2
SHORT_CONV = 3
FILTER_EMB = 33
FILTER_HIDDEN = 64
N_DIRS = 2
DECAY_TARGET = 1e-2
FAST_DECAY_PCT = 0.3
SLOW_DECAY_PCT = 1.5
MIN_DECAY = math.log(DECAY_TARGET) / SLOW_DECAY_PCT
MAX_DECAY = math.log(DECAY_TARGET) / FAST_DECAY_PCT
D_FF = 5632
LN_EPS = 1e-5
ALPHA = (2.0 * DEPTH) ** 0.25
BETA = (8.0 * DEPTH) ** -0.25


def lambda_init_for(layer_idx):
    return 0.8 - 0.6 * math.exp(-0.3 * (layer_idx - 1))

def layer_norm(x, g, b):
    xf = x.astype(jnp.float32)
    mu = jnp.mean(xf, axis=-1, keepdims=True)
    var = jnp.mean(jnp.square(xf - mu), axis=-1, keepdims=True)
    return ((xf - mu) * lax.rsqrt(var + LN_EPS)).astype(x.dtype) * g + b

def rms_norm_2(x, g):
    xf = x.astype(jnp.float32)
    return (xf * lax.rsqrt(jnp.mean(jnp.square(xf), axis=-1, keepdims=True) + LN_EPS)).astype(x.dtype) * g

def swiglu(x, w_gate, w_up, w_down):
    return (jax.nn.silu(x @ w_gate) * (x @ w_up)) @ w_down

def short_conv(u, w, b):
    L = u.shape[1]
    up = jnp.pad(u, ((0, 0), (1, 1), (0, 0)))
    return up[:, :L] * w[0] + up[:, 1:L + 1] * w[1] + up[:, 2:] * w[2] + b

def hyena_filters(L, w1, b1, w2, b2, w3, b3, freq, w_out):
    t = jnp.linspace(0.0, 1.0, L, dtype=jnp.float32)[:, None]
    bands = (FILTER_EMB - 1) // 2
    w = 2.0 * math.pi * jnp.arange(L, dtype=jnp.float32)[:, None] / L
    f = jnp.linspace(1e-4, bands - 1, bands, dtype=jnp.float32)[None, :]
    z = jnp.concatenate([t, jnp.cos(f * w), -jnp.sin(f * w)], axis=-1)
    h = jnp.sin(freq * (z @ w1 + b1))
    h = jnp.sin(freq * (h @ w2 + b2))
    h = jnp.sin(freq * (h @ w3 + b3))
    h = (h @ w_out).astype(jnp.float32)
    deltas = jnp.abs(jnp.linspace(MIN_DECAY, MAX_DECAY, D_HYENA, dtype=jnp.float32))
    decay = jnp.exp(-t * deltas)
    return h.reshape(L, HYENA_ORDER, N_DIRS, D_HYENA) * decay[:, None, None, :]

def bidir_fftconv(u, h_fwd, h_bwd, bias):
    L = u.shape[1]
    k = jnp.concatenate([h_fwd, jnp.zeros_like(h_fwd[:1]), h_bwd[:0:-1]], axis=0)
    k_f = jnp.fft.rfft(k, n=2 * L, axis=0)
    u_f = jnp.fft.rfft(u.astype(jnp.float32), n=2 * L, axis=1)
    y = jnp.fft.irfft(u_f * k_f[None], n=2 * L, axis=1)[:, :L]
    return (y + u.astype(jnp.float32) * bias.astype(jnp.float32)).astype(u.dtype)

def hyena_group(p_hy, conv_w, conv_b, fw1, fb1, fw2, fb2, fw3, fb3, ffreq, fw_out, hyena_bias, hyena_norm_g):
    L = p_hy.shape[1]
    z = short_conv(p_hy, conv_w, conv_b)
    v, g1, g2 = jnp.split(z, 3, axis=-1)
    filt = hyena_filters(L, fw1, fb1, fw2, fb2, fw3, fb3, ffreq, fw_out)
    gates = (g1, g2)
    y = v
    for n in range(HYENA_ORDER):
        y = gates[n] * bidir_fftconv(y, filt[:, n, 0], filt[:, n, 1], hyena_bias[n])
    return rms_norm_2(y, hyena_norm_g)

def partial_rope(x, pos):
    half = ROT_DIM // 2
    inv = ROPE_THETA ** (-jnp.arange(0, ROT_DIM, 2, dtype=jnp.float32) / ROT_DIM)
    ang = pos[:, None] * inv[None, :]
    cos = jnp.concatenate([jnp.cos(ang), jnp.cos(ang)], axis=-1)[None, :, None, None, :]
    sin = jnp.concatenate([jnp.sin(ang), jnp.sin(ang)], axis=-1)[None, :, None, None, :]
    xr = x[..., :ROT_DIM].astype(jnp.float32)
    rot = jnp.concatenate([-xr[..., half:], xr[..., :half]], axis=-1)
    xr = (xr * cos + rot * sin).astype(x.dtype)
    return jnp.concatenate([xr, x[..., ROT_DIM:]], axis=-1)

def diff_attention_group(p_q, p_k, p_v, lq1, lk1, lq2, lk2, subln_g, lambda_init):
    B, L, _ = p_q.shape
    nb = L // Q_BLOCK
    pos = jnp.arange(L, dtype=jnp.float32)
    q = partial_rope(p_q.reshape(B, L, N_DIFF_HEADS, 2, DIFF_HEAD_DIM), pos) * (DIFF_HEAD_DIM ** -0.5)
    k = partial_rope(p_k.reshape(B, L, N_DIFF_HEADS, 2, DIFF_HEAD_DIM), pos)
    v = p_v.reshape(B, L, N_DIFF_HEADS, VAL_DIM)
    lam = (jnp.exp(jnp.sum(lq1.astype(jnp.float32) * lk1.astype(jnp.float32)))
           - jnp.exp(jnp.sum(lq2.astype(jnp.float32) * lk2.astype(jnp.float32))) + lambda_init)
    qb = q.reshape(B, nb, Q_BLOCK, N_DIFF_HEADS, 2, DIFF_HEAD_DIM).transpose(1, 0, 3, 4, 2, 5)
    kt = k.transpose(0, 2, 3, 1, 4)
    vt = v.transpose(0, 2, 1, 3)

    def block(q_blk):
        s = jnp.einsum('bhmqd,bhmkd->bhmqk', q_blk, kt).astype(jnp.float32)
        a = jax.nn.softmax(s, axis=-1)
        w = a[:, :, 0] - lam * a[:, :, 1]
        return jnp.einsum('bhqk,bhkv->bhqv', w.astype(vt.dtype), vt)

    o = lax.map(block, qb)
    o = o.transpose(1, 0, 3, 2, 4).reshape(B, L, N_DIFF_HEADS, VAL_DIM)
    o = rms_norm_2(o, subln_g) * (1.0 - lambda_init)
    return o.reshape(B, L, D_ATTN)

def hybrid_mixer(h, w_in, conv_w, conv_b, fw1, fb1, fw2, fb2, fw3, fb3, ffreq, fw_out,
                 hyena_bias, hyena_norm_g, lq1, lk1, lq2, lk2, subln_g, w_out, lambda_init):
    proj = h @ w_in
    s1 = 3 * D_HYENA
    p_hy, p_q, p_k, p_v = jnp.split(proj, [s1, s1 + D_QK, s1 + 2 * D_QK], axis=-1)
    y_hy = hyena_group(p_hy, conv_w, conv_b, fw1, fb1, fw2, fb2, fw3, fb3, ffreq, fw_out,
                       hyena_bias, hyena_norm_g)
    y_at = diff_attention_group(p_q, p_k, p_v, lq1, lk1, lq2, lk2, subln_g, lambda_init)
    return jnp.concatenate([y_hy, y_at], axis=-1) @ w_out

def second_inputs(seed: int = 0) -> dict:
    key = jax.random.key(seed)
    ks = iter(jax.random.split(key, 40))

    def nrm(shape, scale):
        return jax.random.normal(next(ks), shape, jnp.float32) * scale

    def gain(shape):
        return 1.0 + nrm(shape, 0.05)

    n = DEPTH
    return {
        "x": nrm((BATCH, SEQ, D_MODEL), 1.0),
        "ffn1_w_gate": nrm((n, D_MODEL, D_FF), D_MODEL ** -0.5),
        "ffn1_w_up": nrm((n, D_MODEL, D_FF), D_MODEL ** -0.5),
        "ffn1_w_down": nrm((n, D_FF, D_MODEL), BETA * D_FF ** -0.5),
        "ln1_g": gain((n, D_MODEL)),
        "ln1_b": nrm((n, D_MODEL), 0.02),
        "w_in": nrm((n, D_MODEL, D_IN), D_MODEL ** -0.5),
        "hyena_conv_w": nrm((n, SHORT_CONV, 3 * D_HYENA), 0.5),
        "hyena_conv_b": nrm((n, 3 * D_HYENA), 0.02),
        "filt_w1": nrm((n, FILTER_EMB, FILTER_HIDDEN), FILTER_EMB ** -0.5),
        "filt_b1": nrm((n, FILTER_HIDDEN), 0.1),
        "filt_w2": nrm((n, FILTER_HIDDEN, FILTER_HIDDEN), FILTER_HIDDEN ** -0.5),
        "filt_b2": nrm((n, FILTER_HIDDEN), 0.1),
        "filt_w3": nrm((n, FILTER_HIDDEN, FILTER_HIDDEN), FILTER_HIDDEN ** -0.5),
        "filt_b3": nrm((n, FILTER_HIDDEN), 0.1),
        "filt_freq": gain((n, FILTER_HIDDEN)),
        "filt_w_out": nrm((n, FILTER_HIDDEN, HYENA_ORDER * N_DIRS * D_HYENA), FILTER_HIDDEN ** -0.5),
        "hyena_bias": nrm((n, HYENA_ORDER, D_HYENA), 0.5),
        "hyena_norm_g": gain((n, D_HYENA)),
        "lambda_q1": nrm((n, DIFF_HEAD_DIM), 0.1),
        "lambda_k1": nrm((n, DIFF_HEAD_DIM), 0.1),
        "lambda_q2": nrm((n, DIFF_HEAD_DIM), 0.1),
        "lambda_k2": nrm((n, DIFF_HEAD_DIM), 0.1),
        "subln_g": gain((n, VAL_DIM)),
        "w_out": nrm((n, D_MIX, D_MODEL), BETA * D_MIX ** -0.5),
        "ln2_g": gain((n, D_MODEL)),
        "ln2_b": nrm((n, D_MODEL), 0.02),
        "ffn2_w_gate": nrm((n, D_MODEL, D_FF), D_MODEL ** -0.5),
        "ffn2_w_up": nrm((n, D_MODEL, D_FF), D_MODEL ** -0.5),
        "ffn2_w_down": nrm((n, D_FF, D_MODEL), BETA * D_FF ** -0.5),
        "ln3_g": gain((n, D_MODEL)),
        "ln3_b": nrm((n, D_MODEL), 0.02),
    }

def second_block(x, ffn1_w_gate, ffn1_w_up, ffn1_w_down, ln1_g, ln1_b, w_in, hyena_conv_w, hyena_conv_b,
              filt_w1, filt_b1, filt_w2, filt_b2, filt_w3, filt_b3, filt_freq, filt_w_out, hyena_bias,
              hyena_norm_g, lambda_q1, lambda_k1, lambda_q2, lambda_k2, subln_g, w_out, ln2_g, ln2_b,
              ffn2_w_gate, ffn2_w_up, ffn2_w_down, ln3_g, ln3_b):
    for i in range(DEPTH):
        lam_init = lambda_init_for(i + 1)
        x = layer_norm(ALPHA * x + 0.5 * swiglu(x, ffn1_w_gate[i], ffn1_w_up[i], ffn1_w_down[i]),
                       ln1_g[i], ln1_b[i])
        y = hybrid_mixer(x, w_in[i], hyena_conv_w[i], hyena_conv_b[i], filt_w1[i], filt_b1[i],
                         filt_w2[i], filt_b2[i], filt_w3[i], filt_b3[i], filt_freq[i], filt_w_out[i],
                         hyena_bias[i], hyena_norm_g[i], lambda_q1[i], lambda_k1[i], lambda_q2[i],
                         lambda_k2[i], subln_g[i], w_out[i], lam_init)
        x = layer_norm(ALPHA * x + y, ln2_g[i], ln2_b[i])
        x = layer_norm(ALPHA * x + 0.5 * swiglu(x, ffn2_w_gate[i], ffn2_w_up[i], ffn2_w_down[i]),
                       ln3_g[i], ln3_b[i])
    return x


def setup_inputs(seed=0):
    out = dict(first_inputs(seed))
    for name, value in second_inputs(seed + 1).items():
        if name != "x":
            out[name + "_2"] = value
    return out


def reference(
    x, c, ada_w, ada_b, pre_gain, post_gain, w_in, mu_shift, w0, w2, a0, a2, k_k, k_a, r_k,
    lnx_gain, lnx_bias, conv_w, p_a, p_b, w_out, ffn1_w_gate_2, ffn1_w_up_2, ffn1_w_down_2,
    ln1_g_2, ln1_b_2, w_in_2, hyena_conv_w_2, hyena_conv_b_2, filt_w1_2, filt_b1_2, filt_w2_2,
    filt_b2_2, filt_w3_2, filt_b3_2, filt_freq_2, filt_w_out_2, hyena_bias_2, hyena_norm_g_2,
    lambda_q1_2, lambda_k1_2, lambda_q2_2, lambda_k2_2, subln_g_2, w_out_2, ln2_g_2, ln2_b_2,
    ffn2_w_gate_2, ffn2_w_up_2, ffn2_w_down_2, ln3_g_2, ln3_b_2,
):
    x = first_block(
        x, c, ada_w, ada_b, pre_gain, post_gain, w_in, mu_shift, w0, w2, a0, a2, k_k, k_a, r_k,
        lnx_gain, lnx_bias, conv_w, p_a, p_b, w_out,
    )
    return second_block(
        x, ffn1_w_gate_2, ffn1_w_up_2, ffn1_w_down_2, ln1_g_2, ln1_b_2, w_in_2, hyena_conv_w_2,
        hyena_conv_b_2, filt_w1_2, filt_b1_2, filt_w2_2, filt_b2_2, filt_w3_2, filt_b3_2,
        filt_freq_2, filt_w_out_2, hyena_bias_2, hyena_norm_g_2, lambda_q1_2, lambda_k1_2,
        lambda_q2_2, lambda_k2_2, subln_g_2, w_out_2, ln2_g_2, ln2_b_2, ffn2_w_gate_2,
        ffn2_w_up_2, ffn2_w_down_2, ln3_g_2, ln3_b_2,
    )


_drawn_inputs = setup_inputs


def setup_inputs(seed=0):
    import zlib

    import numpy as np

    out = dict(_drawn_inputs(seed))
    spreads = {}
    factors = {'ada_b': 3.705,
     'post_gain': 3.101,
     'w2': 3.316,
     'k_k': 8.0,
     'k_a': 3.841,
     'lnx_gain': 5.289,
     'lnx_bias': 8.0,
     'hyena_norm_g_2': 3.64,
     'lambda_q1_2': 4.078,
     'lambda_k1_2': 8.0,
     'lambda_k2_2': 8.0,
     'subln_g_2': 4.487,
     'ln2_b_2': 2.816,
     'ln3_b_2': 2.87}
    for name, (base, spread) in spreads.items():
        noise = np.random.default_rng([zlib.crc32(name.encode()), seed]).standard_normal(out[name].shape)
        drawn = base * np.exp(spread * noise) if base else spread * noise
        out[name] = __import__('jax').numpy.asarray(drawn.astype(out[name].dtype))
    for name, factor in factors.items():
        out[name] = (out[name] * factor).astype(out[name].dtype)
    return out
```

```python
from contextlib import ExitStack
import math

import numpy as np
import concourse.bass as bass
from concourse import mybir

F32 = mybir.dt.float32
F32R = mybir.dt.float32r
ALU = mybir.AluOpType
ACT = mybir.ActivationFunctionType
AX = mybir.AxisListType
ds = bass.ds

P = 128
T = 256
TT = T // P
D = 2048
KT = D // P
NB = 512
DA = 1024
HP = DA // P
LORA = 64
COLS_A = 3 * DA + 2 * LORA
OFF_ZA = COLS_A
OFF_B = OFF_ZA + DA
OFF_ZB = OFF_B + 3 * DA
OFF_GATE = OFF_B + 4 * DA
N_IN = OFF_GATE + 2 * D
F = 5632
FB = F // NB
D_IN = 6144
RMS_EPS = 1e-6
GN_EPS = 64e-5
LN_EPS = 1e-5
ALPHA = 2.0 ** 0.25
LAMBDA_INIT = 0.8 - 0.6 * math.exp(0.0)
CH = 64
NCH = T // CH
PARAM_ROWS = 8
TWO_PI_HI = 6.28125
TWO_PI_LO = 2.0 * math.pi - TWO_PI_HI
ROUND = 1.5 * 2.0 ** 23
PI_IN = 3.1415925

H_LORA = 0
H_FIRST = H_LORA + 2
H_IN = H_FIRST + 16
IN_BLOCKS = (N_IN - 2 * LORA) // NB
H_PAB = H_IN + 8 * (IN_BLOCKS - 2)
H_OUT = H_PAB + 4 * 8
H_FFN1 = H_OUT + 4 * 8
FFN_HALVES = 8 + 8 + 4 * 2
H_IN2 = H_FFN1 + FB * FFN_HALVES
H_OUT2 = H_IN2 + 8 * (D_IN // NB)
H_FFN2 = H_OUT2 + 4 * 8
H_END = H_FFN2 + FB * FFN_HALVES

B_LORA = 0
B_FIRST = 1
B_IN = B_FIRST + 2
B_PAB = B_IN + IN_BLOCKS - 2
B_OUT = B_PAB + 8
B_FFN1 = B_OUT + 4
B_IN2 = B_FFN1 + FB * 6
B_OUT2 = B_IN2 + D_IN // NB
B_FFN2 = B_OUT2 + 4


def build(nc, A, out):
    ctx = ExitStack()
    with ctx:
        def sb(name, shape, dt=F32):
            return ctx.enter_context(nc.sbuf_tensor(name, shape, dt))

        def sem(name):
            return ctx.enter_context(nc.semaphore(name))

        raw = sb("w_raw", [P, 4, 4 * NB])
        whi = sb("w_hi", [P, 4, 2 * NB], F32R)
        wlo = sb("w_lo", [P, 4, 2 * NB], F32R)
        ahi = sb("act_hi", [P, KT, T], F32R)
        alo = sb("act_lo", [P, KT, T], F32R)
        ghi = sb("hid_hi", [P, 4, T], F32R)
        glo = sb("hid_lo", [P, 4, T], F32R)
        ident = sb("ident", [P, P])
        ones = sb("ones", [P, P])
        small = sb("small", [P, 128])
        arena = sb("arena", [P, 25600])
        ps = ctx.enter_context(nc.psum_tensor("ps", [P, 8, NB], F32))

        def at(off, *dims):
            v = arena[:, off:off + math.prod(dims)]
            if len(dims) == 1:
                return v
            names = " ".join("abcd"[:len(dims)])
            return v.rearrange(f"p ({names}) -> p {names}", **dict(zip("abcd", dims)))

        def acc(block):
            b = 2 * (block % 2)
            return ps[:, b:b + 2, :]

        def tp(n):
            return ps[:, 4 + n, :]

        XRES = at(0, TT, D)
        SRC = at(4096, TT, D)
        SUM = at(8192, TT, D)
        STG = at(12288, 2, TT, NB)
        R5 = 14336

        proj1 = nc.dram_tensor("proj1", [T + 2, N_IN], F32).ap()
        proj2 = nc.dram_tensor("proj2", [T + 2, D_IN], F32).ap()
        wkv_out = nc.dram_tensor("wkv_out", [T, DA], F32).ap()
        filt = nc.dram_tensor("filt", [2, 2, P, 4 * NB], F32).ap()
        mod_gate = nc.dram_tensor("mod_gate", [1, D], F32).ap()
        hy_out = nc.dram_tensor("hy_out", [T, DA], F32).ap()

        def wait_alone(eng, semaphore, value):
            eng.wait_ge(semaphore, value)
            eng.sem_inc(waits_done, 1)

        def tokens(ap):
            return ap.rearrange("(t p) n -> p t n", p=P)

        def rows(ap, n):
            return ap.partition_broadcast(n)

        raw_in = [sem(f"raw_in{n}") for n in range(4)]
        hi_ready = sem("hi_ready")
        lo_ready = sem("lo_ready")
        half_done = sem("half_done")
        acc_free = [sem(f"acc_free{n}") for n in range(2)]
        tp_ready = sem("tp_ready")
        tp_hi = sem("tp_hi")
        tp_lo = sem("tp_lo")
        stg_ready = sem("stg_ready")
        stg_out = [sem(f"stg_out{n}") for n in range(2)]
        s_const = sem("s_const")
        s_rows = sem("s_rows")
        s_ones = sem("s_ones")
        waits_done = sem("waits_done")
        ada_in = [sem(f"ada_in{n}") for n in range(4)]
        ada_done = sem("ada_done")
        rows_t = sem("rows_t")
        c_sig = sem("c_sig")
        c_act = sem("c_act")
        mod_cols = sem("mod_cols")
        mod_row = sem("mod_row")
        mod_row_sb = sem("mod_row_sb")
        mod_stored = sem("mod_stored")
        mod_scale = sem("mod_scale")
        x_in = sem("x_in")
        x_norm = sem("x_norm")
        f_in = sem("f_in")
        f_mlp = sem("f_mlp")
        f_arg = sem("f_arg")
        f_sin = sem("f_sin")
        f_h = sem("f_h")
        f_sd = sem("f_sd")
        f_sd0 = sem("f_sd0")
        f_k = sem("f_k")
        f_ke = sem("f_ke")
        f_dec = sem("f_dec")
        f_st = sem("f_st")
        zero_rows = sem("zero_rows")
        zero_st = sem("zero_st")


        def load_chunk(sp, i, per, h, src):
            slot = h // 2 % 4
            if h >= 8:
                sp.wait_ge(lo_ready, i * per + (h - 8 + 2))
            else:
                sp.wait_ge(ada_done, 44 + h // 2 + 1)
            dst = raw[:, slot, :].rearrange("p (k n) -> p k n", n=src.shape[-1])
            sp.dma_start(dst, src).then_inc(raw_in[slot], 16)

        def split_hi(act, i, per, h):
            if h >= H_END:
                return
            slot = h // 2 % 4
            if h % 2 == 0:
                act.wait_ge(raw_in[slot], i * (per * 2) + 16 * (h // 8 + 1))
            if h >= 4:
                act.wait_ge(half_done, i * per + (h - 4 + 1))
            act.activation(whi[:, h % 4, :], raw[:, slot, h % 2 * 2 * NB:(h % 2 + 1) * 2 * NB], ACT.Copy)\
               .then_inc(hi_ready, 1)

        def split_lo(dve, i, per, h):
            if h >= H_END:
                return
            dve.wait_ge(hi_ready, i * per + (h + 1))
            dve.tensor_tensor(wlo[:, h % 4, :], raw[:, h // 2 % 4, h % 2 * 2 * NB:(h % 2 + 1) * 2 * NB],
                              whi[:, h % 4, :].bitcast(F32), ALU.subtract).then_inc(lo_ready, 1)

        def products(pe, i, per, h, xh, xl, banks, first, last, cols=NB):
            pe.wait_ge(lo_ready, i * per + (h + 1))
            nk = 2 * NB // cols
            hi = whi[:, h % 4, :].rearrange("p (k n) -> p k n", k=nk)
            lo = wlo[:, h % 4, :].rearrange("p (k n) -> p k n", k=nk)
            for k in range(nk):
                for t in range(TT):
                    ts = slice(t * P, (t + 1) * P)
                    dst = banks[:, t, 0:cols]
                    pe.matmul(dst, xh[:, k, ts], hi[:, k, :], start=first and k == 0, stop=False)
                    pe.matmul(dst, xh[:, k, ts], lo[:, k, :], start=False, stop=False)
                    mm = pe.matmul(dst, xl[:, k, ts], hi[:, k, :], start=False, stop=last and k == nk - 1)
            mm.then_inc(half_done, 1)

        def block_2048(pe, i, per, h, blk_per, blk):
            if blk >= 2:
                pe.wait_ge(acc_free[blk % 2], i * (blk_per // 2) + blk // 2)
            for q in range(8):
                products(pe, i, per, h + q, ahi[:, 2 * q:2 * q + 2, :], alo[:, 2 * q:2 * q + 2, :],
                         acc(blk), q == 0, q == 7)

        def transpose_group(pe, n, src, k):
            if n >= 4:
                pe.wait_ge(tp_lo, n - 3)
            for j in range(2):
                for t in range(TT):
                    mm = pe.transpose(tp(n % 4)[:, j * T + t * P:j * T + (t + 1) * P],
                                      src[:, t, (k + j) * P:(k + j + 1) * P], ident[:, :])
            mm.then_inc(tp_ready, 1)

        def take_hi(act, n, k):
            act.wait_ge(tp_ready, n + 1)
            act.activation(ahi[:, k:k + 2, :], tp(n % 4).rearrange("p (k t) -> p k t", k=2), ACT.Copy)\
               .then_inc(tp_hi, 1)

        def take_lo(dve, n, k):
            dve.wait_ge(tp_hi, n + 1)
            dve.tensor_tensor(alo[:, k:k + 2, :], tp(n % 4).rearrange("p (k t) -> p k t", k=2),
                              ahi[:, k:k + 2, :].bitcast(F32), ALU.subtract).then_inc(tp_lo, 1)

        G_H, G_Y, G_M, G_X1 = 0, 8, 16, 24
        G_FFN1 = 32
        G_X2 = G_FFN1 + 2 * FB
        G_Y2 = G_X2 + 8
        G_X3 = G_Y2 + 8
        G_FFN2 = G_X3 + 8

        ADA = at(0, 3 * D)
        WOF = at(6144, 4 * DA)
        DEC = at(10240, 2, TT, NB)
        BROW = at(12288, 2, DA)
        FC = at(14336, TT, T)
        FS = at(14848, TT, T)
        HFB = at(15360, 2, TT, NB)
        SD = at(17408, 2, TT, NB)
        KST = at(19456, 4, NB)
        ZT = at(21504, T)
        FW = at(21760, 3, 64)
        FCOL = at(21952, 4)
        H1 = at(21960, T)
        H2 = at(22216, T)
        ROWS = at(22472, P)
        COLS = at(22600, 64)
        CACT = at(22664, 32)
        MODC = at(22696, 32)
        GROW = at(22728, 2048)
        HTMP = at(24776, 2, T)
        COEF = small[:, 0:32]
        STATS = small[:, 64:112].rearrange("p (t s v) -> p t s v", t=TT, s=4)
        MV = small[:, 112:116].rearrange("p (t v) -> p t v", t=TT)
        MSQ = small[:, 116:118]
        RSTD = small[:, 118:120]
        RTMP = small[:, 120:122]

        ada_w = A["ada_w"].rearrange("(k p) n -> p k n", p=P)
        w_in = A["w_in"].rearrange("(k p) n -> p k n", p=P)
        wk = {n: A[n].rearrange("(k p) n -> p k n", p=P) for n in
              ("p_a", "p_b", "w_out", "ffn1_w_gate_2", "ffn1_w_up_2", "ffn1_w_down_2", "w_in_2", "w_out_2",
               "ffn2_w_gate_2", "ffn2_w_up_2", "ffn2_w_down_2")}

        HY = 3 * DA

        block = ctx.enter_context(nc.Block())

        @block.sync
        def _(sp):
            sp.dma_start(ident[:, :], A["ident"]).then_inc(s_const, 16)
            sp.dma_start(ROWS[0:16, :], A["c"].rearrange("a (k p) -> (a k) p", p=P)).then_inc(s_rows, 16)
            sp.dma_start(ROWS[16:32, :], A["pre_gain"].rearrange("a (k p) -> (a k) p", p=P)).then_inc(s_rows, 16)
            sp.dma_start(ROWS[32:64, :], A["ada_b"][:, 0:2 * D].rearrange("a (k p) -> (a k) p", p=P))\
              .then_inc(s_rows, 16)
            for n in range(48):
                if n >= 4:
                    sp.wait_ge(ada_done, n - 3)
                sp.dma_start(raw[:, n % 4, :], ada_w[:, n % 16, n // 16 * D:(n // 16 + 1) * D])\
                  .then_inc(ada_in[n % 4], 16)

            load_chunk(sp, 0, 0, H_LORA, w_in[:, :, 3 * DA:3 * DA + P])

            def load_block(i, per, h, w, col):
                for q in range(4):
                    load_chunk(sp, i, per, h + 2 * q, w[:, 4 * q:4 * q + 4, ds(col, NB)])

            for b in range(2):
                load_block(0, 0, H_FIRST + 8 * b, w_in, b * NB)
            with sp.Fori(0, 2) as i:
                for b in range(2):
                    load_block(i, 16, H_IN + 8 * b, w_in, i * (2 * NB) + (2 + b) * NB)
            with sp.Fori(0, 9) as i:
                for b in range(2):
                    load_block(i, 16, H_IN + 32 + 8 * b, w_in, i * (2 * NB) + (OFF_ZA + b * NB))
            with sp.Fori(0, 4) as i:
                for n, w in enumerate(("p_a", "p_b")):
                    for q in range(2):
                        load_chunk(sp, i, 8, H_PAB + 4 * n + 2 * q, wk[w][:, 4 * q:4 * q + 4, ds(i * NB, NB)])
            with sp.Fori(0, 2) as i:
                for b in range(2):
                    load_block(i, 16, H_OUT + 8 * b, wk["w_out"], i * (2 * NB) + b * NB)

            def load_ffn(h0, gate, up, down):
                load_block(0, 0, h0, wk[gate], 0)
                load_block(0, 0, h0 + 8, wk[up], 0)
                with sp.Fori(0, FB - 1) as i:
                    load_block(i, 24, h0 + 16, wk[gate], i * NB + NB)
                    load_block(i, 24, h0 + 24, wk[up], i * NB + NB)
                    for n in range(4):
                        load_chunk(sp, i, 24, h0 + 32 + 2 * n, wk[down][:, ds(i * 4, 4), n * NB:(n + 1) * NB])
                for n in range(4):
                    load_chunk(sp, 0, 0, h0 + 24 * FB - 8 + 2 * n,
                               wk[down][:, 4 * FB - 4:4 * FB, n * NB:(n + 1) * NB])

            load_ffn(H_FFN1, "ffn1_w_gate_2", "ffn1_w_up_2", "ffn1_w_down_2")
            with sp.Fori(0, 6) as i:
                for b in range(2):
                    load_block(i, 16, H_IN2 + 8 * b, wk["w_in_2"], i * (2 * NB) + b * NB)
            with sp.Fori(0, 2) as i:
                for b in range(2):
                    load_block(i, 16, H_OUT2 + 8 * b, wk["w_out_2"], i * (2 * NB) + b * NB)
            load_ffn(H_FFN2, "ffn2_w_gate_2", "ffn2_w_up_2", "ffn2_w_down_2")

        (w_in_s, w_mix, w_z, w_tanh, w_ld, w_cum, w_exp, w_tok, w_t4p, w_t4, w_gram, w_mask, w_t0,
         w_ms, w_u, w_ue, w_dt, w_tn, w_w1, w_w1e, w_sa0, w_sae, w_sap, w_delta, w_state, w_y, w_ye,
         w_yo, w_st, w_prep, w_lora, w_lorat, w_loras, w_kin) = [sem("wkv_" + n) for n in (
             "in mix z tanh logdecay cumulated exp tok t4 t4_sb gram masked t0 "
             "m u u_sb dt tn w1 w1_sb sa0 sa sa_state delta state y y_sb out stored prep lora lora_t "
             "lora_sb const").split()]
        y_in = sem("y_in")
        y_sig = sem("y_sig")
        y_u = sem("y_u")
        y_src = sem("y_src")
        y_free = sem("y_free")
        ga_in = sem("ga_in")
        ga_sig = sem("ga_sig")
        m_done = sem("m_done")
        o_bc = sem("o_bc")
        o_sq = sem("o_sq")
        x1_done = sem("x1_done")
        n_bc = sem("n_bc")
        x_done = sem("x_done")
        ff_sig = sem("ff_sig")
        ff_ghi = sem("ff_ghi")
        ff_glo = sem("ff_glo")
        ff_zero = sem("ff_zero")
        x_out = sem("x_out")
        hy_tab = sem("hy_tab")
        hy_in = sem("hy_in")
        hy_z = sem("hy_z")
        hy_kin = sem("hy_kin")
        hy_f = sem("hy_f")
        hy_m = sem("hy_m")
        hy_i = sem("hy_i")
        hy_y = sem("hy_y")
        hy_g = sem("hy_g")
        at_in = sem("at_in")
        at_lam = sem("at_lam")
        at_le = sem("at_le")
        at_rope = sem("at_rope")
        at_tp = sem("at_tp")
        at_tps = sem("at_tps")
        at_s = sem("at_s")
        at_max = sem("at_max")
        at_e = sem("at_e")
        at_w = sem("at_w")
        at_wt = sem("at_wt")
        at_wts = sem("at_wts")
        at_o = sem("at_o")
        at_oe = sem("at_oe")
        at_g = sem("at_g")

        CUR = at(0, TT, 3, P)
        PRV = at(768, TT, 3, P)
        PRM = at(1536, PARAM_ROWS, P)
        WA = at(2560, 2, P)
        TOK = at(2816, TT, 4, P)
        T4 = at(3840, TT, 4, P)
        GR = at(4864, 4, 4, P)
        TM = at(6912, 4, P)
        TMT = at(7424, 4, P)
        MM = at(7936, 4, P)
        MS = at(8448, 4, P)
        UU = at(8960, 4, P)
        SG = at(9472, 2, TT, P)
        LD = at(9984, TT, P)
        KK = at(10240, TT, P)
        K2 = at(10496, TT, P)
        BB = at(10752, TT, P)
        RK = at(11008, TT, P)
        BV = at(11264, TT, P)
        EXPS = at(11520, 3, TT, P)
        W1S = at(14336, 4, 64)
        AEF = at(14592, TT, P)
        SA = at(14848, 4, 64)
        ST = at(15104, NCH, 64)
        SPC = at(15360, 64)
        YS = at(15424, 4, 64)
        YQ = at(15680, 4, 64)
        MASKS = at(15936, 13, P)
        LORAW = at(17600, T)
        LORAA = at(17856, T)
        LIN = at(18112, 2, TT, P)
        MUL = at(18624, P)
        WST = small[:, 32:64]

        YW = at(R5, TT, NB)
        ZA = at(R5 + 1024, TT, NB)
        BG = at(R5 + 2048, TT, NB)
        ZB = at(R5 + 3072, TT, NB)
        CG = at(R5 + 4096, 3, TT, NB)
        HB = at(R5 + 7168, 3, TT, NB)
        SZ = at(8192, 2, TT, NB)
        YT = at(8192 + 2048, TT, NB)
        CW = at(0, 3, DA)
        GA = at(R5, 2, TT, NB)
        MT = at(R5 + 2048, TT, NB)
        MU = at(R5 + 3072, TT, NB)
        GB = at(R5, 3, D)
        SIG = at(R5, TT, NB)
        GS = at(R5 + 1024, TT, NB)
        HID = at(R5 + 2048, TT, NB)
        NG = at(R5 + 4096, 2, D)
        TAB = at(8192, 4, TT, T)
        HL = at(10240, 3, TT, NB)
        HW = at(13312, 4, NB)
        HZ = at(15360, 3, TT, NB)
        HK = at(18432, 4, NB)
        HY_ = at(20480, 4, NB)
        HT = at(22528, 2, 2, NB)
        HG = at(24576, DA)
        AQ = at(8192, TT, DA)
        AK = at(10240, TT, DA)
        AV = at(12288, TT, DA)
        QT = at(14336, 8, T)
        KTT = at(16384, 8, T)
        EE = at(18432, 2, TT, T)
        WW = at(19456, TT, T)
        WT2 = at(19968, 2, T)
        ROPE = at(20480, 2, TT, 8)
        LAM = at(20512, 4, 64)
        SUBG = at(20768, P)
        AO = SRC[:, :, DA:D]
        AO2 = at(8192, TT, DA)
        RT = at(20896, 4, TT, 128)
        AST = at(21920, 128)
        AMS = at(22048, 16)
        ARS = at(22064, 16)

        @block.gpsimd
        def _(pool):
            pool.memset(ones[:, :], 1.0).then_inc(s_ones, 1)
            for dst, src in ((ZT[0:33, :], A["hy_zt"]), (FW[0:33, 0, :], A["filt_w1_2"]),
                             (FW[0:64, 1, :], A["filt_w2_2"]), (FW[0:64, 2, :], A["filt_w3_2"]),
                             (FCOL[0:64, 0:4], A["filt_cols"]), (WOF[0:64, :], A["filt_w_out_2"]),
                             (FC, A["dft"][0].rearrange("(t p) f -> p t f", p=P)),
                             (FS, A["dft"][1].rearrange("(t p) f -> p t f", p=P)),
                             (BROW[0:1, :, :], A["hyena_bias_2"].rearrange("(a n) c -> a n c", a=1))):
                pool.dma_start(dst, src).then_inc(f_in, 16)
            for r in range(2):
                pool.dma_start(proj1[r:r + 1, 0:OFF_ZB], A["zeros"][:, 0:OFF_ZB]).then_inc(zero_rows, 16)
            for r in (0, T + 1):
                pool.dma_start(proj2[r:r + 1, 0:HY], A["zeros"][:, 0:HY]).then_inc(zero_rows, 16)
            for u in range(4):
                cb, n = u // 2, u % 2
                if n == 0:
                    if u:
                        pool.wait_ge(f_sd0, u)
                    for d in range(2):
                        pool.dma_start(DEC[:, d], A["hy_decay"][d].rearrange("(t p) n -> p t n", p=P)
                                       [:, :, cb * NB:(cb + 1) * NB]).then_inc(f_dec, 16)
                pool.wait_ge(f_ke, u + 1)
                pool.dma_start(filt[n, cb], KST).then_inc(f_st, 16)
            pool.wait_ge(f_sd0, 4)
            for t in range(TT):
                pool.dma_start(SUM[:, t, :], A["x"][0, t * P:(t + 1) * P, :]).then_inc(x_in, 16)
            pool.wait_ge(mod_row_sb, 1)
            pool.dma_start(mod_gate, GROW[0:1, :]).then_inc(mod_stored, 16)

            def store_block(i, per2, s, blk, dst):
                wait_alone(pool, acc_free[blk % 2], i + (blk // 2 + 1))
                pool.dma_start(dst, STG[:, s % 2, :, 0:dst.shape[-1]]).then_inc(stg_out[s % 2], 16)

            p1 = tokens(proj1[2:T + 2, :])
            store_block(0, 0, 0, B_LORA, p1[:, :, 3 * DA:3 * DA + P])
            for b in range(2):
                store_block(0, 0, 1 + b, B_FIRST + b, p1[:, :, b * NB:(b + 1) * NB])
            with pool.Fori(0, 2) as i:
                for b in range(2):
                    store_block(i, 1, 3 + b, B_IN + b, p1[:, :, ds(i * (2 * NB) + (2 + b) * NB, NB)])
            with pool.Fori(0, 9) as i:
                for b in range(2):
                    store_block(i, 1, 7 + b, B_IN + 4 + b, p1[:, :, ds(i * (2 * NB) + (OFF_ZA + b * NB), NB)])
            pool.wait_ge(stg_out[0], 16 * 13)
            pool.wait_ge(stg_out[1], 16 * 12)
            pool.wait_ge(zero_rows, 64)

            for a, w in enumerate((LIN[:, 0], LIN[:, 1])):
                pool.dma_start(w, tokens(proj1[2 - a:T + 2 - a, 3 * DA:3 * DA + P])).then_inc(w_lora, 16)
            pool.dma_start(MUL, A["mu_lora"].rearrange("a n -> (a n)").partition_broadcast(P)).then_inc(w_lora, 16)
            pool.dma_start(MASKS, A["masks"]).then_inc(w_kin, 16)
            with pool.Fori(0, HP) as i:
                wait_alone(pool, w_yo, i)
                for a, w in enumerate((CUR, PRV)):
                    for t in range(TT):
                        pool.dma_start(w[:, t], proj1[2 - a + t * P:2 - a + (t + 1) * P, 0:3 * DA]
                                       .rearrange("p (q n) -> p q n", q=3)[:, :, ds(i * P, P)]).then_inc(w_in_s, 16)
                pool.dma_start(PRM, A["wkv_rows"][:, ds(i * P, P)].partition_broadcast(P)).then_inc(w_in_s, 16)
                pool.dma_start(WA[0:LORA + 1], A["lora_w"].rearrange("a k n -> k a n")[:, :, ds(i * P, P)])\
                    .then_inc(w_in_s, 16)
                for lv in range(5):
                    if lv == 0:
                        pool.wait_ge(w_mask, i * 2 + 2)
                    else:
                        pool.wait_ge(w_u, i * 5 + lv)
                    mt = GR.rearrange("p u g n -> p g u n")[:, 0]
                    pool.tensor_tensor(MS, mt, MASKS[:, 5 + lv, :].unsqueeze(1).to_broadcast([P, 4, P]), ALU.mult)\
                        .then_inc(w_ms, 1)
                wait_alone(pool, w_yo, i + 1)
                pool.dma_start(tokens(wkv_out)[:, :, ds(i * P, P)], YS.rearrange("p (t h) n -> p t (h n)", t=TT))\
                    .then_inc(w_st, 16)

            pool.wait_ge(w_st, 16 * HP)
            pool.dma_start(CW, A["conv_w"].partition_broadcast(P)).then_inc(y_in, 16)
            for c in range(2):
                if c:
                    pool.wait_ge(y_src, c)
                cs = slice(c * NB, (c + 1) * NB)
                pool.dma_start(YW, tokens(wkv_out)[:, :, cs]).then_inc(y_in, 16)
                for dst, off, back in ((ZA, OFF_ZA, 0), (BG, OFF_B, 0), (ZB, OFF_ZB, 0),
                                       (CG[:, 0], OFF_B + DA, 0), (CG[:, 1], OFF_B + DA, 1), (CG[:, 2], OFF_B + DA, 2),
                                       (HB[:, 0], OFF_B + 2 * DA, 0), (HB[:, 1], OFF_B + 2 * DA, 1),
                                       (HB[:, 2], OFF_B + 2 * DA, 2)):
                    pool.dma_start(dst, tokens(proj1[2 - back:T + 2 - back, off + c * NB:off + (c + 1) * NB]))\
                        .then_inc(y_in, 16)
                pool.wait_ge(y_in, 16 + 160 * (c + 1))
                pool.tensor_tensor(CG, CG, HB, ALU.mult).then_inc(y_u, 1)
            pool.wait_ge(y_src, 2)
            with pool.Fori(0, 4) as i:
                wait_alone(pool, m_done, i)
                for n in range(2):
                    pool.dma_start(GA[:, n], p1[:, :, ds(i * NB + (OFF_GATE + n * D), NB)]).then_inc(ga_in, 16)
            pool.wait_ge(m_done, 4)
            pool.wait_ge(mod_stored, 16)
            for n, src in enumerate((mod_gate[0], A["ada_b"][0, 2 * D:3 * D], A["post_gain"][0])):
                pool.dma_start(GB[:, n], rows(src, P)).then_inc(o_bc, 16)
            pool.dma_start(XRES, tokens(A["x"][0])).then_inc(o_bc, 16)

            def norm_rows(n, g, b):
                if n:
                    pool.wait_ge(x_done, 2 * n)
                for j, name in enumerate((g, b)):
                    pool.dma_start(NG[:, j], rows(A[name][0], P)).then_inc(n_bc, 16)

            pool.wait_ge(x1_done, 2)
            pool.memset(SUM, 0.0).then_inc(ff_zero, 1)
            norm_rows(0, "ln1_g_2", "ln1_b_2")

            p2 = tokens(proj2[1:T + 1, :])
            with pool.Fori(0, 6) as i:
                for b in range(2):
                    store_block(i, 1, 25 + b, B_IN2 + b, p2[:, :, ds(i * (2 * NB) + b * NB, NB)])
            pool.wait_ge(stg_out[0], 16 * (13 + 6))
            pool.wait_ge(stg_out[1], 16 * (12 + 6))
            for n in range(4):
                pool.dma_start(TAB[:, n], A["dft"][n].rearrange("(t p) f -> p t f", p=P)).then_inc(hy_tab, 16)
            for cb in range(2):
                for part in range(3):
                    u = 3 * cb + part
                    if u:
                        pool.wait_ge(hy_z, u)
                    off = part * DA + cb * NB
                    pool.dma_start(HW, A["hyena_rows"][:, off:off + NB].partition_broadcast(P)).then_inc(hy_in, 16)
                    for s in range(3):
                        pool.dma_start(HL[:, s], tokens(proj2[s:T + s, off:off + NB])).then_inc(hy_in, 16)
                for n in range(2):
                    if 2 * cb + n:
                        pool.wait_ge(hy_m, 2 * cb + n)
                    pool.dma_start(HK, filt[n, cb]).then_inc(hy_kin, 16)
            pool.dma_start(HG, rows(A["hyena_norm_g_2"][0], P)).then_inc(hy_tab, 16)
            pool.wait_ge(hy_g, 2)
            for dst, off in ((AQ, HY), (AK, HY + DA), (AV, HY + 2 * DA)):
                pool.dma_start(dst, p2[:, :, off:off + DA]).then_inc(at_in, 16)
            pool.dma_start(ROPE, A["rope"].rearrange("a (t p) f -> p a t f", p=P)).then_inc(at_in, 16)
            pool.dma_start(LAM, A["lambdas"].partition_broadcast(P)).then_inc(at_in, 16)
            pool.dma_start(SUBG, rows(A["subln_g_2"][0], P)).then_inc(at_in, 16)
            pool.wait_ge(at_g, 2)
            norm_rows(1, "ln2_g_2", "ln2_b_2")
            pool.wait_ge(x_done, 4)
            pool.memset(SUM, 0.0).then_inc(ff_zero, 1)
            norm_rows(2, "ln3_g_2", "ln3_b_2")
            for t in range(TT):
                pool.wait_ge(x_done, 5 + t)
                pool.dma_start(out[0, t * P:(t + 1) * P, :], XRES[:, t, :]).then_inc(x_out, 16)
            pool.wait_ge(x_out, 32)
            for st, n in ((f_st, 64), (zero_rows, 64), (mod_stored, 16)):
                pool.wait_ge(st, n)

        @block.scalar
        def _(act):
            act.wait_ge(rows_t, 1)
            act.activation(CACT[:, 16:32], tp(0)[:, 0:16], ACT.Sigmoid).then_inc(c_sig, 1)
            for n in range(3):
                act.wait_ge(f_arg, n + 1)
                act.activation((H1, H2, H1)[n][0:64, :], KST[0:64, 0, 0:T], ACT.Sin).then_inc(f_sin, 1)
            for u in range(4):
                act.wait_ge(f_k, u + 1)
                if u:
                    act.wait_ge(f_st, 16 * u)
                act.activation(KST, ps[:, 4:8, :], ACT.Copy).then_inc(f_ke, 1)
            act.wait_ge(mod_row, 1)
            act.activation(GROW[0:1, :].rearrange("p (a n) -> p a n", a=4), ps[0:1, 4:8, :], ACT.Copy)\
               .then_inc(mod_row_sb, 1)
            for h in range(3):
                split_hi(act, 0, 0, h)
            for g in range(8):
                act.wait_ge(tp_ready, G_H + g + 1)
                for j in range(2):
                    k = 2 * g + j
                    ins = act.activation(ahi[:, k, :], tp(g % 4)[:, j * T:(j + 1) * T], ACT.Identity,
                                         scale=COEF[:, k:k + 1], bias=COEF[:, 16 + k:17 + k])
                ins.then_inc(tp_hi, 1)

            def stage(i, per, h_end, s, blk, cols=NB):
                act.wait_ge(half_done, i * per + h_end)
                if s >= 2:
                    act.wait_ge(stg_out[s % 2], i * 16 + 16 * (s // 2))
                act.activation(STG[:, s % 2, :, 0:cols], acc(blk)[:, :, 0:cols], ACT.Copy)\
                   .then_inc(acc_free[blk % 2], 1)

            def split_hi_block(i, per, h):
                for q in range(8):
                    split_hi(act, i, per, h + q + 3)

            split_hi(act, 0, 0, 3)
            split_hi(act, 0, 0, 4)
            stage(0, 0, 2, 0, B_LORA, P)
            for b in range(2):
                split_hi_block(0, 0, H_FIRST + 8 * b)
                stage(0, 0, H_FIRST + 8 * b + 8, 1 + b, B_FIRST + b)
            with act.Fori(0, 2) as i:
                for b in range(2):
                    split_hi_block(i, 16, H_IN + 8 * b)
                    stage(i, 16, H_IN + 8 * b + 8, 3 + b, B_IN + b)
            with act.Fori(0, 9) as i:
                for b in range(2):
                    split_hi_block(i, 16, H_IN + 32 + 8 * b)
                    stage(i, 16, H_IN + 32 + 8 * b + 8, 7 + b, B_IN + 4 + b)

            act.wait_ge(w_prep, 1)
            act.activation(LIN[:, 0, :, 0:LORA], LIN[:, 0, :, 0:LORA], ACT.Tanh).then_inc(w_prep, 1)
            act.wait_ge(w_lorat, 1)
            act.activation(LORAW[0:LORA, :], tp(0)[0:LORA, 0:T], ACT.Copy).then_inc(w_loras, 1)
            act.activation(LORAA[0:LORA, :], tp(1)[0:LORA, 0:T], ACT.Copy).then_inc(w_loras, 1)
            with act.Fori(0, HP) as i:
                act.wait_ge(w_z, i + 1)
                act.activation(SG.rearrange("p a t n -> p (a t n)"), tp(0), ACT.Tanh, scale=0.5).then_inc(w_tanh, 1)
                act.wait_ge(w_cum, i + 1)
                act.activation(EXPS[:, 0:2].rearrange("p a t n -> p (a t n)"), tp(1), ACT.Exp)
                act.activation(EXPS[:, 2].rearrange("p t n -> p (t n)"), tp(1)[:, 0:T], ACT.Exp, scale=-1.0)
                act.activation(WST[:, 20:24], tp(2)[:, 0:4], ACT.Exp).then_inc(w_exp, 1)
                for t in range(TT):
                    act.wait_ge(w_t4p, i * 2 + (t + 1))
                    act.activation(T4[:, t].rearrange("p a n -> p (a n)"), tp(2 + t), ACT.Copy).then_inc(w_t4, 1)
                for lv in range(5):
                    act.wait_ge(w_u, i * 5 + (lv + 1))
                    act.activation(UU.rearrange("p u n -> p (u n)"), tp(0), ACT.Copy).then_inc(w_ue, 1)
                act.wait_ge(w_w1, i + 1)
                act.activation(W1S.rearrange("p u n -> p (u n)"), tp(0)[:, 0:T], ACT.Copy)
                act.activation(AEF.rearrange("p t n -> p (t n)"), tp(1)[:, 0:T], ACT.Copy).then_inc(w_w1e, 1)
                act.wait_ge(w_y, i + 1)
                act.activation(YS.rearrange("p (t h) n -> p t h n", t=TT),
                               ps[:, 4:6, 0:P].rearrange("p h (t n) -> p t h n", t=TT), ACT.Copy).then_inc(w_ye, 1)

            for c in range(2):
                act.wait_ge(y_in, 16 + 160 * (c + 1))
                act.activation(SZ[:, 0], ZA, ACT.Sigmoid)
                act.activation(SZ[:, 1], ZB, ACT.Sigmoid).then_inc(y_sig, 1)
            for g in range(8):
                take_hi(act, G_Y + g, 2 * g)
            with act.Fori(0, 4) as i:
                for q in range(4):
                    split_hi(act, i, 8, H_PAB + q + 3)
                act.wait_ge(ga_in, i * 32 + 32)
                act.activation(GA, GA, ACT.Sigmoid).then_inc(ga_sig, 1)
                for q in range(4, 8):
                    split_hi(act, i, 8, H_PAB + q + 3)
            for g in range(8):
                take_hi(act, G_M + g, 2 * g)

            def sum_blocks(h, blk):
                with act.Fori(0, 2) as i:
                    for b in range(2):
                        split_hi_block(i, 16, h + 8 * b)
                        act.wait_ge(half_done, i * 16 + (h + 8 * b + 8))
                        act.activation(SUM[:, :, ds(i * (2 * NB) + b * NB, NB)], acc(blk + b), ACT.Copy)\
                           .then_inc(acc_free[(blk + b) % 2], 1)

            sum_blocks(H_OUT, B_OUT)
            act.drain()
            for t in range(TT):
                act.activation(SRC[:, t, :], SUM[:, t, :], ACT.Square, accum_out=MSQ[:, t:t + 1]).then_inc(o_sq, 1)
            for g in range(8):
                take_hi(act, G_X1 + g, 2 * g)

            def hidden_hi(i, g):
                for j in range(2):
                    act.wait_ge(tp_ready, i * 2 + (g + j + 1))
                    act.activation(ghi[:, 2 * j:2 * j + 2, :], tp(j).rearrange("p (k t) -> p k t", k=2), ACT.Copy)\
                       .then_inc(tp_hi, 1)

            def ffn(h0, blk, g0):
                def gate_up(i, per, h, b):
                    split_hi_block(i, per, h)
                    act.wait_ge(half_done, i * per + (h + 8))
                    act.activation(SIG, acc(b), ACT.Sigmoid).then_inc(ff_sig, 1)
                    split_hi_block(i, per, h + 8)

                gate_up(0, 0, h0, blk)
                hidden_hi(0, g0)
                with act.Fori(0, FB - 1) as i:
                    gate_up(i, 24, h0 + 16, blk + 2)
                    split_hi_block(i, 24, h0 + 32)
                    hidden_hi(i, g0 + 2)
                split_hi_block(0, 0, h0 + 24 * FB - 8)

            ffn(H_FFN1, B_FFN1, G_FFN1)
            for g in range(8):
                take_hi(act, G_X2 + g, 2 * g)
            with act.Fori(0, 6) as i:
                for b in range(2):
                    split_hi_block(i, 16, H_IN2 + 8 * b)
                    stage(i, 16, H_IN2 + 8 * b + 8, 25 + b, B_IN2 + b)
            act.wait_ge(at_lam, 1)
            act.activation(AST[:, 2:4], AST[:, 0:2], ACT.Exp).then_inc(at_le, 1)
            for h in range(8):
                act.wait_ge(at_tp, h + 1)
                act.activation(QT[:, h, :], tp(h % 4)[:, 0:T], ACT.Copy)
                act.activation(KTT[:, h, :], tp(h % 4)[:, T:2 * T], ACT.Copy).then_inc(at_tps, 1)

            def exps(h):
                act.wait_ge(at_max, h + 1)
                if h:
                    act.wait_ge(at_w, h)
                for m in range(2):
                    for t in range(TT):
                        n = 4 * h + 2 * m + t
                        ins = act.activation(EE[:, m, t, :], ps[:, 2 * (h % 2) + m, t * T:(t + 1) * T], ACT.Exp,
                                             scale=0.125, bias=AST[:, 8 + n:9 + n],
                                             accum_out=AST[:, 40 + n:41 + n])
                ins.then_inc(at_e, 1)

            exps(0)
            for h in range(8):
                if h < 7:
                    exps(h + 1)
                act.wait_ge(at_wt, h + 1)
                act.activation(WT2, ps[:, 4 + h % 2, :].rearrange("p (k q) -> p k q", k=2), ACT.Copy)\
                   .then_inc(at_wts, 1)
                act.wait_ge(at_o, h + 1)
                act.activation(AO[:, :, h * P:(h + 1) * P],
                               ps[:, 6 + h % 2, 0:T].rearrange("p (t n) -> p t n", t=TT), ACT.Copy).then_inc(at_oe, 1)
            for g in range(8):
                take_hi(act, G_Y2 + g, 2 * g)
            sum_blocks(H_OUT2, B_OUT2)
            for g in range(8):
                take_hi(act, G_X3 + g, 2 * g)
            ffn(H_FFN2, B_FFN2, G_FFN2)

        @block.tensor
        def _(pe):
            pe.wait_ge(s_const, 16)
            pe.wait_ge(s_rows, 48)
            pe.transpose(tp(0)[:, 0:64], ROWS[0:64, :], ident[0:64, 0:64]).then_inc(rows_t, 1)
            pe.wait_ge(f_in, 9 * 16)
            pe.matmul(tp(1)[0:64, 0:T], FW[0:33, 0, :], ZT[0:33, :], start=True, stop=True).then_inc(f_mlp, 1)
            for n, src in ((1, H1), (2, H2)):
                pe.wait_ge(f_sin, n)
                pe.matmul(tp(1)[0:64, 0:T], FW[0:64, n, :], src[0:64, :], start=True, stop=True).then_inc(f_mlp, 1)
            pe.wait_ge(f_sin, 3)
            pe.wait_ge(c_act, 1)
            for u in range(4):
                cb, n = u // 2, u % 2
                if u:
                    pe.wait_ge(f_sd0, u)
                for d in range(2):
                    for t in range(TT):
                        col = n * 2 * DA + d * DA + cb * NB
                        mm = pe.matmul(ps[:, 2 * d + t, :], H1[0:64, t * P:(t + 1) * P], WOF[0:64, col:col + NB],
                                       start=True, stop=True)
                mm.then_inc(f_h, 1)
                pe.wait_ge(f_sd, 2 * u + 2)
                if u:
                    pe.wait_ge(f_ke, u)
                for part, tab in enumerate((FC, FS)):
                    for m in range(2):
                        for t in range(TT):
                            mm = pe.matmul(tp(2 * part + m), tab[:, t, m * P:(m + 1) * P], SD[:, part, t, :],
                                           start=t == 0, stop=t == 1)
                mm.then_inc(f_k, 1)
            pe.wait_ge(ada_done, 48)
            pe.wait_ge(s_ones, 1)
            for j in range(32):
                mm = pe.matmul(ps[:, 0, j:j + 1], ADA[:, j * P:(j + 1) * P], ones[:, 0:1], start=True, stop=True)
            mm.then_inc(mod_cols, 1)
            pe.wait_ge(f_ke, 4)
            for n in range(4):
                mm = pe.matmul(ps[0:1, 4 + n, :], ones[:, 0:1], ADA[:, 2 * D + n * NB:2 * D + (n + 1) * NB],
                               start=True, stop=True)
            mm.then_inc(mod_row, 1)
            pe.wait_ge(mod_row_sb, 1)
            pe.wait_ge(x_norm, 2)
            for g in range(8):
                transpose_group(pe, G_H + g, SRC, 2 * g)
            pe.wait_ge(tp_lo, G_H + 8)
            pe.wait_ge(mod_scale, 1)
            products(pe, 0, 0, 0, ahi[:, 0:8, :], alo[:, 0:8, :], acc(B_LORA), True, False, P)
            products(pe, 0, 0, 1, ahi[:, 8:16, :], alo[:, 8:16, :], acc(B_LORA), False, True, P)
            for b in range(2):
                block_2048(pe, 0, 0, H_FIRST + 8 * b, 0, B_FIRST + b)
            with pe.Fori(0, 2) as i:
                for b in range(2):
                    block_2048(pe, i, 16, H_IN + 8 * b, 2, B_IN + b)
            with pe.Fori(0, 9) as i:
                for b in range(2):
                    block_2048(pe, i, 16, H_IN + 32 + 8 * b, 2, B_IN + 4 + b)

            pe.wait_ge(w_prep, 2)
            for t in range(TT):
                pe.transpose(tp(0)[0:LORA, t * P:(t + 1) * P], LIN[:, 0, t, 0:LORA], ident[:, :])
                mm = pe.transpose(tp(1)[0:LORA, t * P:(t + 1) * P], LIN[:, 0, t, LORA:P], ident[:, :])
            mm.then_inc(w_lorat, 1)
            pe.wait_ge(w_loras, 3)
            pe.wait_ge(w_kin, 16)
            V = CUR[:, :, 2, :]
            with pe.Fori(0, HP) as i:
                pe.wait_ge(w_in_s, i * 96 + 96)
                for a, lora in enumerate((LORAW, LORAA)):
                    for t in range(TT):
                        mm = pe.matmul(tp(0)[:, (2 * a + t) * P:(2 * a + t + 1) * P],
                                       lora[0:LORA + 1, t * P:(t + 1) * P], WA[0:LORA + 1, a, :], start=True, stop=True)
                mm.then_inc(w_z, 1)
                pe.wait_ge(w_ld, i + 1)
                for t in range(TT):
                    pe.matmul(tp(1)[:, t * P:(t + 1) * P], MASKS[:, 1, :], LD[:, t, :], start=True, stop=True)
                    pe.matmul(tp(1)[:, T + t * P:T + (t + 1) * P], MASKS[:, 0, :], LD[:, t, :], start=True, stop=True)
                    mm = pe.matmul(tp(2)[:, 2 * t:2 * t + 2], LD[:, t, :], MASKS[:, 12, 0:2], start=True, stop=True)
                mm.then_inc(w_cum, 1)
                pe.wait_ge(w_tok, i + 1)
                for t in range(TT):
                    for n in range(4):
                        mm = pe.transpose(tp(2 + t)[:, n * P:(n + 1) * P], TOK[:, t, n, :], ident[:, :])
                    mm.then_inc(w_t4p, 1)
                for t in range(TT):
                    pe.wait_ge(w_t4, i * 2 + 2)
                    if t:
                        pe.wait_ge(w_mask, i * 2 + t)
                    for h in range(2):
                        hs = slice(64 * h, 64 * h + 64)
                        ar = T4[hs, t, 0:2, :].rearrange("p a n -> p (a n)")
                        pe.matmul(tp(h)[:, 0:T], T4[hs, t, 2, :], ar, start=True, stop=True)
                        pe.matmul(tp(h)[:, T:2 * T], T4[hs, t, 3, :], ar, start=True, stop=True)
                        mm = pe.matmul(tp(2 + h)[:, t * P:(t + 1) * P],
                                       T4[hs, t, 0, :], T4[hs, t, 2, :], start=True, stop=True)
                    mm.then_inc(w_gram, 1)
                pe.wait_ge(w_t0, i + 1)
                for lv in range(5):
                    if lv:
                        pe.wait_ge(w_tn, i * 5 + lv)
                    pe.wait_ge(w_ms, i * 5 + (lv + 1))
                    for u in range(4):
                        mm = pe.matmul(tp(0)[:, u * P:(u + 1) * P], MS[:, u, :], TM[:, u, :], start=True, stop=True)
                    mm.then_inc(w_u, 1)
                    pe.wait_ge(w_ue, i * 5 + (lv + 1))
                    for u in range(4):
                        if lv < 4:
                            pe.matmul(tp(1)[:, u * P:(u + 1) * P], TMT[:, u, :], UU[:, u, :], start=True, stop=True)
                        mm = pe.matmul(tp(2)[:, u * P:(u + 1) * P], UU[:, u, :], TMT[:, u, :], start=True, stop=True)
                    mm.then_inc(w_dt, 1)
                pe.wait_ge(w_tn, i * 5 + 5)
                for t in range(TT):
                    for h in range(2):
                        u = 2 * t + h
                        hs = slice(64 * h, 64 * h + 64)
                        pe.matmul(tp(0)[:, u * 64:(u + 1) * 64], GR[:, u, 2, :], V[:, t, hs], start=True, stop=True)
                        mm = pe.matmul(tp(1)[hs, t * P:(t + 1) * P], TOK[:, t, 0, hs], TMT[:, u, :],
                                       start=True, stop=True)
                mm.then_inc(w_w1, 1)
                pe.wait_ge(w_w1e, i + 1)
                for u in range(4):
                    mm = pe.matmul(tp(2)[:, u * 64:(u + 1) * 64], TMT[:, u, :], W1S[:, u, :], start=True, stop=True)
                mm.then_inc(w_sa0, 1)
                for c in range(NCH):
                    t, rs = c // 2, slice(CH * (c % 2), CH * (c % 2) + CH)
                    cs = slice(CH * (c % 2), CH * (c % 2) + CH)
                    if c:
                        wait_alone(pe, w_state, i * 3 + c)
                        for h in range(2):
                            hs = slice(64 * h, 64 * h + 64)
                            mm = pe.matmul(tp(h)[rs, 0:64], AEF[hs, t, cs], ST[hs, c, :], start=True, stop=True)
                        mm.then_inc(w_sap, 1)
                    wait_alone(pe, w_sae, i * 4 + (c + 1))
                    if c == NCH - 1:
                        break
                    for h in range(2):
                        hs = slice(64 * h, 64 * h + 64)
                        pe.matmul(tp(3)[hs, c * 64:(c + 1) * 64], TOK[rs, t, 2, hs], SA[rs, 2 * t + h, :],
                                  start=True, stop=False)
                        mm = pe.matmul(tp(3)[hs, c * 64:(c + 1) * 64], TOK[rs, t, 3, hs], V[rs, t, hs],
                                       start=False, stop=True)
                    mm.then_inc(w_delta, 1)
                for t in range(TT):
                    for h in range(2):
                        u = 2 * t + h
                        hs = slice(64 * h, 64 * h + 64)
                        dst = tp(h)[:, t * 64:(t + 1) * 64]
                        pe.matmul(dst, GR[:, u, 1, :], SA[:, u, :], start=True, stop=False)
                        pe.matmul(dst, GR[:, u, 3, :], V[:, t, hs], start=False, stop=False)
                        for c in (2 * t, 2 * t + 1):
                            rs = slice(CH * (c % 2), CH * (c % 2) + CH)
                            mm = pe.matmul(tp(h)[rs, t * 64:(t + 1) * 64], T4[hs, t, 1, rs], ST[hs, c, :],
                                           start=False, stop=True)
                mm.then_inc(w_y, 1)

            pe.wait_ge(y_src, 2)
            for g in range(8):
                transpose_group(pe, G_Y + g, SRC, 2 * g)
            pe.wait_ge(tp_lo, G_Y + 8)
            with pe.Fori(0, 4) as i:
                for n in range(2):
                    blk = B_PAB + n
                    pe.wait_ge(acc_free[blk % 2], i + blk // 2)
                    for q in range(4):
                        k = 8 * n + 2 * q
                        products(pe, i, 8, H_PAB + 4 * n + q, ahi[:, k:k + 2, :], alo[:, k:k + 2, :], acc(blk),
                                 q == 0, q == 3)
            pe.wait_ge(m_done, 4)
            for g in range(8):
                transpose_group(pe, G_M + g, SRC, 2 * g)
            pe.wait_ge(tp_lo, G_M + 8)
            with pe.Fori(0, 2) as i:
                for b in range(2):
                    block_2048(pe, i, 16, H_OUT + 8 * b, 2, B_OUT + b)
            pe.wait_ge(x1_done, 2)
            for g in range(8):
                transpose_group(pe, G_X1 + g, XRES, 2 * g)
            pe.wait_ge(tp_lo, G_X1 + 8)

            def ffn(h0, blk, g0):
                def hidden(i, g, up):
                    pe.wait_ge(acc_free[up % 2], i * 3 + (up // 2 + 1))
                    pe.wait_ge(tp_lo, i * 2 + g)
                    for j in range(2):
                        for k in range(2):
                            for t in range(TT):
                                col = (2 * j + k) * P
                                mm = pe.transpose(tp(j)[:, k * T + t * P:k * T + (t + 1) * P],
                                                  HID[:, t, col:col + P], ident[:, :])
                        mm.then_inc(tp_ready, 1)

                def down(i, per, h, blk_per, b, g):
                    pe.wait_ge(tp_lo, i * 2 + g)
                    for n in range(4):
                        pe.wait_ge(acc_free[(b + n) % 2], i * (blk_per // 2) + (b + n) // 2)
                        for q in range(2):
                            products(pe, i, per, h + 2 * n + q, ghi[:, 2 * q:2 * q + 2, :], glo[:, 2 * q:2 * q + 2, :],
                                     acc(b + n), q == 0, q == 1)

                block_2048(pe, 0, 0, h0, 0, blk)
                block_2048(pe, 0, 0, h0 + 8, 0, blk + 1)
                hidden(0, g0, blk + 1)
                with pe.Fori(0, FB - 1) as i:
                    block_2048(pe, i, 24, h0 + 16, 6, blk + 2)
                    block_2048(pe, i, 24, h0 + 24, 6, blk + 3)
                    down(i, 24, h0 + 32, 6, blk + 4, g0 + 2)
                    hidden(i, g0 + 2, blk + 3)
                down(0, 0, h0 + 24 * FB - 8, 0, blk + 6 * FB - 4, g0 + 2 * FB)

            ffn(H_FFN1, B_FFN1, G_FFN1)
            pe.wait_ge(x_done, 2)
            for g in range(8):
                transpose_group(pe, G_X2 + g, XRES, 2 * g)
            pe.wait_ge(tp_lo, G_X2 + 8)
            with pe.Fori(0, 6) as i:
                for b in range(2):
                    block_2048(pe, i, 16, H_IN2 + 8 * b, 2, B_IN2 + b)

            pe.wait_ge(hy_tab, 64)
            for cb in range(2):
                for n in range(2):
                    u = 2 * cb + n
                    if n == 0:
                        pe.wait_ge(hy_z, 3 * cb + 3)
                    else:
                        pe.wait_ge(hy_y, u)
                    for part in range(2):
                        for m in range(2):
                            for t in range(TT):
                                mm = pe.matmul(tp(2 * part + m), TAB[:, part, t, m * P:(m + 1) * P], HZ[:, 0, t, :],
                                               start=t == 0, stop=t == 1)
                    mm.then_inc(hy_f, 1)
                    pe.wait_ge(hy_m, u + 1)
                    for t in range(TT):
                        for part in range(2):
                            for m in range(2):
                                mm = pe.matmul(ps[:, t, :], TAB[:, 2 + part, m, t * P:(t + 1) * P],
                                               HY_[:, 2 * part + m, :], start=part == 0 and m == 0,
                                               stop=part == 1 and m == 1)
                    mm.then_inc(hy_i, 1)

            pe.wait_ge(at_rope, 2)
            pe.wait_ge(hy_y, 4)
            for h in range(8):
                if h >= 4:
                    pe.wait_ge(at_tps, h - 3)
                for n, src in enumerate((AQ, AK)):
                    for t in range(TT):
                        mm = pe.transpose(tp(h % 4)[:, n * T + t * P:n * T + (t + 1) * P],
                                          src[:, t, h * P:(h + 1) * P], ident[:, :])
                mm.then_inc(at_tp, 1)

            def scores(h):
                pe.wait_ge(at_tps, h + 1)
                if h >= 2:
                    pe.wait_ge(at_e, h - 1)
                for m in range(2):
                    rs = slice(64 * m, 64 * m + 64)
                    for t in range(TT):
                        mm = pe.matmul(ps[:, 2 * (h % 2) + m, t * T:(t + 1) * T], QT[rs, h, t * P:(t + 1) * P],
                                       KTT[rs, h, :], start=True, stop=True)
                mm.then_inc(at_s, 1)

            scores(0)
            for h in range(8):
                if h < 7:
                    scores(h + 1)
                pe.wait_ge(at_w, h + 1)
                pe.wait_ge(at_tps, 8)
                for k in range(2):
                    for t in range(TT):
                        mm = pe.transpose(ps[:, 4 + h % 2, k * T + t * P:k * T + (t + 1) * P],
                                          WW[:, t, k * P:(k + 1) * P], ident[:, :])
                mm.then_inc(at_wt, 1)
                pe.wait_ge(at_wts, h + 1)
                if h >= 2:
                    pe.wait_ge(at_oe, h - 1)
                for t in range(TT):
                    for k in range(2):
                        mm = pe.matmul(ps[:, 6 + h % 2, t * P:(t + 1) * P], WT2[:, k, t * P:(t + 1) * P],
                                       AV[:, k, h * P:(h + 1) * P], start=k == 0, stop=k == 1)
                mm.then_inc(at_o, 1)

            pe.wait_ge(at_g, 2)
            pe.wait_ge(hy_g, 2)
            for g in range(8):
                transpose_group(pe, G_Y2 + g, SRC, 2 * g)
            pe.wait_ge(tp_lo, G_Y2 + 8)
            with pe.Fori(0, 2) as i:
                for b in range(2):
                    block_2048(pe, i, 16, H_OUT2 + 8 * b, 2, B_OUT2 + b)
            pe.wait_ge(x_done, 4)
            for g in range(8):
                transpose_group(pe, G_X3 + g, XRES, 2 * g)
            pe.wait_ge(tp_lo, G_X3 + 8)
            ffn(H_FFN2, B_FFN2, G_FFN2)

        @block.vector
        def _(dve):
            def bc(ap, n):
                return ap.unsqueeze(1).to_broadcast([ap.shape[0], n, ap.shape[-1]])

            def bcl(ap, n):
                return ap.unsqueeze(2).to_broadcast([ap.shape[0], ap.shape[1], n])

            def rsqrt(dst, src, tmp):
                dve.tensor_scalar(tmp.bitcast(mybir.dt.int32), src.bitcast(mybir.dt.int32), 1, None,
                                  ALU.logical_shift_right)
                dve.drain()
                dve.tensor_scalar(dst.bitcast(mybir.dt.int32), tmp.bitcast(mybir.dt.int32), -1.0, 1597463007.0,
                                  ALU.mult, ALU.add)
                dve.drain()
                for _ in range(3):
                    dve.tensor_tensor(tmp, dst, dst, ALU.mult)
                    dve.drain()
                    dve.tensor_tensor(tmp, tmp, src, ALU.mult)
                    dve.drain()
                    dve.tensor_scalar(tmp, tmp, -0.5, 1.5, ALU.mult, ALU.add)
                    dve.drain()
                    dve.tensor_tensor(dst, dst, tmp, ALU.mult)
                    dve.drain()

            dve.wait_ge(rows_t, 1)
            dve.wait_ge(c_sig, 1)
            dve.tensor_copy(COLS[:, 0:64], tp(0)[:, 0:64])
            dve.drain()
            dve.tensor_tensor(CACT[:, 0:16], COLS[:, 0:16], CACT[:, 16:32], ALU.mult).then_inc(c_act, 1)
            dve.drain()

            def ada(n):
                k, part = n % 16, ADA[:, n // 16 * D:(n // 16 + 1) * D]
                dve.wait_ge(ada_in[n % 4], 16 * (n // 4 + 1))
                if k == 0:
                    dve.tensor_scalar(part, raw[:, n % 4, :], CACT[:, 0:1], None, ALU.mult).then_inc(ada_done, 1)
                else:
                    dve.scalar_tensor_tensor(part, raw[:, n % 4, :], CACT[:, k:k + 1], part, ALU.mult, ALU.add)\
                       .then_inc(ada_done, 1)
                dve.drain()

            def sine_argument(n):
                arg, turns = KST[0:64, 0, 0:T], KST[0:64, 1, 0:T]
                dve.wait_ge(f_mlp, n + 1)
                if n == 0:
                    dve.wait_ge(f_in, 9 * 16)
                dve.tensor_scalar(arg, tp(1)[0:64, 0:T], FCOL[0:64, n:n + 1], FCOL[0:64, 3:4], ALU.add, ALU.mult)
                dve.drain()
                dve.tensor_scalar(turns, arg, 1.0 / (2.0 * math.pi), ROUND, ALU.mult, ALU.add)
                dve.drain()
                dve.tensor_scalar(turns, turns, ROUND, None, ALU.subtract)
                dve.drain()
                for part in (TWO_PI_HI, TWO_PI_LO):
                    dve.scalar_tensor_tensor(arg, turns, -part, arg, ALU.mult, ALU.add)
                    dve.drain()
                dve.tensor_scalar(arg, arg, PI_IN, -PI_IN, ALU.min, ALU.max).then_inc(f_arg, 1)

            def filter_unit(u):
                cb, n = u // 2, u % 2
                dve.wait_ge(f_h, u + 1)
                dve.wait_ge(f_dec, 32 * (cb + 1))
                dve.tensor_tensor(HFB, ps[:, 0:4, :].rearrange("p (d t) n -> p d t n", d=2), DEC, ALU.mult)\
                   .then_inc(f_sd0, 1)
                dve.drain()
                row = HFB[0:1, 0, 0, :]
                dve.tensor_tensor(row, row, BROW[0:1, n, cb * NB:(cb + 1) * NB], ALU.add)
                dve.drain()
                if u:
                    dve.wait_ge(f_k, u)
                dve.tensor_tensor(SD[:, 0], HFB[:, 0], HFB[:, 1], ALU.add).then_inc(f_sd, 1)
                dve.tensor_tensor(SD[:, 1], HFB[:, 0], HFB[:, 1], ALU.subtract).then_inc(f_sd, 1)

            for n in range(48):
                ada(n)
                if n in (2, 5, 8):
                    sine_argument((n - 2) // 3)
                if n in (12, 20, 28, 36):
                    filter_unit((n - 12) // 8)
            dve.wait_ge(x_in, 32)

            def stats(src, t):
                for s in range(4):
                    dve.bn_stats(STATS[:, t, s, :], src[:, t, s * NB:(s + 1) * NB])
                dve.drain()
                return dve.bn_aggr(MV[:, t, :], STATS[:, t])

            for t in range(TT):
                stats(SUM, t)
            dve.drain()
            dve.tensor_tensor(MSQ, MV[:, :, 0], MV[:, :, 0], ALU.mult)
            dve.drain()
            dve.tensor_tensor(MSQ, MSQ, MV[:, :, 1], ALU.add)
            dve.drain()
            dve.tensor_scalar(MSQ, MSQ, RMS_EPS, None, ALU.add)
            dve.drain()
            rsqrt(RSTD, MSQ, RTMP)
            dve.wait_ge(mod_cols, 1)
            dve.tensor_tensor(MODC, ps[:, 0, 0:32], COLS[:, 32:64], ALU.add)
            dve.drain()
            dve.scalar_tensor_tensor(COEF[:, 0:16], MODC[:, 16:32], 1.0, COLS[:, 16:32], ALU.add, ALU.mult)
            dve.tensor_copy(COEF[:, 16:32], MODC[:, 0:16]).then_inc(mod_scale, 1)
            dve.wait_ge(mod_row, 1)
            for t in range(TT):
                dve.tensor_scalar(SRC[:, t, :], SUM[:, t, :], RSTD[:, t:t + 1], None, ALU.mult).then_inc(x_norm, 1)
            for h in range(2):
                split_lo(dve, 0, 0, h)
            for g in range(8):
                dve.wait_ge(tp_hi, G_H + g + 1)
                for j in range(2):
                    k = 2 * g + j
                    dve.tensor_scalar(HTMP[:, j, :], tp(g % 4)[:, j * T:(j + 1) * T], COEF[:, k:k + 1],
                                      COEF[:, 16 + k:17 + k], ALU.mult, ALU.add)
                dve.drain()
                dve.tensor_tensor(alo[:, 2 * g:2 * g + 2, :], HTMP, ahi[:, 2 * g:2 * g + 2, :].bitcast(F32),
                                  ALU.subtract).then_inc(tp_lo, 1)
                dve.drain()

            def split_lo_block(i, per, h):
                for q in range(8):
                    split_lo(dve, i, per, h + q + 2)

            split_lo(dve, 0, 0, 2)
            split_lo(dve, 0, 0, 3)
            for b in range(2):
                split_lo_block(0, 0, H_FIRST + 8 * b)
            for turns, h in ((2, H_IN), (9, H_IN + 32)):
                with dve.Fori(0, turns) as i:
                    for b in range(2):
                        split_lo_block(i, 16, h + 8 * b)

            dve.wait_ge(w_lora, 48)
            dve.tensor_tensor(LIN[:, 1], LIN[:, 1], LIN[:, 0], ALU.subtract)
            dve.memset(ST[:, 0, :], 0.0)
            dve.memset(LORAW[LORA:LORA + 1, :], 1.0)
            dve.memset(LORAA[LORA:LORA + 1, :], 1.0).then_inc(w_loras, 1)
            dve.drain()
            dve.tensor_tensor(LIN[:, 1], LIN[:, 1], bc(MUL, TT), ALU.mult)
            dve.drain()
            dve.tensor_tensor(LIN[:, 0], LIN[:, 0], LIN[:, 1], ALU.add).then_inc(w_prep, 1)
            R, K, V = (CUR[:, :, n, :] for n in range(3))

            def heads(ap):
                return ap.rearrange("p t (h n) -> p t h n", h=2)

            def per_head(ap):
                return ap.rearrange("p (t h) -> p t h", t=TT).unsqueeze(3).to_broadcast([P, TT, 2, 64])

            def th(ap):
                return ap.rearrange("p (t h) -> p t h", t=TT)

            dve.wait_ge(w_kin, 16)
            with dve.Fori(0, HP) as i:
                dve.wait_ge(w_in_s, i * 96 + 96)
                cur, prv = (a.rearrange("p t q n -> p t (q n)") for a in (CUR, PRV))
                dve.tensor_tensor(prv, prv, cur, ALU.subtract)
                dve.drain()
                dve.tensor_tensor(prv, prv, bc(PRM[:, 0:3, :].rearrange("p q n -> p (q n)"), TT), ALU.mult)
                dve.drain()
                dve.tensor_tensor(cur, cur, prv, ALU.add)
                dve.drain()
                dve.tensor_tensor(KK, K, bc(PRM[:, 3, :], TT), ALU.mult)
                dve.drain()
                dve.tensor_tensor(RK, KK, KK, ALU.mult)
                dve.drain()
                dve.tensor_reduce(th(WST[:, 0:4]), heads(RK), AX.X, ALU.add)
                dve.drain()
                dve.tensor_scalar(WST[:, 0:4], WST[:, 0:4], 1e-24, None, ALU.max)
                dve.drain()
                rsqrt(WST[:, 4:8], WST[:, 0:4], WST[:, 16:20])
                dve.wait_ge(w_tanh, i + 1)
                sg = SG.rearrange("p a t n -> p (a t n)")
                dve.tensor_scalar(sg, sg, 0.5, 0.5, ALU.mult, ALU.add)
                dve.drain()
                dve.tensor_scalar(LD, SG[:, 0], -math.exp(-0.5), None, ALU.mult).then_inc(w_ld, 1)
                dve.scalar_tensor_tensor(K2, SG[:, 1], -1.0, bc(PRM[:, 4, :], TT), ALU.add, ALU.mult)
                dve.drain()
                dve.scalar_tensor_tensor(K2, K2, 1.0, K, ALU.add, ALU.mult)
                dve.drain()
                dve.tensor_tensor(RK, R, K2, ALU.mult)
                dve.drain()
                dve.tensor_tensor(RK, RK, bc(PRM[:, 5, :], TT), ALU.mult)
                dve.drain()
                dve.tensor_reduce(th(WST[:, 8:12]), heads(RK), AX.X, ALU.add)
                dve.drain()
                dve.tensor_tensor(heads(BV), heads(V), per_head(WST[:, 8:12]), ALU.mult)
                dve.tensor_tensor(heads(KK), heads(KK), per_head(WST[:, 4:8]), ALU.mult)
                dve.drain()
                dve.tensor_tensor(BB, KK, SG[:, 1], ALU.mult)
                dve.drain()
                dve.wait_ge(w_exp, i + 1)
                dve.scalar_tensor_tensor(TOK[:, :, 0, :], KK, -1.0, EXPS[:, 1], ALU.mult, ALU.mult)
                dve.tensor_tensor(TOK[:, :, 1, :], R, EXPS[:, 0], ALU.mult)
                dve.tensor_tensor(TOK[:, :, 2, :], BB, EXPS[:, 2], ALU.mult)
                dve.tensor_tensor(TOK[:, :, 3, :], K2, EXPS[:, 2], ALU.mult).then_inc(w_tok, 1)
                for t in range(TT):
                    dve.wait_ge(w_gram, i * 2 + (t + 1))
                    dve.tensor_tensor(GR[:, 2 * t:2 * t + 2].rearrange("p u g n -> p u (g n)"), ps[:, 4:6, :],
                                      bc(MASKS[:, 0:4, :].rearrange("p g n -> p (g n)"), 2), ALU.mult)
                    dve.tensor_tensor(MM[:, 2 * t:2 * t + 2, :], ps[:, 6:8, t * P:(t + 1) * P], bc(MASKS[:, 4, :], 2),
                                      ALU.mult).then_inc(w_mask, 1)
                dve.drain()
                dve.tensor_tensor(TM, MM, bc(MASKS[:, 10, :], 4), ALU.mult)
                dve.tensor_tensor(TMT, GR[:, :, 0, :], bc(MASKS[:, 11, :], 4), ALU.mult)
                dve.drain()
                dve.tensor_tensor(TM, TM, bc(ident[:, :], 4), ALU.add)
                dve.tensor_tensor(TMT, TMT, bc(ident[:, :], 4), ALU.add).then_inc(w_t0, 1)
                for lv in range(5):
                    dve.wait_ge(w_dt, i * 5 + (lv + 1))
                    if lv < 4:
                        dve.tensor_tensor(TM, TM, tp(1).rearrange("p (u n) -> p u n", u=4), ALU.add)
                    dve.tensor_tensor(TMT, TMT, tp(2).rearrange("p (u n) -> p u n", u=4), ALU.add).then_inc(w_tn, 1)
                dve.wait_ge(w_sa0, i + 1)
                dve.tensor_copy(SA, tp(2)[:, 0:T].rearrange("p (u n) -> p u n", u=4)).then_inc(w_sae, 1)
                for c in range(NCH - 1):
                    decay = WST[:, 20 + c:21 + c]
                    if c:
                        dve.tensor_scalar(SPC, ST[:, c, :], decay, None, ALU.mult)
                        dve.drain()
                    dve.wait_ge(w_delta, i * 3 + (c + 1))
                    delta = tp(3)[:, c * 64:(c + 1) * 64]
                    if c:
                        dve.scalar_tensor_tensor(ST[:, c + 1, :], delta, decay, SPC, ALU.mult, ALU.add)\
                           .then_inc(w_state, 1)
                    else:
                        dve.tensor_scalar(ST[:, 1, :], delta, decay, None, ALU.mult).then_inc(w_state, 1)
                    t, rs = (c + 1) // 2, slice(CH * ((c + 1) % 2), CH * ((c + 1) % 2) + CH)
                    dve.wait_ge(w_sap, i * 3 + (c + 1))
                    dve.tensor_tensor(SA[rs, 2 * t:2 * t + 2, :], SA[rs, 2 * t:2 * t + 2, :], ps[rs, 4:6, 0:64],
                                      ALU.add).then_inc(w_sae, 1)
                dve.wait_ge(w_ye, i + 1)
                dve.tensor_reduce(WST[:, 24:28], YS, AX.X, ALU.add)
                dve.drain()
                dve.tensor_scalar(WST[:, 24:28], WST[:, 24:28], -1.0 / 64, None, ALU.mult)
                dve.drain()
                dve.tensor_tensor(YS, YS, bcl(WST[:, 24:28], 64), ALU.add)
                dve.drain()
                dve.tensor_tensor(YQ, YS, YS, ALU.mult)
                dve.drain()
                dve.tensor_reduce(WST[:, 28:32], YQ, AX.X, ALU.add)
                dve.drain()
                dve.tensor_scalar(WST[:, 12:16], WST[:, 28:32], 1.0 / 64, GN_EPS, ALU.mult, ALU.add)
                dve.drain()
                rsqrt(WST[:, 16:20], WST[:, 12:16], WST[:, 0:4])
                dve.tensor_tensor(YS, YS, bcl(WST[:, 16:20], 64), ALU.mult)
                dve.drain()
                ys = YS.rearrange("p (t h) n -> p t (h n)", t=TT)
                dve.tensor_tensor(ys, ys, bc(PRM[:, 6, :], TT), ALU.mult)
                dve.drain()
                dve.tensor_tensor(ys, ys, bc(PRM[:, 7, :], TT), ALU.add)
                dve.drain()
                dve.wait_ge(w_st, i * 16)
                dve.tensor_tensor(ys, ys, BV, ALU.add).then_inc(w_yo, 1)

            for c in range(2):
                dve.wait_ge(y_sig, c + 1)
                dve.tensor_tensor(YW, YW, ZA, ALU.mult)
                dve.tensor_tensor(ZB, ZB, BG, ALU.mult)
                dve.drain()
                dve.tensor_tensor(SRC[:, :, c * NB:(c + 1) * NB], YW, SZ[:, 0], ALU.mult)
                dve.tensor_tensor(ZB, ZB, SZ[:, 1], ALU.mult)
                dve.wait_ge(y_u, c + 1)
                for n in range(3):
                    dve.tensor_tensor(CG[:, n], CG[:, n], bc(CW[:, 2 - n, c * NB:(c + 1) * NB], TT), ALU.mult)
                dve.drain()
                dve.tensor_tensor(YT, CG[:, 0], CG[:, 1], ALU.add)
                dve.drain()
                dve.tensor_tensor(YT, YT, CG[:, 2], ALU.add)
                dve.drain()
                dve.tensor_tensor(SRC[:, :, DA + c * NB:DA + (c + 1) * NB], YT, ZB, ALU.mult).then_inc(y_src, 1)
            for g in range(8):
                take_lo(dve, G_Y + g, 2 * g)
            with dve.Fori(0, 4) as i:
                for q in range(4):
                    split_lo(dve, i, 8, H_PAB + q + 2)
                dve.wait_ge(half_done, i * 8 + (H_PAB + 4))
                dve.wait_ge(ga_sig, i + 1)
                dve.tensor_tensor(MT, acc(B_PAB), GA[:, 0], ALU.mult).then_inc(acc_free[B_PAB % 2], 1)
                for q in range(4, 8):
                    split_lo(dve, i, 8, H_PAB + q + 2)
                dve.wait_ge(half_done, i * 8 + (H_PAB + 8))
                dve.tensor_tensor(MU, acc(B_PAB + 1), GA[:, 1], ALU.mult).then_inc(acc_free[(B_PAB + 1) % 2], 1)
                dve.drain()
                dve.tensor_tensor(SRC[:, :, ds(i * NB, NB)], MT, MU, ALU.add).then_inc(m_done, 1)
                dve.drain()
            for g in range(8):
                take_lo(dve, G_M + g, 2 * g)
            with dve.Fori(0, 2) as i:
                for b in range(2):
                    split_lo_block(i, 16, H_OUT + 8 * b)
            dve.wait_ge(o_bc, 64)
            dve.tensor_tensor(GB[:, 0], GB[:, 0], GB[:, 1], ALU.add)
            dve.drain()
            dve.tensor_tensor(GB[:, 0], GB[:, 0], GB[:, 2], ALU.mult)
            dve.drain()
            dve.wait_ge(o_sq, 2)
            dve.tensor_scalar(MSQ, MSQ, 1.0 / D, RMS_EPS, ALU.mult, ALU.add)
            dve.drain()
            rsqrt(RSTD, MSQ, RTMP)
            for t in range(TT):
                dve.scalar_tensor_tensor(SUM[:, t, :], SUM[:, t, :], RSTD[:, t:t + 1], GB[:, 0], ALU.mult, ALU.mult)
                dve.drain()
                dve.tensor_tensor(XRES[:, t, :], XRES[:, t, :], SUM[:, t, :], ALU.add).then_inc(x1_done, 1)
            for g in range(8):
                take_lo(dve, G_X1 + g, 2 * g)

            def ffn(h0, blk, g0, n0, zeroed):
                def gate_up(i, per, h, b, n):
                    split_lo_block(i, per, h)
                    dve.wait_ge(ff_sig, i + n)
                    dve.tensor_tensor(GS, acc(b), SIG, ALU.mult).then_inc(acc_free[b % 2], 1)
                    split_lo_block(i, per, h + 8)
                    dve.wait_ge(half_done, i * per + (h + 16))
                    dve.tensor_tensor(HID, acc(b + 1), GS, ALU.mult).then_inc(acc_free[(b + 1) % 2], 1)

                def hidden_lo(i, g):
                    for j in range(2):
                        dve.wait_ge(tp_hi, i * 2 + (g + j + 1))
                        dve.tensor_tensor(glo[:, 2 * j:2 * j + 2, :], tp(j).rearrange("p (k t) -> p k t", k=2),
                                          ghi[:, 2 * j:2 * j + 2, :].bitcast(F32), ALU.subtract).then_inc(tp_lo, 1)

                def down(i, per, h, b):
                    for n in range(4):
                        split_lo(dve, i, per, h + 2 * n + 2)
                        split_lo(dve, i, per, h + 2 * n + 3)
                        dve.wait_ge(half_done, i * per + (h + 2 * n + 2))
                        part = SUM[:, :, n * NB:(n + 1) * NB]
                        dve.tensor_tensor(part, part, acc(b + n), ALU.add).then_inc(acc_free[(b + n) % 2], 1)

                gate_up(0, 0, h0, blk, n0 + 1)
                hidden_lo(0, g0)
                dve.wait_ge(ff_zero, zeroed)
                with dve.Fori(0, FB - 1) as i:
                    gate_up(i, 24, h0 + 16, blk + 2, n0 + 2)
                    down(i, 24, h0 + 32, blk + 4)
                    hidden_lo(i, g0 + 2)
                down(0, 0, h0 + 24 * FB - 8, blk + 6 * FB - 4)
                dve.drain()

            def layer_norm(n, scale):
                for t in range(TT):
                    dve.tensor_scalar(XRES[:, t, :], XRES[:, t, :], ALPHA, None, ALU.mult)
                    dve.drain()
                    dve.scalar_tensor_tensor(SUM[:, t, :], SUM[:, t, :], scale, XRES[:, t, :], ALU.mult, ALU.add)
                    dve.drain()
                    stats(SUM, t)
                dve.drain()
                dve.tensor_scalar(MSQ, MV[:, :, 1], LN_EPS, None, ALU.add)
                dve.drain()
                rsqrt(RSTD, MSQ, RTMP)
                dve.wait_ge(n_bc, 32 * (n + 1))
                for t in range(TT):
                    dve.tensor_scalar(XRES[:, t, :], SUM[:, t, :], MV[:, t, 0:1], RSTD[:, t:t + 1], ALU.subtract,
                                      ALU.mult)
                    dve.drain()
                    dve.tensor_tensor(XRES[:, t, :], XRES[:, t, :], NG[:, 0], ALU.mult)
                    dve.drain()
                    dve.tensor_tensor(XRES[:, t, :], XRES[:, t, :], NG[:, 1], ALU.add).then_inc(x_done, 1)

            ffn(H_FFN1, B_FFN1, G_FFN1, 0, 1)
            layer_norm(0, 0.5)
            for g in range(8):
                take_lo(dve, G_X2 + g, 2 * g)
            with dve.Fori(0, 6) as i:
                for b in range(2):
                    split_lo_block(i, 16, H_IN2 + 8 * b)

            for cb in range(2):
                for part in range(3):
                    u = 3 * cb + part
                    dve.wait_ge(hy_in, 64 * (u + 1))
                    for s in range(3):
                        dve.tensor_tensor(HL[:, s], HL[:, s], bc(HW[:, s, :], TT), ALU.mult)
                    dve.drain()
                    dve.tensor_tensor(HZ[:, part], HL[:, 0], HL[:, 1], ALU.add)
                    dve.tensor_tensor(HL[:, 2], HL[:, 2], bc(HW[:, 3, :], TT), ALU.add)
                    dve.drain()
                    dve.tensor_tensor(HZ[:, part], HZ[:, part], HL[:, 2], ALU.add).then_inc(hy_z, 1)
                for n in range(2):
                    u = 2 * cb + n
                    dve.wait_ge(hy_f, u + 1)
                    dve.wait_ge(hy_kin, 16 * (u + 1))
                    re, im = ps[:, 4:6, :], ps[:, 6:8, :]
                    dve.tensor_tensor(HY_[:, 0:2], re, HK[:, 0:2], ALU.mult)
                    dve.tensor_tensor(HT[:, 0], im, HK[:, 2:4], ALU.mult)
                    dve.tensor_tensor(HY_[:, 2:4], re, HK[:, 2:4], ALU.mult)
                    dve.tensor_tensor(HT[:, 1], im, HK[:, 0:2], ALU.mult)
                    dve.drain()
                    dve.tensor_tensor(HY_[:, 0:2], HY_[:, 0:2], HT[:, 0], ALU.subtract)
                    dve.tensor_tensor(HY_[:, 2:4], HY_[:, 2:4], HT[:, 1], ALU.add).then_inc(hy_m, 1)
                    dve.wait_ge(hy_i, u + 1)
                    dst = HZ[:, 0] if n == 0 else SRC[:, :, cb * NB:(cb + 1) * NB]
                    dve.tensor_tensor(dst, ps[:, 0:2, :], HZ[:, 1 + n], ALU.mult).then_inc(hy_y, 1)
                    dve.drain()
            for t in range(TT):
                for s in range(2):
                    dve.bn_stats(STATS[:, t, s, :], SRC[:, t, s * NB:(s + 1) * NB])
                dve.drain()
                dve.bn_aggr(MV[:, t, :], STATS[:, t, 0:2])
            dve.drain()
            dve.tensor_tensor(MSQ, MV[:, :, 0], MV[:, :, 0], ALU.mult)
            dve.drain()
            dve.tensor_tensor(MSQ, MSQ, MV[:, :, 1], ALU.add)
            dve.drain()
            dve.tensor_scalar(MSQ, MSQ, LN_EPS, None, ALU.add)
            dve.drain()
            rsqrt(RSTD, MSQ, RTMP)
            dve.wait_ge(hy_tab, 80)
            for t in range(TT):
                dve.scalar_tensor_tensor(SRC[:, t, 0:DA], SRC[:, t, 0:DA], RSTD[:, t:t + 1], HG, ALU.mult, ALU.mult)\
                   .then_inc(hy_g, 1)

            dve.wait_ge(at_in, 96)
            for n, x in enumerate((AQ, AK)):
                g = x.rearrange("p t (g e) -> p t g e", e=64)
                a, b = g[:, :, :, 0:8], g[:, :, :, 8:16]
                cos, sin = (ROPE[:, s].unsqueeze(2).to_broadcast([P, TT, 16, 8]) for s in range(2))
                tmp = [RT[:, s].rearrange("p t (g e) -> p t g e", e=8) for s in range(4)]
                for dst, src, tab in ((tmp[0], a, cos), (tmp[1], b, sin), (tmp[2], b, cos), (tmp[3], a, sin)):
                    dve.tensor_tensor(dst, src, tab, ALU.mult)
                dve.drain()
                dve.tensor_tensor(a, tmp[0], tmp[1], ALU.subtract)
                dve.tensor_tensor(b, tmp[2], tmp[3], ALU.add).then_inc(at_rope, 1)
                dve.drain()
            for n in range(2):
                dve.tensor_tensor(RT[:, n, 0, 0:64], LAM[:, 2 * n], LAM[:, 2 * n + 1], ALU.mult)
            dve.drain()
            dve.tensor_reduce(AST[:, 0:2], RT[:, 0:2, 0, 0:64], AX.X, ALU.add).then_inc(at_lam, 1)
            dve.wait_ge(at_le, 1)
            dve.scalar_tensor_tensor(AST[:, 4:5], AST[:, 2:3], LAMBDA_INIT, AST[:, 3:4], ALU.add, ALU.subtract)
            dve.tensor_scalar(SUBG, SUBG, 1.0 - LAMBDA_INIT, None, ALU.mult)
            dve.drain()

            def maxima(h):
                dve.wait_ge(at_s, h + 1)
                n = 8 + 4 * h
                dve.tensor_reduce(AST[:, n:n + 4], ps[:, 2 * (h % 2):2 * (h % 2) + 2, :]
                                  .rearrange("p m (t k) -> p (m t) k", t=TT), AX.X, ALU.max)
                dve.drain()
                dve.tensor_scalar(AST[:, n:n + 4], AST[:, n:n + 4], -0.125, None, ALU.mult).then_inc(at_max, 1)

            maxima(0)
            for h in range(8):
                if h < 7:
                    maxima(h + 1)
                dve.wait_ge(at_e, h + 1)
                n = 40 + 4 * h
                dve.reciprocal(AST[:, 72:76], AST[:, n:n + 4])
                dve.drain()
                dve.tensor_scalar(AST[:, 76:78], AST[:, 74:76], AST[:, 4:5], None, ALU.mult)
                dve.drain()
                if h:
                    dve.wait_ge(at_wt, h)
                for t in range(TT):
                    dve.tensor_scalar(EE[:, 1, t, :], EE[:, 1, t, :], AST[:, 76 + t:77 + t], None, ALU.mult)
                dve.drain()
                for t in range(TT):
                    ins = dve.scalar_tensor_tensor(WW[:, t, :], EE[:, 0, t, :], AST[:, 72 + t:73 + t], EE[:, 1, t, :],
                                                   ALU.mult, ALU.subtract)
                ins.then_inc(at_w, 1)
            dve.wait_ge(at_oe, 8)
            dve.tensor_tensor(AO2, AO, AO, ALU.mult)
            dve.drain()
            dve.tensor_reduce(AMS, AO2.rearrange("p t (h n) -> p (t h) n", n=P), AX.X, ALU.add)
            dve.drain()
            dve.tensor_scalar(AMS, AMS, 1.0 / P, LN_EPS, ALU.mult, ALU.add)
            dve.drain()
            rsqrt(ARS, AMS, AST[:, 80:96])
            for t in range(TT):
                ao = AO[:, t, :].rearrange("p (h n) -> p h n", n=P)
                dve.tensor_tensor(ao, ao, bcl(ARS[:, 8 * t:8 * t + 8], P), ALU.mult)
                dve.drain()
                dve.tensor_tensor(ao, ao, bc(SUBG, 8), ALU.mult).then_inc(at_g, 1)
            for g in range(8):
                take_lo(dve, G_Y2 + g, 2 * g)
            with dve.Fori(0, 2) as i:
                for b in range(2):
                    split_lo_block(i, 16, H_OUT2 + 8 * b)
            for b in range(2):
                dve.wait_ge(acc_free[b], (B_OUT2 + 4 - b) // 2 + (1 if (B_OUT2 + 4 - b) % 2 else 0))
            layer_norm(1, 1.0)
            for g in range(8):
                take_lo(dve, G_X3 + g, 2 * g)
            ffn(H_FFN2, B_FFN2, G_FFN2, FB, 2)
            layer_norm(2, 0.5)



def constants():
    t = np.arange(T)
    theta = 2.0 * np.pi * (np.arange(T) + 0.5) / (2 * T)
    ang = np.outer(t, theta)
    dft = np.stack([np.cos(ang), -np.sin(ang), np.cos(ang).T / T, -np.sin(ang).T / T])
    bands = 16
    lin = np.linspace(0.0, 1.0, T, dtype=np.float32)[:, None]
    w = (2.0 * np.pi * np.arange(T)[:, None] / T).astype(np.float32)
    f = np.linspace(1e-4, bands - 1, bands, dtype=np.float32)[None, :]
    fw = (f * w).astype(np.float64)
    z = np.concatenate([lin, np.cos(fw), -np.sin(fw)], axis=-1)
    lo, hi = math.log(1e-2) / 1.5, math.log(1e-2) / 0.3
    deltas = np.abs(np.linspace(lo, hi, DA))
    decay = np.exp(-lin.astype(np.float64) * deltas)
    back = decay.copy()
    back[0] = 0.0
    inv = 500000.0 ** (-np.arange(0, 16, 2) / 16.0)
    pos = np.outer(t, inv.astype(np.float32))
    p = np.arange(P)
    same = p[:, None] // CH == p[None, :] // CH
    before = same & (p[:, None] < p[None, :])
    upto = same & (p[:, None] <= p[None, :])
    levels = []
    for s in (1, 2, 4, 8, 16, 32):
        pair = p[:, None] // (2 * s) == p[None, :] // (2 * s)
        levels.append(pair & (p[:, None] // s % 2 == 0) & (p[None, :] // s % 2 == 1))
    steps = np.zeros((P, P))
    steps[p, p // CH] = 1.0
    masks = [before, upto, before, upto, before.T] + levels[1:] + [levels[0].T, levels[0], steps]
    return {
        "ident": np.eye(P), "dft": dft, "hy_zt": z.T, "hy_decay": np.stack([decay, back]),
        "rope": np.stack([np.cos(pos), np.sin(pos)]), "masks": np.stack(masks, axis=1),
        "zeros": np.zeros((1, N_IN)),
    }


def kernel(**inputs):
    import concourse.bacc as _bacc
    from concourse.bass_utils import run_bass_kernel_spmd as _run

    g = {n: np.asarray(a) for n, a in inputs.items()}
    arrays = {}
    for n in ("x", "c", "ada_b", "pre_gain", "post_gain", "ln1_g_2", "ln1_b_2", "ln2_g_2", "ln2_b_2", "ln3_g_2",
              "ln3_b_2", "hyena_norm_g_2", "subln_g_2"):
        arrays[n] = g[n]
    for n in ("ada_w", "w_in", "p_a", "p_b", "w_out", "ffn1_w_gate_2", "ffn1_w_up_2", "ffn1_w_down_2", "w_in_2",
              "w_out_2", "ffn2_w_gate_2", "ffn2_w_up_2", "ffn2_w_down_2", "conv_w", "filt_w1_2", "filt_w2_2",
              "filt_w3_2", "filt_w_out_2", "hyena_bias_2"):
        arrays[n] = g[n][0]
    mu = g["mu_shift"][0]
    arrays["mu_lora"] = mu[None, 3 * DA:]
    arrays["wkv_rows"] = np.stack([mu[0:DA], mu[DA:2 * DA], mu[2 * DA:3 * DA], g["k_k"][0], g["k_a"][0],
                                   g["r_k"][0].reshape(DA), g["lnx_gain"][0], g["lnx_bias"][0]])
    arrays["lora_w"] = np.stack([np.concatenate([g["w2"][0], g["w0"]]), np.concatenate([g["a2"][0], g["a0"]])])
    arrays["filt_cols"] = np.stack([g["filt_b1_2"][0], g["filt_b2_2"][0], g["filt_b3_2"][0], g["filt_freq_2"][0]],
                                   axis=1)
    arrays["hyena_rows"] = np.concatenate([g["hyena_conv_w_2"][0], g["hyena_conv_b_2"]])
    arrays["lambdas"] = np.concatenate([g["lambda_q1_2"], g["lambda_k1_2"], g["lambda_q2_2"], g["lambda_k2_2"]])
    for n, a in constants().items():
        arrays[n] = a.astype(np.float32)
    arrays = {f"in_{n}": np.ascontiguousarray(a) for n, a in arrays.items()}

    nc = _bacc.Bacc("TRN2", target_bir_lowering=False, num_devices=1)
    aps = {n[3:]: nc.dram_tensor(n, a.shape, F32, kind="ExternalInput").ap() for n, a in arrays.items()}
    out = nc.dram_tensor("out", (1, T, D), F32, kind="ExternalOutput").ap()
    with nc.allow_non_contiguous_dma(reason="short rows of parameters"):
        build(nc, aps, out)
    r = _run(nc, [arrays], core_ids=[0])
    return r.results[0]["out"]
```

```python
from contextlib import ExitStack
import math

import numpy as np
import concourse.bass as bass
from concourse import mybir

F32 = mybir.dt.float32
F32R = mybir.dt.float32r
ALU = mybir.AluOpType
ACT = mybir.ActivationFunctionType
AX = mybir.AxisListType
ds = bass.ds

P = 128
T = 256
TT = T // P
D = 2048
KT = D // P
NB = 512
DA = 1024
HP = DA // P
LORA = 64
COLS_A = 3 * DA + 2 * LORA
OFF_ZA = COLS_A
OFF_B = OFF_ZA + DA
OFF_ZB = OFF_B + 3 * DA
OFF_GATE = OFF_B + 4 * DA
N_IN = OFF_GATE + 2 * D
F = 5632
FB = F // NB
D_IN = 6144
RMS_EPS = 1e-6
GN_EPS = 64e-5
LN_EPS = 1e-5
ALPHA = 2.0 ** 0.25
LAMBDA_INIT = 0.8 - 0.6 * math.exp(0.0)
CH = 64
NCH = T // CH
PARAM_ROWS = 8
TWO_PI_HI = 6.28125
TWO_PI_LO = 2.0 * math.pi - TWO_PI_HI
ROUND = 1.5 * 2.0 ** 23
PI_IN = 3.1415925

H_LORA = 0
H_FIRST = H_LORA + 2
H_IN = H_FIRST + 16
IN_BLOCKS = (N_IN - 2 * LORA) // NB
H_PAB = H_IN + 8 * (IN_BLOCKS - 2)
H_OUT = H_PAB + 4 * 8
H_FFN1 = H_OUT + 4 * 8
FFN_HALVES = 8 + 8 + 4 * 2
H_IN2 = H_FFN1 + FB * FFN_HALVES
H_HY = H_IN2 + 4 * 8
H_OUT2 = H_IN2 + 8 * (D_IN // NB)
H_FFN2 = H_OUT2 + 4 * 8
H_END = H_FFN2 + FB * FFN_HALVES

B_LORA = 0
B_FIRST = 1
B_IN = B_FIRST + 2
B_PAB = B_IN + IN_BLOCKS - 2
B_OUT = B_PAB + 8
B_FFN1 = B_OUT + 4
B_IN2 = B_FFN1 + FB * 6
B_HY = B_IN2 + 4
HY_PARTS = 5, 11, 18, 32, 38, 45
HY_UNITS = 21, 27, 48, 54
B_OUT2 = B_IN2 + D_IN // NB
B_FFN2 = B_OUT2 + 8


def build(nc, A, out):
    ctx = ExitStack()
    with ctx:
        def sb(name, shape, dt=F32):
            return ctx.enter_context(nc.sbuf_tensor(name, shape, dt))

        def sem(name):
            return ctx.enter_context(nc.semaphore(name))

        raw = sb("w_raw", [P, 4, 4 * NB])
        whi = sb("w_hi", [P, 4, 2 * NB], F32R)
        wlo = sb("w_lo", [P, 4, 2 * NB], F32R)
        ahi = sb("act_hi", [P, KT, T], F32R)
        alo = sb("act_lo", [P, KT, T], F32R)
        ghi = sb("hid_hi", [P, 4, T], F32R)
        glo = sb("hid_lo", [P, 4, T], F32R)
        ident = sb("ident", [P, P])
        ones = sb("ones", [P, P])
        small = sb("small", [P, 128])
        arena = sb("arena", [P, 25600])
        ps = ctx.enter_context(nc.psum_tensor("ps", [P, 8, NB], F32))

        def at(off, *dims):
            v = arena[:, off:off + math.prod(dims)]
            if len(dims) == 1:
                return v
            names = " ".join("abcd"[:len(dims)])
            return v.rearrange(f"p ({names}) -> p {names}", **dict(zip("abcd", dims)))

        def acc(block):
            b = 2 * (block % 2)
            return ps[:, b:b + 2, :]

        def tp(n):
            return ps[:, 4 + n, :]

        XRES = at(0, TT, D)
        SRC = at(4096, TT, D)
        SUM = at(8192, TT, D)
        STG = at(12288, 2, TT, NB)
        R5 = 14336

        proj1 = nc.dram_tensor("proj1", [T + 2, N_IN], F32).ap()
        proj2 = nc.dram_tensor("proj2", [T + 2, D_IN], F32).ap()
        wkv_out = nc.dram_tensor("wkv_out", [T, DA], F32).ap()
        filt = nc.dram_tensor("filt", [2, 2, P, 4 * NB], F32).ap()
        mod_gate = nc.dram_tensor("mod_gate", [1, D], F32).ap()
        hy_out = nc.dram_tensor("hy_out", [T, DA], F32).ap()

        def wait_alone(eng, semaphore, value):
            eng.wait_ge(semaphore, value)
            eng.sem_inc(waits_done, 1)

        def tokens(ap):
            return ap.rearrange("(t p) n -> p t n", p=P)

        def bc(ap, n):
            return ap.unsqueeze(1).to_broadcast([ap.shape[0], n, ap.shape[-1]])

        def rows(ap, n):
            return ap.partition_broadcast(n)

        raw_in = [sem(f"raw_in{n}") for n in range(4)]
        hi_ready = sem("hi_ready")
        lo_ready = sem("lo_ready")
        half_done = sem("half_done")
        acc_free = [sem(f"acc_free{n}") for n in range(2)]
        tp_ready = sem("tp_ready")
        tp_hi = sem("tp_hi")
        tp_lo = sem("tp_lo")
        stg_ready = sem("stg_ready")
        stg_out = [sem(f"stg_out{n}") for n in range(2)]
        s_const = sem("s_const")
        s_rows = sem("s_rows")
        s_ones = sem("s_ones")
        waits_done = sem("waits_done")
        ada_in = [sem(f"ada_in{n}") for n in range(4)]
        ada_done = sem("ada_done")
        rows_t = sem("rows_t")
        c_sig = sem("c_sig")
        c_act = sem("c_act")
        mod_cols = sem("mod_cols")
        mod_row = sem("mod_row")
        mod_row_sb = sem("mod_row_sb")
        mod_stored = sem("mod_stored")
        mod_scale = sem("mod_scale")
        x_in = sem("x_in")
        x_norm = sem("x_norm")
        f_in = sem("f_in")
        f_mlp = sem("f_mlp")
        f_arg = sem("f_arg")
        f_sin = sem("f_sin")
        f_h = sem("f_h")
        f_sd = sem("f_sd")
        f_sd0 = sem("f_sd0")
        f_k = sem("f_k")
        f_ke = sem("f_ke")
        f_dec = sem("f_dec")
        f_st = sem("f_st")
        zero_rows = sem("zero_rows")
        zero_st = sem("zero_st")


        def load_chunk(sp, i, per, h, src):
            slot = h // 2 % 4
            if h >= 8:
                sp.wait_ge(lo_ready, i * per + (h - 8 + 2))
            else:
                sp.wait_ge(ada_done, 44 + h // 2 + 1)
            dst = raw[:, slot, :].rearrange("p (k n) -> p k n", n=src.shape[-1])
            sp.dma_start(dst, src).then_inc(raw_in[slot], 16)

        def split_hi(act, i, per, h):
            if h >= H_END:
                return
            slot = h // 2 % 4
            if h % 2 == 0:
                act.wait_ge(raw_in[slot], i * (per * 2) + 16 * (h // 8 + 1))
            if h >= 4:
                act.wait_ge(half_done, i * per + (h - 4 + 1))
            act.activation(whi[:, h % 4, :], raw[:, slot, h % 2 * 2 * NB:(h % 2 + 1) * 2 * NB], ACT.Copy)\
               .then_inc(hi_ready, 1)

        def split_lo(dve, i, per, h):
            if h >= H_END:
                return
            dve.wait_ge(hi_ready, i * per + (h + 1))
            dve.tensor_tensor(wlo[:, h % 4, :], raw[:, h // 2 % 4, h % 2 * 2 * NB:(h % 2 + 1) * 2 * NB],
                              whi[:, h % 4, :].bitcast(F32), ALU.subtract).then_inc(lo_ready, 1)

        def products(pe, i, per, h, xh, xl, banks, first, last, cols=NB, part=None):
            nk = 2 * NB // cols
            ks = range(nk) if part is None else (part,)
            if 0 in ks:
                pe.wait_ge(lo_ready, i * per + (h + 1))
            hi = whi[:, h % 4, :].rearrange("p (k n) -> p k n", k=nk)
            lo = wlo[:, h % 4, :].rearrange("p (k n) -> p k n", k=nk)
            for k in ks:
                for t in range(TT):
                    ts = slice(t * P, (t + 1) * P)
                    dst = banks[:, t, 0:cols]
                    pe.matmul(dst, xh[:, k, ts], hi[:, k, :], start=first and k == 0, stop=False)
                    pe.matmul(dst, xh[:, k, ts], lo[:, k, :], start=False, stop=False)
                    mm = pe.matmul(dst, xl[:, k, ts], hi[:, k, :], start=False, stop=last and k == nk - 1)
            if part != 0:
                mm.then_inc(half_done, 1)

        def block_2048(pe, i, per, h, blk_per, blk):
            if blk >= 2:
                pe.wait_ge(acc_free[blk % 2], i * (blk_per // 2) + blk // 2)
            for q in range(8):
                products(pe, i, per, h + q, ahi[:, 2 * q:2 * q + 2, :], alo[:, 2 * q:2 * q + 2, :],
                         acc(blk), q == 0, q == 7)

        def transpose_group(pe, n, src, k):
            if n >= 4:
                pe.wait_ge(tp_lo, n - 3)
            for j in range(2):
                for t in range(TT):
                    mm = pe.transpose(tp(n % 4)[:, j * T + t * P:j * T + (t + 1) * P],
                                      src[:, t, (k + j) * P:(k + j + 1) * P], ident[:, :])
            mm.then_inc(tp_ready, 1)

        def take_hi(act, n, k):
            act.wait_ge(tp_ready, n + 1)
            act.activation(ahi[:, k:k + 2, :], tp(n % 4).rearrange("p (k t) -> p k t", k=2), ACT.Copy)\
               .then_inc(tp_hi, 1)

        def take_lo(dve, n, k):
            dve.wait_ge(tp_hi, n + 1)
            dve.tensor_tensor(alo[:, k:k + 2, :], tp(n % 4).rearrange("p (k t) -> p k t", k=2),
                              ahi[:, k:k + 2, :].bitcast(F32), ALU.subtract).then_inc(tp_lo, 1)

        G_H, G_Y, G_M, G_X1 = 0, 8, 16, 24
        G_FFN1 = 32
        G_X2 = G_FFN1 + 2 * FB
        G_Y2 = G_X2 + 8
        G_X3 = G_Y2 + 8
        G_FFN2 = G_X3 + 8

        ADA = at(0, 3 * D)
        WOF = at(6144, 4 * DA)
        DEC = at(10240, 2, TT, NB)
        BROW = at(12288, 2, DA)
        FC = at(14336, TT, T)
        FS = at(14848, TT, T)
        HFB = at(15360, 2, TT, NB)
        SD = at(17408, 2, TT, NB)
        KST = at(19456, 4, NB)
        ZT = at(21504, T)
        FW = at(21760, 3, 64)
        FCOL = at(21952, 4)
        H1 = at(21960, T)
        H2 = at(22216, T)
        ROWS = at(22472, P)
        COLS = at(22600, 64)
        CACT = at(22664, 32)
        MODC = at(22696, 32)
        GROW = at(22728, 2048)
        HTMP = at(24776, 2, T)
        COEF = small[:, 0:32]
        STATS = small[:, 64:112].rearrange("p (t s v) -> p t s v", t=TT, s=4)
        MV = small[:, 112:116].rearrange("p (t v) -> p t v", t=TT)
        MSQ = small[:, 116:118]
        RSTD = small[:, 118:120]
        RTMP = small[:, 120:122]

        ada_w = A["ada_w"].rearrange("(k p) n -> p k n", p=P)
        w_in = A["w_in"].rearrange("(k p) n -> p k n", p=P)
        wk = {n: A[n].rearrange("(k p) n -> p k n", p=P) for n in
              ("p_a", "p_b", "w_out", "ffn1_w_gate_2", "ffn1_w_up_2", "ffn1_w_down_2", "w_in_2", "w_out_2",
               "ffn2_w_gate_2", "ffn2_w_up_2", "ffn2_w_down_2")}

        HY = 3 * DA

        block = ctx.enter_context(nc.Block())

        @block.sync
        def _(sp):
            sp.dma_start(ident[:, :], A["ident"]).then_inc(s_const, 16)
            sp.dma_start(ROWS[0:16, :], A["c"].rearrange("a (k p) -> (a k) p", p=P)).then_inc(s_rows, 16)
            sp.dma_start(ROWS[16:32, :], A["pre_gain"].rearrange("a (k p) -> (a k) p", p=P)).then_inc(s_rows, 16)
            sp.dma_start(ROWS[32:64, :], A["ada_b"][:, 0:2 * D].rearrange("a (k p) -> (a k) p", p=P))\
              .then_inc(s_rows, 16)
            for n in range(48):
                if n >= 4:
                    sp.wait_ge(ada_done, n - 3)
                sp.dma_start(raw[:, n % 4, :], ada_w[:, n % 16, n // 16 * D:(n // 16 + 1) * D])\
                  .then_inc(ada_in[n % 4], 16)

            load_chunk(sp, 0, 0, H_LORA, w_in[:, :, 3 * DA:3 * DA + P])

            def load_block(i, per, h, w, col):
                for q in range(4):
                    load_chunk(sp, i, per, h + 2 * q, w[:, 4 * q:4 * q + 4, ds(col, NB)])

            for b in range(2):
                load_block(0, 0, H_FIRST + 8 * b, w_in, b * NB)
            with sp.Fori(0, 2) as i:
                for b in range(2):
                    load_block(i, 16, H_IN + 8 * b, w_in, i * (2 * NB) + (2 + b) * NB)
            with sp.Fori(0, 9) as i:
                for b in range(2):
                    load_block(i, 16, H_IN + 32 + 8 * b, w_in, i * (2 * NB) + (OFF_ZA + b * NB))
            with sp.Fori(0, 4) as i:
                for n, w in enumerate(("p_a", "p_b")):
                    for q in range(2):
                        load_chunk(sp, i, 8, H_PAB + 4 * n + 2 * q, wk[w][:, 4 * q:4 * q + 4, ds(i * NB, NB)])
            with sp.Fori(0, 2) as i:
                for b in range(2):
                    load_block(i, 16, H_OUT + 8 * b, wk["w_out"], i * (2 * NB) + b * NB)

            def load_ffn(h0, gate, up, down):
                load_block(0, 0, h0, wk[gate], 0)
                load_block(0, 0, h0 + 8, wk[up], 0)
                with sp.Fori(0, FB - 1) as i:
                    load_block(i, 24, h0 + 16, wk[gate], i * NB + NB)
                    load_block(i, 24, h0 + 24, wk[up], i * NB + NB)
                    for n in range(4):
                        load_chunk(sp, i, 24, h0 + 32 + 2 * n, wk[down][:, ds(i * 4, 4), n * NB:(n + 1) * NB])
                for n in range(4):
                    load_chunk(sp, 0, 0, h0 + 24 * FB - 8 + 2 * n,
                               wk[down][:, 4 * FB - 4:4 * FB, n * NB:(n + 1) * NB])

            load_ffn(H_FFN1, "ffn1_w_gate_2", "ffn1_w_up_2", "ffn1_w_down_2")
            with sp.Fori(0, 2) as i:
                for b in range(2):
                    load_block(i, 16, H_IN2 + 8 * b, wk["w_in_2"], i * (2 * NB) + b * NB)
            for b, col in enumerate((4, 5, 10, 11, 6, 7, 8, 9)):
                load_block(0, 0, H_HY + 8 * b, wk["w_in_2"], col * NB)
            for part in range(2):
                with sp.Fori(0, 2) as i:
                    for b in range(2):
                        for q in range(2):
                            k = 8 * part + 4 * q
                            load_chunk(sp, i, 8, H_OUT2 + 16 * part + 4 * b + 2 * q,
                                       wk["w_out_2"][:, k:k + 4, ds(i * (2 * NB) + b * NB, NB)])
            load_ffn(H_FFN2, "ffn2_w_gate_2", "ffn2_w_up_2", "ffn2_w_down_2")

        (w_mix, w_z, w_tanh, w_ld, w_cum, w_exp, w_tok, w_t4p, w_t4, w_gram, w_mask, w_t0,
         w_ms, w_u, w_ue, w_dt, w_tn, w_w1, w_w1e, w_sa0, w_sae, w_sap, w_delta, w_state, w_y, w_ye,
         w_yo, w_st, w_prep, w_lora, w_lorat, w_loras, w_kin) = [sem("wkv_" + n) for n in (
             "mix z tanh logdecay cumulated exp tok t4 t4_sb gram masked t0 "
             "m u u_sb dt tn w1 w1_sb sa0 sa sa_state delta state y y_sb out stored prep lora lora_t "
             "lora_sb const").split()]
        w_in_s = [sem(f"wkv_in{n}") for n in range(2)]
        y_in = sem("y_in")
        y_sig = sem("y_sig")
        y_u = sem("y_u")
        y_src = sem("y_src")
        y_free = sem("y_free")
        ga_in = sem("ga_in")
        ga_sig = sem("ga_sig")
        m_done = sem("m_done")
        o_bc = sem("o_bc")
        o_sq = sem("o_sq")
        x1_done = sem("x1_done")
        n_bc = sem("n_bc")
        x_done = sem("x_done")
        ff_sig = sem("ff_sig")
        ff_ghi = sem("ff_ghi")
        ff_glo = sem("ff_glo")
        ff_zero = sem("ff_zero")
        x_out = sem("x_out")
        hy_tab = sem("hy_tab")
        hy_in = sem("hy_in")
        hy_z = sem("hy_z")
        hy_kin = sem("hy_kin")
        hy_f = sem("hy_f")
        hy_m = sem("hy_m")
        hy_i = sem("hy_i")
        hy_y = sem("hy_y")
        hy_g = sem("hy_g")
        at_in = sem("at_in")
        at_lam = sem("at_lam")
        at_le = sem("at_le")
        at_rope = sem("at_rope")
        at_tp = sem("at_tp")
        at_tps = sem("at_tps")
        at_s = sem("at_s")
        at_max = sem("at_max")
        at_e = sem("at_e")
        at_w = sem("at_w")
        at_wt = sem("at_wt")
        at_wts = sem("at_wts")
        at_o = sem("at_o")
        at_oe = sem("at_oe")
        at_g = sem("at_g")

        CUR = at(0, TT, 3, P), at(18816, TT, 3, P)
        PRV = at(768, TT, 3, P), at(19584, TT, 3, P)
        PRM = at(1536, PARAM_ROWS, P), at(20352, PARAM_ROWS, P)
        WA = at(2560, 2, P), at(21376, 2, P)
        TOK = at(2816, TT, 4, P)
        T4 = at(3840, TT, 4, P)
        GR = at(4864, 4, 4, P)
        TM = at(6912, 4, P)
        TMT = at(7424, 4, P)
        MM = at(7936, 4, P)
        MS = at(8448, 4, P)
        UU = at(8960, 4, P)
        SG = at(9472, 2, TT, P)
        LD = at(9984, TT, P)
        KK = at(10240, TT, P)
        K2 = at(10496, TT, P)
        BB = at(10752, TT, P)
        RK = at(11008, TT, P)
        BV = at(11264, TT, P)
        EXPS = at(11520, 3, TT, P)
        W1S = at(14336, 4, 64)
        AEF = at(14592, TT, P)
        SA = at(14848, 4, 64)
        ST = at(15104, NCH, 64)
        SPC = at(15360, 64)
        YS = at(15424, 4, 64)
        YQ = at(15680, 4, 64)
        MASKS = at(15936, 13, P)
        LORAW = at(17600, T)
        LORAA = at(17856, T)
        LIN = at(18112, 2, TT, P)
        MUL = at(18624, P)
        WST = small[:, 32:64]

        YW = at(R5, TT, NB)
        ZA = at(R5 + 1024, TT, NB)
        BG = at(R5 + 2048, TT, NB)
        ZB = at(R5 + 3072, TT, NB)
        CG = at(R5 + 4096, 3, TT, NB)
        HB = at(R5 + 7168, 3, TT, NB)
        SZ = at(8192, 2, TT, NB)
        YT = at(8192 + 2048, TT, NB)
        CW = at(0, 3, DA)
        GA = at(R5, 2, TT, NB)
        MT = at(R5 + 2048, TT, NB)
        MU = at(R5 + 3072, TT, NB)
        GB = at(R5, 3, D)
        SIG = at(R5, TT, NB)
        GS = at(R5 + 1024, TT, NB)
        HID = at(R5 + 2048, TT, NB)
        NG = at(R5 + 4096, 2, D)
        AQ = at(8192, TT, DA)
        AK = at(10240, TT, DA)
        AV = SRC[:, :, DA:D]
        TAB = at(12288, 4, TT, T)
        HL = at(R5, 3, TT, NB)
        HT = at(10240, 2, 2, NB)
        HW = at(17408, 4, NB)
        HK = [g.bitcast(F32).rearrange("p k t -> p (k t)").rearrange("p (m n) -> p m n", n=NB) for g in (ghi, glo)]
        HZ = at(19456, 3, TT, NB)
        HY_ = at(22528, 4, NB)
        HG = at(24576, DA)
        QT = at(14336, 8, T)
        KTT = at(16384, 8, T)
        EE = at(18432, 2, TT, T)
        WW = at(19456, TT, T)
        WT2 = at(19968, 2, T)
        ROPE = at(20480, 2, TT, 8)
        LAM = at(20512, 4, 64)
        SUBG = at(20768, P)
        AO = AV
        AO2 = at(22528, TT, DA)
        RT = at(20896, 4, TT, 128)
        AST = at(21920, 128)
        AMS = at(22048, 16)
        ARS = at(22064, 16)

        @block.gpsimd
        def _(pool):
            pool.memset(ones[:, :], 1.0).then_inc(s_ones, 1)
            for dst, src in ((ZT[0:33, :], A["hy_zt"]), (FW[0:33, 0, :], A["filt_w1_2"]),
                             (FW[0:64, 1, :], A["filt_w2_2"]), (FW[0:64, 2, :], A["filt_w3_2"]),
                             (FCOL[0:64, 0:4], A["filt_cols"]), (WOF[0:64, :], A["filt_w_out_2"]),
                             (FC, A["dft"][0].rearrange("(t p) f -> p t f", p=P)),
                             (FS, A["dft"][1].rearrange("(t p) f -> p t f", p=P)),
                             (BROW[0:1, :, :], A["hyena_bias_2"].rearrange("(a n) c -> a n c", a=1))):
                pool.dma_start(dst, src).then_inc(f_in, 16)
            for r in range(2):
                pool.dma_start(proj1[r:r + 1, 0:OFF_ZB], A["zeros"][:, 0:OFF_ZB]).then_inc(zero_rows, 16)
            for r in (0, T + 1):
                pool.dma_start(proj2[r:r + 1, 0:HY], A["zeros"][:, 0:HY]).then_inc(zero_rows, 16)
            for u in range(4):
                cb, n = u // 2, u % 2
                if n == 0:
                    if u:
                        pool.wait_ge(f_sd0, u)
                    for d in range(2):
                        pool.dma_start(DEC[:, d], A["hy_decay"][d].rearrange("(t p) n -> p t n", p=P)
                                       [:, :, cb * NB:(cb + 1) * NB]).then_inc(f_dec, 16)
                pool.wait_ge(f_ke, u + 1)
                pool.dma_start(filt[n, cb], KST).then_inc(f_st, 16)
            pool.wait_ge(f_sd0, 4)
            for t in range(TT):
                pool.dma_start(SUM[:, t, :], A["x"][0, t * P:(t + 1) * P, :]).then_inc(x_in, 16)
            pool.wait_ge(mod_row_sb, 1)
            pool.dma_start(mod_gate, GROW[0:1, :]).then_inc(mod_stored, 16)

            def store_block(i, per2, s, blk, dst):
                wait_alone(pool, acc_free[blk % 2], i * per2 + (blk // 2 + 1))
                pool.dma_start(dst, STG[:, s % 2, :, 0:dst.shape[-1]]).then_inc(stg_out[s % 2], 16)

            p1 = tokens(proj1[2:T + 2, :])
            store_block(0, 0, 0, B_LORA, p1[:, :, 3 * DA:3 * DA + P])
            for b in range(2):
                store_block(0, 0, 1 + b, B_FIRST + b, p1[:, :, b * NB:(b + 1) * NB])
            with pool.Fori(0, 2) as i:
                for b in range(2):
                    store_block(i, 1, 3 + b, B_IN + b, p1[:, :, ds(i * (2 * NB) + (2 + b) * NB, NB)])

            pool.sem_inc(w_yo, 1)
            pool.wait_ge(stg_out[0], 16 * 4)
            pool.wait_ge(stg_out[1], 16 * 3)
            pool.wait_ge(zero_rows, 64)
            for a, w in enumerate((LIN[:, 0], LIN[:, 1])):
                pool.dma_start(w, tokens(proj1[2 - a:T + 2 - a, 3 * DA:3 * DA + P])).then_inc(w_lora, 16)
            pool.dma_start(MUL, A["mu_lora"].rearrange("a n -> (a n)").partition_broadcast(P)).then_inc(w_lora, 16)
            pool.dma_start(MASKS, A["masks"]).then_inc(w_kin, 16)

            def load_pair(i, p):
                for a, w in enumerate((CUR[p % 2], PRV[p % 2])):
                    for t in range(TT):
                        pool.dma_start(w[:, t], proj1[2 - a + t * P:2 - a + (t + 1) * P, 0:3 * DA]
                                       .rearrange("r (q n) -> r q n", q=3)[:, :, ds(i * (2 * P) + p * P, P)])\
                            .then_inc(w_in_s[p % 2], 16)
                pool.dma_start(PRM[p % 2], A["wkv_rows"][:, ds(i * (2 * P) + p * P, P)].partition_broadcast(P))\
                    .then_inc(w_in_s[p % 2], 16)
                pool.dma_start(WA[p % 2][0:LORA + 1], A["lora_w"].rearrange("a k n -> k a n")
                               [:, :, ds(i * (2 * P) + p * P, P)]).then_inc(w_in_s[p % 2], 16)

            def mix_pair(i, p):
                pool.wait_ge(w_in_s[p % 2], i * 96 + (96 * (p // 2) + 96))
                cur, prv = (a.rearrange("p t q n -> p t (q n)") for a in (CUR[p % 2], PRV[p % 2]))
                pool.tensor_tensor(prv, prv, cur, ALU.subtract)
                pool.drain()
                pool.tensor_tensor(prv, prv, bc(PRM[p % 2][:, 0:3, :].rearrange("p q n -> p (q n)"), TT), ALU.mult)
                pool.drain()
                pool.tensor_tensor(cur, cur, prv, ALU.add).then_inc(w_mix, 1)

            def pair(i, p, more):
                wait_alone(pool, w_yo, i * 2 + (p + 1))
                if more:
                    load_pair(i, p + 1)
                for lv in range(5):
                    if lv == 0:
                        pool.wait_ge(w_mask, i * 4 + (2 * p + 2))
                    else:
                        pool.wait_ge(w_u, i * 10 + (5 * p + lv))
                    mt = GR.rearrange("p u g n -> p g u n")[:, 0]
                    pool.tensor_tensor(MS, mt, MASKS[:, 5 + lv, :].unsqueeze(1).to_broadcast([P, 4, P]), ALU.mult)\
                        .then_inc(w_ms, 1)
                    if lv == 2:
                        store_block(i, 2, 9 + 2 * p, B_IN + 6 + 2 * p,
                                    p1[:, :, ds(i * (4 * NB) + (OFF_ZA + (2 + 2 * p) * NB), NB)])
                if more:
                    mix_pair(i, p + 1)
                wait_alone(pool, w_yo, i * 2 + (p + 2))
                pool.dma_start(tokens(wkv_out)[:, :, ds(i * (2 * P) + p * P, P)],
                               YS.rearrange("p (t h) n -> p t (h n)", t=TT)).then_inc(w_st, 16)
                store_block(i, 2, 10 + 2 * p, B_IN + 7 + 2 * p,
                            p1[:, :, ds(i * (4 * NB) + (OFF_ZA + (3 + 2 * p) * NB), NB)])
                wait_alone(pool, w_st, i * 32 + (16 * p + 16))

            load_pair(0, 0)
            mix_pair(0, 0)
            for b in range(2):
                store_block(0, 0, 7 + b, B_IN + 4 + b, p1[:, :, OFF_ZA + b * NB:OFF_ZA + (b + 1) * NB])
            with pool.Fori(0, HP // 2 - 1) as i:
                for p in range(2):
                    pair(i, p, True)
            for p in range(2):
                pair(HP // 2 - 1, p, p == 0)
            pool.wait_ge(stg_out[0], 16 * 13)
            pool.wait_ge(stg_out[1], 16 * 12)

            pool.wait_ge(w_st, 16 * HP)
            pool.dma_start(CW, A["conv_w"].partition_broadcast(P)).then_inc(y_in, 16)
            for c in range(2):
                if c:
                    pool.wait_ge(y_src, c)
                cs = slice(c * NB, (c + 1) * NB)
                pool.dma_start(YW, tokens(wkv_out)[:, :, cs]).then_inc(y_in, 16)
                for dst, off, back in ((ZA, OFF_ZA, 0), (BG, OFF_B, 0), (ZB, OFF_ZB, 0),
                                       (CG[:, 0], OFF_B + DA, 0), (CG[:, 1], OFF_B + DA, 1), (CG[:, 2], OFF_B + DA, 2),
                                       (HB[:, 0], OFF_B + 2 * DA, 0), (HB[:, 1], OFF_B + 2 * DA, 1),
                                       (HB[:, 2], OFF_B + 2 * DA, 2)):
                    pool.dma_start(dst, tokens(proj1[2 - back:T + 2 - back, off + c * NB:off + (c + 1) * NB]))\
                        .then_inc(y_in, 16)
                pool.wait_ge(y_in, 16 + 160 * (c + 1))
                pool.tensor_tensor(CG, CG, HB, ALU.mult).then_inc(y_u, 1)
            pool.wait_ge(y_src, 2)
            pool.sem_inc(m_done, 1)
            with pool.Fori(0, 4) as i:
                wait_alone(pool, m_done, i + 1)
                for n in range(2):
                    pool.dma_start(GA[:, n], p1[:, :, ds(i * NB + (OFF_GATE + n * D), NB)]).then_inc(ga_in, 16)
            pool.wait_ge(m_done, 5)
            pool.wait_ge(mod_stored, 16)
            for n, src in enumerate((mod_gate[0], A["ada_b"][0, 2 * D:3 * D], A["post_gain"][0])):
                pool.dma_start(GB[:, n], rows(src, P)).then_inc(o_bc, 16)
            pool.dma_start(XRES, tokens(A["x"][0])).then_inc(o_bc, 16)

            def norm_rows(n, g, b):
                if n:
                    pool.wait_ge(x_done, 2 * n)
                for j, name in enumerate((g, b)):
                    pool.dma_start(NG[:, j], rows(A[name][0], P)).then_inc(n_bc, 16)

            pool.wait_ge(x1_done, 2)
            pool.memset(SUM, 0.0).then_inc(ff_zero, 1)
            norm_rows(0, "ln1_g_2", "ln1_b_2")

            p2 = tokens(proj2[1:T + 1, :])
            with pool.Fori(0, 2) as i:
                for b in range(2):
                    store_block(i, 1, 25 + b, B_IN2 + b, p2[:, :, ds(i * (2 * NB) + b * NB, NB)])

            def load_input(u):
                if u:
                    pool.wait_ge(hy_z, u)
                off = u % 3 * DA + u // 3 * NB
                pool.dma_start(HW, A["hyena_rows"][:, off:off + NB].partition_broadcast(P)).then_inc(hy_in, 16)
                for s in range(3):
                    pool.dma_start(HL[:, s], tokens(proj2[s:T + s, off:off + NB])).then_inc(hy_in, 16)

            def load_spectrum(u):
                if u:
                    pool.wait_ge(hy_m, u)
                for part in range(2):
                    pool.dma_start(HK[part], filt[u % 2, u // 2].rearrange("p (m n) -> p m n", n=NB)
                                   [:, 2 * part:2 * part + 2, :]).then_inc(hy_kin, 16)

            pool.wait_ge(stg_out[1], 16 * (12 + 2))
            pool.wait_ge(stg_out[0], 16 * (13 + 2))
            load_input(0)
            load_input(1)
            store_block(0, 0, 29, B_HY, p2[:, :, 4 * NB:5 * NB])
            pool.wait_ge(stg_out[1], 16 * (12 + 3))
            load_input(2)
            store_block(0, 0, 30, B_HY + 1, p2[:, :, 5 * NB:6 * NB])
            load_spectrum(0)
            pool.wait_ge(stg_out[0], 16 * (13 + 3))
            for n in range(4):
                pool.dma_start(TAB[:, n], A["dft"][n].rearrange("(t p) f -> p t f", p=P)).then_inc(hy_tab, 16)
            pool.dma_start(HG, rows(A["hyena_norm_g_2"][0], P)).then_inc(hy_tab, 16)
            load_input(3)
            load_spectrum(1)
            load_spectrum(2)
            load_input(4)
            load_input(5)
            load_spectrum(3)
            pool.wait_ge(hy_y, 4)
            pool.dma_start(ROPE, A["rope"].rearrange("a (t p) f -> p a t f", p=P)).then_inc(at_in, 16)
            pool.dma_start(LAM, A["lambdas"].partition_broadcast(P)).then_inc(at_in, 16)
            pool.dma_start(SUBG, rows(A["subln_g_2"][0], P)).then_inc(at_in, 16)
            pool.wait_ge(at_g, 2)
            norm_rows(1, "ln2_g_2", "ln2_b_2")
            pool.wait_ge(x_done, 4)
            pool.memset(SUM, 0.0).then_inc(ff_zero, 1)
            norm_rows(2, "ln3_g_2", "ln3_b_2")
            for t in range(TT):
                pool.wait_ge(x_done, 5 + t)
                pool.dma_start(out[0, t * P:(t + 1) * P, :], XRES[:, t, :]).then_inc(x_out, 16)
            pool.wait_ge(x_out, 32)
            for st, n in ((f_st, 64), (zero_rows, 64), (mod_stored, 16)):
                pool.wait_ge(st, n)

        @block.scalar
        def _(act):
            act.wait_ge(rows_t, 1)
            act.activation(CACT[:, 16:32], tp(0)[:, 0:16], ACT.Sigmoid).then_inc(c_sig, 1)
            for n in range(3):
                act.wait_ge(f_arg, n + 1)
                act.activation((H1, H2, H1)[n][0:64, :], KST[0:64, 0, 0:T], ACT.Sin).then_inc(f_sin, 1)
            for u in range(4):
                act.wait_ge(f_k, u + 1)
                if u:
                    act.wait_ge(f_st, 16 * u)
                act.activation(KST, ps[:, 4:8, :], ACT.Copy).then_inc(f_ke, 1)
            act.wait_ge(mod_row, 1)
            act.activation(GROW[0:1, :].rearrange("p (a n) -> p a n", a=4), ps[0:1, 4:8, :], ACT.Copy)\
               .then_inc(mod_row_sb, 1)
            for h in range(3):
                split_hi(act, 0, 0, h)
            for g in range(8):
                act.wait_ge(tp_ready, G_H + g + 1)
                for j in range(2):
                    k = 2 * g + j
                    ins = act.activation(ahi[:, k, :], tp(g % 4)[:, j * T:(j + 1) * T], ACT.Identity,
                                         scale=COEF[:, k:k + 1], bias=COEF[:, 16 + k:17 + k])
                ins.then_inc(tp_hi, 1)

            def stage(i, per, h_end, s, blk, cols=NB):
                act.wait_ge(half_done, i * per + h_end)
                if s >= 2:
                    act.wait_ge(stg_out[s % 2], i * per + 16 * (s // 2))
                act.activation(STG[:, s % 2, :, 0:cols], acc(blk)[:, :, 0:cols], ACT.Copy)\
                   .then_inc(acc_free[blk % 2], 1)

            def split_hi_block(i, per, h):
                for q in range(8):
                    split_hi(act, i, per, h + q + 3)

            split_hi(act, 0, 0, 3)
            split_hi(act, 0, 0, 4)
            stage(0, 0, 2, 0, B_LORA, P)
            for b in range(2):
                split_hi_block(0, 0, H_FIRST + 8 * b)
                stage(0, 0, H_FIRST + 8 * b + 8, 1 + b, B_FIRST + b)
            with act.Fori(0, 2) as i:
                for b in range(2):
                    split_hi_block(i, 16, H_IN + 8 * b)
                    stage(i, 16, H_IN + 8 * b + 8, 3 + b, B_IN + b)
            for b in range(2):
                for q in range(8):
                    split_hi(act, 0, 0, H_IN + 32 + 8 * b + q + 3)
                    if b and q == 0:
                        act.wait_ge(w_prep, 1)
                        act.activation(LIN[:, 0, :, 0:LORA], LIN[:, 0, :, 0:LORA], ACT.Tanh).then_inc(w_prep, 1)
                    if b and q == 2:
                        act.wait_ge(w_lorat, 1)
                        act.activation(LORAW[0:LORA, :], tp(0)[0:LORA, 0:T], ACT.Copy).then_inc(w_loras, 1)
                        act.activation(LORAA[0:LORA, :], tp(1)[0:LORA, 0:T], ACT.Copy).then_inc(w_loras, 1)
                stage(0, 0, H_IN + 32 + 8 * b + 8, 7 + b, B_IN + 4 + b)
            with act.Fori(0, HP // 2) as i:
                for p in range(2):
                    h0, s0, blk = H_IN + 48 + 16 * p, 9 + 2 * p, B_IN + 6 + 2 * p

                    def split(q):
                        split_hi(act, i, 32, h0 + q + 3)

                    act.wait_ge(w_z, i * 2 + (p + 1))
                    act.activation(SG.rearrange("p a t n -> p (a t n)"), tp(2), ACT.Tanh, scale=0.5)\
                       .then_inc(w_tanh, 1)
                    for q in range(5):
                        split(q)
                    act.wait_ge(w_cum, i * 2 + (p + 1))
                    act.activation(EXPS[:, 0:2].rearrange("p a t n -> p (a t n)"), tp(1), ACT.Exp)
                    act.activation(EXPS[:, 2].rearrange("p t n -> p (t n)"), tp(1)[:, 0:T], ACT.Exp, scale=-1.0)
                    act.activation(WST[:, 20:24], tp(2)[:, 0:4], ACT.Exp).then_inc(w_exp, 1)
                    split(5)
                    for t in range(TT):
                        act.wait_ge(w_t4p, i * 4 + (2 * p + t + 1))
                        act.activation(T4[:, t].rearrange("p a n -> p (a n)"), tp(2 + t), ACT.Copy).then_inc(w_t4, 1)
                    split(6)
                    split(7)
                    for lv in range(5):
                        if lv == 1:
                            stage(i, 32, h0 + 8, s0, blk)
                        act.wait_ge(w_u, i * 10 + (5 * p + lv + 1))
                        act.activation(UU.rearrange("p u n -> p (u n)"), tp(0), ACT.Copy).then_inc(w_ue, 1)
                        split(8 + lv)
                    act.wait_ge(w_w1, i * 2 + (p + 1))
                    act.activation(W1S.rearrange("p u n -> p (u n)"), tp(0)[:, 0:T], ACT.Copy)
                    act.activation(AEF.rearrange("p t n -> p (t n)"), tp(1)[:, 0:T], ACT.Copy).then_inc(w_w1e, 1)
                    for q in range(13, 16):
                        split(q)
                    act.wait_ge(w_y, i * 2 + (p + 1))
                    act.activation(YS.rearrange("p (t h) n -> p t h n", t=TT),
                                   ps[:, 4:6, 0:P].rearrange("p h (t n) -> p t h n", t=TT), ACT.Copy)\
                       .then_inc(w_ye, 1)
                    stage(i, 32, h0 + 16, s0 + 1, blk + 1)

            for c in range(2):
                act.wait_ge(y_in, 16 + 160 * (c + 1))
                act.activation(SZ[:, 0], ZA, ACT.Sigmoid)
                act.activation(SZ[:, 1], ZB, ACT.Sigmoid).then_inc(y_sig, 1)
            for g in range(8):
                take_hi(act, G_Y + g, 2 * g)
            with act.Fori(0, 4) as i:
                for q in range(4):
                    split_hi(act, i, 8, H_PAB + q + 3)
                act.wait_ge(ga_in, i * 32 + 32)
                act.activation(GA, GA, ACT.Sigmoid).then_inc(ga_sig, 1)
                for q in range(4, 8):
                    split_hi(act, i, 8, H_PAB + q + 3)
            for g in range(8):
                take_hi(act, G_M + g, 2 * g)

            def sum_blocks(h, blk):
                with act.Fori(0, 2) as i:
                    for b in range(2):
                        split_hi_block(i, 16, h + 8 * b)
                        act.wait_ge(half_done, i * 16 + (h + 8 * b + 8))
                        act.activation(SUM[:, :, ds(i * (2 * NB) + b * NB, NB)], acc(blk + b), ACT.Copy)\
                           .then_inc(acc_free[(blk + b) % 2], 1)

            sum_blocks(H_OUT, B_OUT)
            act.drain()
            for t in range(TT):
                act.activation(SRC[:, t, :], SUM[:, t, :], ACT.Square, accum_out=MSQ[:, t:t + 1]).then_inc(o_sq, 1)
            for g in range(8):
                take_hi(act, G_X1 + g, 2 * g)

            def hidden_hi(i, g):
                for j in range(2):
                    act.wait_ge(tp_ready, i * 2 + (g + j + 1))
                    act.activation(ghi[:, 2 * j:2 * j + 2, :], tp(j).rearrange("p (k t) -> p k t", k=2), ACT.Copy)\
                       .then_inc(tp_hi, 1)

            def ffn(h0, blk, g0):
                def gate_up(i, per, h, b):
                    split_hi_block(i, per, h)
                    act.wait_ge(half_done, i * per + (h + 8))
                    act.activation(SIG, acc(b), ACT.Sigmoid).then_inc(ff_sig, 1)
                    split_hi_block(i, per, h + 8)

                gate_up(0, 0, h0, blk)
                hidden_hi(0, g0)
                with act.Fori(0, FB - 1) as i:
                    gate_up(i, 24, h0 + 16, blk + 2)
                    split_hi_block(i, 24, h0 + 32)
                    hidden_hi(i, g0 + 2)
                split_hi_block(0, 0, h0 + 24 * FB - 8)

            ffn(H_FFN1, B_FFN1, G_FFN1)
            for g in range(8):
                take_hi(act, G_X2 + g, 2 * g)
            with act.Fori(0, 2) as i:
                for b in range(2):
                    split_hi_block(i, 16, H_IN2 + 8 * b)
                    stage(i, 16, H_IN2 + 8 * b + 8, 25 + b, B_IN2 + b)
            for b in range(2):
                split_hi_block(0, 0, H_HY + 8 * b)
                stage(0, 0, H_HY + 8 * b + 8, 29 + b, B_HY + b)
            for b in range(2, 8):
                split_hi_block(0, 0, H_HY + 8 * b)
                act.wait_ge(half_done, H_HY + 8 * b + 8)
                if b >= 6:
                    act.wait_ge(hy_m, 4)
                act.activation((AV, AQ, AK)[b // 2 - 1][:, :, b % 2 * NB:(b % 2 + 1) * NB], acc(B_HY + b), ACT.Copy)\
                   .then_inc(acc_free[(B_HY + b) % 2], 1)
            for g in range(4):
                take_hi(act, G_Y2 + g, 2 * g)

            def splits(m, end):
                for h in range(m, end):
                    split_hi(act, 0, 0, H_OUT2 + h + 3)

            def upper_sum(n):
                act.wait_ge(half_done, H_OUT2 + 4 * n + 4)
                act.activation(SUM[:, :, n * NB:(n + 1) * NB], acc(B_OUT2 + n), ACT.Copy)\
                   .then_inc(acc_free[(B_OUT2 + n) % 2], 1)

            splits(0, 3)
            act.wait_ge(at_lam, 1)
            act.activation(AST[:, 2:4], AST[:, 0:2], ACT.Exp).then_inc(at_le, 1)
            for h in range(8):
                act.wait_ge(at_tp, h + 1)
                act.activation(QT[:, h, :], tp(h % 4)[:, 0:T], ACT.Copy)
                act.activation(KTT[:, h, :], tp(h % 4)[:, T:2 * T], ACT.Copy).then_inc(at_tps, 1)

            def exps(h):
                act.wait_ge(at_max, h + 1)
                if h:
                    act.wait_ge(at_w, h)
                for m in range(2):
                    for t in range(TT):
                        n = 4 * h + 2 * m + t
                        ins = act.activation(EE[:, m, t, :], tp(m)[:, t * T:(t + 1) * T], ACT.Exp,
                                             scale=0.125, bias=AST[:, 8 + n:9 + n],
                                             accum_out=AST[:, 40 + n:41 + n])
                ins.then_inc(at_e, 1)

            splits(3, 4)
            exps(0)
            splits(4, 5)
            upper_sum(0)
            for h in range(8):
                act.wait_ge(at_wt, h + 1)
                act.activation(WT2, tp(2).rearrange("p (k q) -> p k q", k=2), ACT.Copy).then_inc(at_wts, 1)
                if h < 7:
                    exps(h + 1)
                splits(5 + h, 6 + h)
                act.wait_ge(at_o, h + 1)
                act.activation(AO[:, :, h * P:(h + 1) * P], tp(3)[:, 0:T].rearrange("p (t n) -> p t n", t=TT),
                               ACT.Copy).then_inc(at_oe, 1)
                if h % 4 == 3:
                    upper_sum(1 + h // 4)
            splits(13, 16)
            upper_sum(3)
            for g in range(4, 8):
                take_hi(act, G_Y2 + g, 2 * g)
            with act.Fori(0, 2) as i:
                for q in range(8):
                    split_hi(act, i, 8, H_OUT2 + 16 + q + 3)
            for g in range(8):
                take_hi(act, G_X3 + g, 2 * g)
            ffn(H_FFN2, B_FFN2, G_FFN2)

        @block.tensor
        def _(pe):
            pe.wait_ge(s_const, 16)
            pe.wait_ge(s_rows, 48)
            pe.transpose(tp(0)[:, 0:64], ROWS[0:64, :], ident[0:64, 0:64]).then_inc(rows_t, 1)
            pe.wait_ge(f_in, 9 * 16)
            pe.matmul(tp(1)[0:64, 0:T], FW[0:33, 0, :], ZT[0:33, :], start=True, stop=True).then_inc(f_mlp, 1)
            for n, src in ((1, H1), (2, H2)):
                pe.wait_ge(f_sin, n)
                pe.matmul(tp(1)[0:64, 0:T], FW[0:64, n, :], src[0:64, :], start=True, stop=True).then_inc(f_mlp, 1)
            pe.wait_ge(f_sin, 3)
            pe.wait_ge(c_act, 1)
            for u in range(4):
                cb, n = u // 2, u % 2
                if u:
                    pe.wait_ge(f_sd0, u)
                for d in range(2):
                    for t in range(TT):
                        col = n * 2 * DA + d * DA + cb * NB
                        mm = pe.matmul(ps[:, 2 * d + t, :], H1[0:64, t * P:(t + 1) * P], WOF[0:64, col:col + NB],
                                       start=True, stop=True)
                mm.then_inc(f_h, 1)
                pe.wait_ge(f_sd, 2 * u + 2)
                if u:
                    pe.wait_ge(f_ke, u)
                for part, tab in enumerate((FC, FS)):
                    for m in range(2):
                        for t in range(TT):
                            mm = pe.matmul(tp(2 * part + m), tab[:, t, m * P:(m + 1) * P], SD[:, part, t, :],
                                           start=t == 0, stop=t == 1)
                mm.then_inc(f_k, 1)
            pe.wait_ge(ada_done, 48)
            pe.wait_ge(s_ones, 1)
            for j in range(32):
                mm = pe.matmul(ps[:, 0, j:j + 1], ADA[:, j * P:(j + 1) * P], ones[:, 0:1], start=True, stop=True)
            mm.then_inc(mod_cols, 1)
            pe.wait_ge(f_ke, 4)
            for n in range(4):
                mm = pe.matmul(ps[0:1, 4 + n, :], ones[:, 0:1], ADA[:, 2 * D + n * NB:2 * D + (n + 1) * NB],
                               start=True, stop=True)
            mm.then_inc(mod_row, 1)
            pe.wait_ge(mod_row_sb, 1)
            pe.wait_ge(x_norm, 2)
            for g in range(8):
                transpose_group(pe, G_H + g, SRC, 2 * g)
            pe.wait_ge(tp_lo, G_H + 8)
            pe.wait_ge(mod_scale, 1)
            products(pe, 0, 0, 0, ahi[:, 0:8, :], alo[:, 0:8, :], acc(B_LORA), True, False, P)
            products(pe, 0, 0, 1, ahi[:, 8:16, :], alo[:, 8:16, :], acc(B_LORA), False, True, P)
            for b in range(2):
                block_2048(pe, 0, 0, H_FIRST + 8 * b, 0, B_FIRST + b)
            with pe.Fori(0, 2) as i:
                for b in range(2):
                    block_2048(pe, i, 16, H_IN + 8 * b, 2, B_IN + b)
            for b in range(2):
                pe.wait_ge(acc_free[(B_IN + b) % 2], (B_IN + 4 + b) // 2)
                for q in range(8):
                    products(pe, 0, 0, H_IN + 32 + 8 * b + q, ahi[:, 2 * q:2 * q + 2, :], alo[:, 2 * q:2 * q + 2, :],
                             acc(B_IN + b), q == 0, q == 7)
                    if b and q == 1:
                        pe.wait_ge(w_prep, 2)
                        for t in range(TT):
                            pe.transpose(tp(0)[0:LORA, t * P:(t + 1) * P], LIN[:, 0, t, 0:LORA], ident[:, :])
                            mm = pe.transpose(tp(1)[0:LORA, t * P:(t + 1) * P], LIN[:, 0, t, LORA:P], ident[:, :])
                        mm.then_inc(w_lorat, 1)
            pe.wait_ge(w_loras, 3)
            pe.wait_ge(w_kin, 16)
            with pe.Fori(0, HP // 2) as i:
                for p in range(2):
                    h0, blk, V = H_IN + 48 + 16 * p, B_IN + 6 + 2 * p, CUR[p][:, :, 2, :]

                    def part(n):
                        q, b = n // 2 % 8, n // 16
                        if n % 16 == 0:
                            pe.wait_ge(acc_free[(blk + b) % 2], i * 2 + (blk + b) // 2)
                        products(pe, i, 32, h0 + n // 2, ahi[:, 2 * q:2 * q + 2, :], alo[:, 2 * q:2 * q + 2, :],
                                 acc(blk + b), q == 0, q == 7, part=n % 2)

                    def parts(n, end):
                        for m in range(n, end):
                            part(m)

                    pe.wait_ge(w_in_s[p], i * 96 + 96)
                    for a, lora in enumerate((LORAW, LORAA)):
                        for t in range(TT):
                            mm = pe.matmul(tp(2)[:, (2 * a + t) * P:(2 * a + t + 1) * P],
                                           lora[0:LORA + 1, t * P:(t + 1) * P], WA[p][0:LORA + 1, a, :],
                                           start=True, stop=True)
                    mm.then_inc(w_z, 1)
                    parts(0, 8)
                    pe.wait_ge(w_ld, i * 2 + (p + 1))
                    for t in range(TT):
                        pe.matmul(tp(1)[:, t * P:(t + 1) * P], MASKS[:, 1, :], LD[:, t, :], start=True, stop=True)
                        pe.matmul(tp(1)[:, T + t * P:T + (t + 1) * P], MASKS[:, 0, :], LD[:, t, :],
                                  start=True, stop=True)
                        mm = pe.matmul(tp(2)[:, 2 * t:2 * t + 2], LD[:, t, :], MASKS[:, 12, 0:2], start=True, stop=True)
                    mm.then_inc(w_cum, 1)
                    parts(8, 12)
                    pe.wait_ge(w_tok, i * 2 + (p + 1))
                    for t in range(TT):
                        for n in range(4):
                            mm = pe.transpose(tp(2 + t)[:, n * P:(n + 1) * P], TOK[:, t, n, :], ident[:, :])
                        mm.then_inc(w_t4p, 1)
                    part(12)
                    for t in range(TT):
                        pe.wait_ge(w_t4, i * 4 + (2 * p + 2))
                        if t:
                            pe.wait_ge(w_mask, i * 4 + (2 * p + t))
                        for h in range(2):
                            hs = slice(64 * h, 64 * h + 64)
                            ar = T4[hs, t, 0:2, :].rearrange("p a n -> p (a n)")
                            pe.matmul(tp(h)[:, 0:T], T4[hs, t, 2, :], ar, start=True, stop=True)
                            pe.matmul(tp(h)[:, T:2 * T], T4[hs, t, 3, :], ar, start=True, stop=True)
                            mm = pe.matmul(tp(2 + h)[:, t * P:(t + 1) * P],
                                           T4[hs, t, 0, :], T4[hs, t, 2, :], start=True, stop=True)
                        mm.then_inc(w_gram, 1)
                        part(13 + t)
                    pe.wait_ge(w_t0, i * 2 + (p + 1))
                    for lv in range(5):
                        if lv:
                            pe.wait_ge(w_tn, i * 10 + (5 * p + lv))
                        pe.wait_ge(w_ms, i * 10 + (5 * p + lv + 1))
                        for u in range(4):
                            mm = pe.matmul(tp(0)[:, u * P:(u + 1) * P], MS[:, u, :], TM[:, u, :], start=True, stop=True)
                        mm.then_inc(w_u, 1)
                        part(15 + 2 * lv)
                        pe.wait_ge(w_ue, i * 10 + (5 * p + lv + 1))
                        for u in range(4):
                            if lv < 4:
                                pe.matmul(tp(1)[:, u * P:(u + 1) * P], TMT[:, u, :], UU[:, u, :], start=True, stop=True)
                            mm = pe.matmul(tp(2)[:, u * P:(u + 1) * P], UU[:, u, :], TMT[:, u, :],
                                           start=True, stop=True)
                        mm.then_inc(w_dt, 1)
                        part(16 + 2 * lv)
                    pe.wait_ge(w_tn, i * 10 + (5 * p + 5))
                    for t in range(TT):
                        for h in range(2):
                            u = 2 * t + h
                            hs = slice(64 * h, 64 * h + 64)
                            pe.matmul(tp(0)[:, u * 64:(u + 1) * 64], GR[:, u, 2, :], V[:, t, hs], start=True, stop=True)
                            mm = pe.matmul(tp(1)[hs, t * P:(t + 1) * P], TOK[:, t, 0, hs], TMT[:, u, :],
                                           start=True, stop=True)
                    mm.then_inc(w_w1, 1)
                    part(25)
                    pe.wait_ge(w_w1e, i * 2 + (p + 1))
                    for u in range(4):
                        mm = pe.matmul(tp(2)[:, u * 64:(u + 1) * 64], TMT[:, u, :], W1S[:, u, :], start=True, stop=True)
                    mm.then_inc(w_sa0, 1)
                    part(26)
                    for c in range(NCH):
                        t, rs = c // 2, slice(CH * (c % 2), CH * (c % 2) + CH)
                        cs = slice(CH * (c % 2), CH * (c % 2) + CH)
                        if c:
                            wait_alone(pe, w_state, i * 6 + (3 * p + c))
                            for h in range(2):
                                hs = slice(64 * h, 64 * h + 64)
                                mm = pe.matmul(tp(h)[rs, 0:64], AEF[hs, t, cs], ST[hs, c, :], start=True, stop=True)
                            mm.then_inc(w_sap, 1)
                            if c < 3:
                                part(26 + 2 * c)
                        if c == NCH - 1:
                            break
                        wait_alone(pe, w_sae, i * 8 + (4 * p + c + 1))
                        for h in range(2):
                            hs = slice(64 * h, 64 * h + 64)
                            pe.matmul(tp(3)[hs, c * 64:(c + 1) * 64], TOK[rs, t, 2, hs], SA[rs, 2 * t + h, :],
                                      start=True, stop=False)
                            mm = pe.matmul(tp(3)[hs, c * 64:(c + 1) * 64], TOK[rs, t, 3, hs], V[rs, t, hs],
                                           start=False, stop=True)
                        mm.then_inc(w_delta, 1)
                        part(27 + 2 * c)
                    wait_alone(pe, w_sae, i * 8 + (4 * p + NCH))
                    for t in range(TT):
                        for h in range(2):
                            u = 2 * t + h
                            hs = slice(64 * h, 64 * h + 64)
                            dst = tp(h)[:, t * 64:(t + 1) * 64]
                            pe.matmul(dst, GR[:, u, 1, :], SA[:, u, :], start=True, stop=False)
                            pe.matmul(dst, GR[:, u, 3, :], V[:, t, hs], start=False, stop=False)
                            for c in (2 * t, 2 * t + 1):
                                rs = slice(CH * (c % 2), CH * (c % 2) + CH)
                                mm = pe.matmul(tp(h)[rs, t * 64:(t + 1) * 64], T4[hs, t, 1, rs], ST[hs, c, :],
                                               start=False, stop=True)
                    mm.then_inc(w_y, 1)
            pe.wait_ge(y_src, 2)
            for g in range(8):
                transpose_group(pe, G_Y + g, SRC, 2 * g)
            pe.wait_ge(tp_lo, G_Y + 8)
            with pe.Fori(0, 4) as i:
                for n in range(2):
                    blk = B_PAB + n
                    pe.wait_ge(acc_free[blk % 2], i + blk // 2)
                    for q in range(4):
                        k = 8 * n + 2 * q
                        products(pe, i, 8, H_PAB + 4 * n + q, ahi[:, k:k + 2, :], alo[:, k:k + 2, :], acc(blk),
                                 q == 0, q == 3)
            pe.wait_ge(m_done, 5)
            for g in range(8):
                transpose_group(pe, G_M + g, SRC, 2 * g)
            pe.wait_ge(tp_lo, G_M + 8)
            with pe.Fori(0, 2) as i:
                for b in range(2):
                    block_2048(pe, i, 16, H_OUT + 8 * b, 2, B_OUT + b)
            pe.wait_ge(x1_done, 2)
            for g in range(8):
                transpose_group(pe, G_X1 + g, XRES, 2 * g)
            pe.wait_ge(tp_lo, G_X1 + 8)

            def ffn(h0, blk, g0):
                def hidden(i, g, up):
                    pe.wait_ge(acc_free[up % 2], i * 3 + (up // 2 + 1))
                    pe.wait_ge(tp_lo, i * 2 + g)
                    for j in range(2):
                        for k in range(2):
                            for t in range(TT):
                                col = (2 * j + k) * P
                                mm = pe.transpose(tp(j)[:, k * T + t * P:k * T + (t + 1) * P],
                                                  HID[:, t, col:col + P], ident[:, :])
                        mm.then_inc(tp_ready, 1)

                def down(i, per, h, blk_per, b, g):
                    pe.wait_ge(tp_lo, i * 2 + g)
                    for n in range(4):
                        pe.wait_ge(acc_free[(b + n) % 2], i * (blk_per // 2) + (b + n) // 2)
                        for q in range(2):
                            products(pe, i, per, h + 2 * n + q, ghi[:, 2 * q:2 * q + 2, :], glo[:, 2 * q:2 * q + 2, :],
                                     acc(b + n), q == 0, q == 1)

                block_2048(pe, 0, 0, h0, 0, blk)
                block_2048(pe, 0, 0, h0 + 8, 0, blk + 1)
                hidden(0, g0, blk + 1)
                with pe.Fori(0, FB - 1) as i:
                    block_2048(pe, i, 24, h0 + 16, 6, blk + 2)
                    block_2048(pe, i, 24, h0 + 24, 6, blk + 3)
                    down(i, 24, h0 + 32, 6, blk + 4, g0 + 2)
                    hidden(i, g0 + 2, blk + 3)
                down(0, 0, h0 + 24 * FB - 8, 0, blk + 6 * FB - 4, g0 + 2 * FB)

            ffn(H_FFN1, B_FFN1, G_FFN1)
            pe.wait_ge(x_done, 2)
            for g in range(8):
                transpose_group(pe, G_X2 + g, XRES, 2 * g)
            pe.wait_ge(tp_lo, G_X2 + 8)
            with pe.Fori(0, 2) as i:
                for b in range(2):
                    block_2048(pe, i, 16, H_IN2 + 8 * b, 2, B_IN2 + b)

            def halves(n, end):
                for m in range(n, end):
                    blk, q = B_HY + m // 8, m % 8
                    if q == 0:
                        pe.wait_ge(acc_free[blk % 2], blk // 2)
                    products(pe, 0, 0, H_HY + m, ahi[:, 2 * q:2 * q + 2, :], alo[:, 2 * q:2 * q + 2, :],
                             acc(blk), q == 0, q == 7)

            halves(0, HY_UNITS[0])
            pe.wait_ge(hy_tab, 80)
            for u in range(4):
                if u % 2 == 0:
                    pe.wait_ge(hy_z, 3 * (u // 2) + 3)
                else:
                    pe.wait_ge(hy_y, u)
                for part in range(2):
                    for m in range(2):
                        for t in range(TT):
                            mm = pe.matmul(tp(2 * part + m), TAB[:, part, t, m * P:(m + 1) * P], HZ[:, 0, t, :],
                                           start=t == 0, stop=t == 1)
                mm.then_inc(hy_f, 1)
                m0 = HY_UNITS[u]
                halves(m0, m0 + 3)
                pe.wait_ge(hy_m, u + 1)
                for t in range(TT):
                    for part in range(2):
                        for m in range(2):
                            mm = pe.matmul(tp(t), TAB[:, 2 + part, m, t * P:(t + 1) * P],
                                           HY_[:, 2 * part + m, :], start=part == 0 and m == 0,
                                           stop=part == 1 and m == 1)
                mm.then_inc(hy_i, 1)
                halves(m0 + 3, HY_UNITS[u + 1] if u < 3 else 64)

            pe.wait_ge(hy_g, 2)
            for g in range(4):
                transpose_group(pe, G_Y2 + g, SRC, 2 * g)
            pe.wait_ge(tp_lo, G_Y2 + 4)

            def upper(n, end):
                for m in range(n, end):
                    blk, q = B_OUT2 + m // 4, m % 4
                    if q == 0:
                        pe.wait_ge(acc_free[blk % 2], blk // 2)
                    products(pe, 0, 0, H_OUT2 + m, ahi[:, 2 * q:2 * q + 2, :], alo[:, 2 * q:2 * q + 2, :],
                             acc(blk), q == 0, q == 3)

            upper(0, 3)
            pe.wait_ge(at_rope, 2)
            for h in range(8):
                if h >= 4:
                    pe.wait_ge(at_tps, h - 3)
                for n, src in enumerate((AQ, AK)):
                    for t in range(TT):
                        mm = pe.transpose(tp(h % 4)[:, n * T + t * P:n * T + (t + 1) * P],
                                          src[:, t, h * P:(h + 1) * P], ident[:, :])
                mm.then_inc(at_tp, 1)
            pe.wait_ge(at_tps, 8)

            def scores(h):
                if h:
                    pe.wait_ge(at_e, h)
                for m in range(2):
                    rs = slice(64 * m, 64 * m + 64)
                    for t in range(TT):
                        mm = pe.matmul(tp(m)[:, t * T:(t + 1) * T], QT[rs, h, t * P:(t + 1) * P],
                                       KTT[rs, h, :], start=True, stop=True)
                mm.then_inc(at_s, 1)

            scores(0)
            upper(3, 4)
            for h in range(8):
                pe.wait_ge(at_w, h + 1)
                for k in range(2):
                    for t in range(TT):
                        mm = pe.transpose(tp(2)[:, k * T + t * P:k * T + (t + 1) * P],
                                          WW[:, t, k * P:(k + 1) * P], ident[:, :])
                mm.then_inc(at_wt, 1)
                if h < 7:
                    scores(h + 1)
                upper(4 + h, 5 + h)
                pe.wait_ge(at_wts, h + 1)
                if h:
                    pe.wait_ge(at_oe, h)
                for t in range(TT):
                    for k in range(2):
                        mm = pe.matmul(tp(3)[:, t * P:(t + 1) * P], WT2[:, k, t * P:(t + 1) * P],
                                       AV[:, k, h * P:(h + 1) * P], start=k == 0, stop=k == 1)
                mm.then_inc(at_o, 1)
            upper(12, 16)
            pe.wait_ge(at_g, 2)
            for g in range(4, 8):
                transpose_group(pe, G_Y2 + g, SRC, 2 * g)
            pe.wait_ge(tp_lo, G_Y2 + 8)
            with pe.Fori(0, 2) as i:
                for b in range(2):
                    blk = B_OUT2 + 4 + b
                    pe.wait_ge(acc_free[blk % 2], i + blk // 2)
                    for q in range(4):
                        products(pe, i, 8, H_OUT2 + 16 + 4 * b + q, ahi[:, 8 + 2 * q:10 + 2 * q, :],
                                 alo[:, 8 + 2 * q:10 + 2 * q, :], acc(blk), q == 0, q == 3)
            pe.wait_ge(x_done, 4)
            for g in range(8):
                transpose_group(pe, G_X3 + g, XRES, 2 * g)
            pe.wait_ge(tp_lo, G_X3 + 8)
            ffn(H_FFN2, B_FFN2, G_FFN2)

        @block.vector
        def _(dve):
            def bcl(ap, n):
                return ap.unsqueeze(2).to_broadcast([ap.shape[0], ap.shape[1], n])

            def rsqrt(dst, src, tmp):
                dve.tensor_scalar(tmp.bitcast(mybir.dt.int32), src.bitcast(mybir.dt.int32), 1, None,
                                  ALU.logical_shift_right)
                dve.drain()
                dve.tensor_scalar(dst.bitcast(mybir.dt.int32), tmp.bitcast(mybir.dt.int32), -1.0, 1597463007.0,
                                  ALU.mult, ALU.add)
                dve.drain()
                for _ in range(3):
                    dve.tensor_tensor(tmp, dst, dst, ALU.mult)
                    dve.drain()
                    dve.tensor_tensor(tmp, tmp, src, ALU.mult)
                    dve.drain()
                    dve.tensor_scalar(tmp, tmp, -0.5, 1.5, ALU.mult, ALU.add)
                    dve.drain()
                    dve.tensor_tensor(dst, dst, tmp, ALU.mult)
                    dve.drain()

            dve.wait_ge(rows_t, 1)
            dve.wait_ge(c_sig, 1)
            dve.tensor_copy(COLS[:, 0:64], tp(0)[:, 0:64])
            dve.drain()
            dve.tensor_tensor(CACT[:, 0:16], COLS[:, 0:16], CACT[:, 16:32], ALU.mult).then_inc(c_act, 1)
            dve.drain()

            def ada(n):
                k, part = n % 16, ADA[:, n // 16 * D:(n // 16 + 1) * D]
                dve.wait_ge(ada_in[n % 4], 16 * (n // 4 + 1))
                if k == 0:
                    dve.tensor_scalar(part, raw[:, n % 4, :], CACT[:, 0:1], None, ALU.mult).then_inc(ada_done, 1)
                else:
                    dve.scalar_tensor_tensor(part, raw[:, n % 4, :], CACT[:, k:k + 1], part, ALU.mult, ALU.add)\
                       .then_inc(ada_done, 1)
                dve.drain()

            def sine_argument(n):
                arg, turns = KST[0:64, 0, 0:T], KST[0:64, 1, 0:T]
                dve.wait_ge(f_mlp, n + 1)
                if n == 0:
                    dve.wait_ge(f_in, 9 * 16)
                dve.tensor_scalar(arg, tp(1)[0:64, 0:T], FCOL[0:64, n:n + 1], FCOL[0:64, 3:4], ALU.add, ALU.mult)
                dve.drain()
                dve.tensor_scalar(turns, arg, 1.0 / (2.0 * math.pi), ROUND, ALU.mult, ALU.add)
                dve.drain()
                dve.tensor_scalar(turns, turns, ROUND, None, ALU.subtract)
                dve.drain()
                for part in (TWO_PI_HI, TWO_PI_LO):
                    dve.scalar_tensor_tensor(arg, turns, -part, arg, ALU.mult, ALU.add)
                    dve.drain()
                dve.tensor_scalar(arg, arg, PI_IN, -PI_IN, ALU.min, ALU.max).then_inc(f_arg, 1)

            def filter_unit(u):
                cb, n = u // 2, u % 2
                dve.wait_ge(f_h, u + 1)
                dve.wait_ge(f_dec, 32 * (cb + 1))
                dve.tensor_tensor(HFB, ps[:, 0:4, :].rearrange("p (d t) n -> p d t n", d=2), DEC, ALU.mult)\
                   .then_inc(f_sd0, 1)
                dve.drain()
                row = HFB[0:1, 0, 0, :]
                dve.tensor_tensor(row, row, BROW[0:1, n, cb * NB:(cb + 1) * NB], ALU.add)
                dve.drain()
                if u:
                    dve.wait_ge(f_k, u)
                dve.tensor_tensor(SD[:, 0], HFB[:, 0], HFB[:, 1], ALU.add).then_inc(f_sd, 1)
                dve.tensor_tensor(SD[:, 1], HFB[:, 0], HFB[:, 1], ALU.subtract).then_inc(f_sd, 1)

            for n in range(48):
                ada(n)
                if n in (2, 5, 8):
                    sine_argument((n - 2) // 3)
                if n in (12, 20, 28, 36):
                    filter_unit((n - 12) // 8)
            dve.wait_ge(x_in, 32)

            def stats(src, t):
                for s in range(4):
                    dve.bn_stats(STATS[:, t, s, :], src[:, t, s * NB:(s + 1) * NB])
                dve.drain()
                return dve.bn_aggr(MV[:, t, :], STATS[:, t])

            for t in range(TT):
                stats(SUM, t)
            dve.drain()
            dve.tensor_tensor(MSQ, MV[:, :, 0], MV[:, :, 0], ALU.mult)
            dve.drain()
            dve.tensor_tensor(MSQ, MSQ, MV[:, :, 1], ALU.add)
            dve.drain()
            dve.tensor_scalar(MSQ, MSQ, RMS_EPS, None, ALU.add)
            dve.drain()
            rsqrt(RSTD, MSQ, RTMP)
            dve.wait_ge(mod_cols, 1)
            dve.tensor_tensor(MODC, ps[:, 0, 0:32], COLS[:, 32:64], ALU.add)
            dve.drain()
            dve.scalar_tensor_tensor(COEF[:, 0:16], MODC[:, 16:32], 1.0, COLS[:, 16:32], ALU.add, ALU.mult)
            dve.tensor_copy(COEF[:, 16:32], MODC[:, 0:16]).then_inc(mod_scale, 1)
            dve.wait_ge(mod_row, 1)
            for t in range(TT):
                dve.tensor_scalar(SRC[:, t, :], SUM[:, t, :], RSTD[:, t:t + 1], None, ALU.mult).then_inc(x_norm, 1)
            for h in range(2):
                split_lo(dve, 0, 0, h)
            for g in range(8):
                dve.wait_ge(tp_hi, G_H + g + 1)
                for j in range(2):
                    k = 2 * g + j
                    dve.tensor_scalar(HTMP[:, j, :], tp(g % 4)[:, j * T:(j + 1) * T], COEF[:, k:k + 1],
                                      COEF[:, 16 + k:17 + k], ALU.mult, ALU.add)
                dve.drain()
                dve.tensor_tensor(alo[:, 2 * g:2 * g + 2, :], HTMP, ahi[:, 2 * g:2 * g + 2, :].bitcast(F32),
                                  ALU.subtract).then_inc(tp_lo, 1)
                dve.drain()

            def split_lo_block(i, per, h):
                for q in range(8):
                    split_lo(dve, i, per, h + q + 2)

            split_lo(dve, 0, 0, 2)
            split_lo(dve, 0, 0, 3)
            for b in range(2):
                split_lo_block(0, 0, H_FIRST + 8 * b)
            with dve.Fori(0, 2) as i:
                for b in range(2):
                    split_lo_block(i, 16, H_IN + 8 * b)
            split_lo_block(0, 0, H_IN + 32)
            split_lo(dve, 0, 0, H_IN + 42)
            dve.wait_ge(w_lora, 48)
            dve.tensor_tensor(LIN[:, 1], LIN[:, 1], LIN[:, 0], ALU.subtract)
            dve.memset(ST[:, 0, :], 0.0)
            dve.memset(LORAW[LORA:LORA + 1, :], 1.0)
            dve.memset(LORAA[LORA:LORA + 1, :], 1.0).then_inc(w_loras, 1)
            dve.drain()
            dve.tensor_tensor(LIN[:, 1], LIN[:, 1], bc(MUL, TT), ALU.mult)
            dve.drain()
            dve.tensor_tensor(LIN[:, 0], LIN[:, 0], LIN[:, 1], ALU.add).then_inc(w_prep, 1)
            for q in range(11, 20):
                split_lo(dve, 0, 0, H_IN + 32 + q)

            def heads(ap):
                return ap.rearrange("p t (h n) -> p t h n", h=2)

            def per_head(ap):
                return ap.rearrange("p (t h) -> p t h", t=TT).unsqueeze(3).to_broadcast([P, TT, 2, 64])

            def th(ap):
                return ap.rearrange("p (t h) -> p t h", t=TT)

            dve.wait_ge(w_kin, 16)
            def norm_keys(i, p):
                dve.wait_ge(w_mix, i * 2 + (p + 1))
                dve.tensor_tensor(KK, CUR[p % 2][:, :, 1, :], bc(PRM[p % 2][:, 3, :], TT), ALU.mult)
                dve.drain()
                dve.tensor_tensor(RK, KK, KK, ALU.mult)
                dve.drain()
                dve.tensor_reduce(th(WST[:, 0:4]), heads(RK), AX.X, ALU.add)
                dve.drain()
                dve.tensor_scalar(WST[:, 0:4], WST[:, 0:4], 1e-24, None, ALU.max)
                dve.drain()
                rsqrt(WST[:, 4:8], WST[:, 0:4], small[:, 64:68])

            def pair(i, p, more):
                h0 = H_IN + 48 + 16 * p
                R, K, V = (CUR[p][:, :, n, :] for n in range(3))
                prm = PRM[p]

                def split(q):
                    split_lo(dve, i, 32, h0 + q + 2)

                dve.wait_ge(w_tanh, i * 2 + (p + 1))
                sg = SG.rearrange("p a t n -> p (a t n)")
                dve.tensor_scalar(sg, sg, 0.5, 0.5, ALU.mult, ALU.add)
                dve.drain()
                dve.tensor_scalar(LD, SG[:, 0], -math.exp(-0.5), None, ALU.mult).then_inc(w_ld, 1)
                split(2)
                split(3)
                dve.scalar_tensor_tensor(K2, SG[:, 1], -1.0, bc(prm[:, 4, :], TT), ALU.add, ALU.mult)
                dve.drain()
                dve.scalar_tensor_tensor(K2, K2, 1.0, K, ALU.add, ALU.mult)
                dve.drain()
                dve.tensor_tensor(RK, R, K2, ALU.mult)
                dve.drain()
                dve.tensor_tensor(RK, RK, bc(prm[:, 5, :], TT), ALU.mult)
                dve.drain()
                dve.tensor_reduce(th(WST[:, 8:12]), heads(RK), AX.X, ALU.add)
                dve.drain()
                dve.tensor_tensor(heads(BV), heads(V), per_head(WST[:, 8:12]), ALU.mult)
                dve.tensor_tensor(heads(KK), heads(KK), per_head(WST[:, 4:8]), ALU.mult)
                dve.drain()
                dve.tensor_tensor(BB, KK, SG[:, 1], ALU.mult)
                dve.drain()
                split(4)
                dve.wait_ge(w_exp, i * 2 + (p + 1))
                dve.scalar_tensor_tensor(TOK[:, :, 0, :], KK, -1.0, EXPS[:, 1], ALU.mult, ALU.mult)
                dve.tensor_tensor(TOK[:, :, 1, :], R, EXPS[:, 0], ALU.mult)
                dve.tensor_tensor(TOK[:, :, 2, :], BB, EXPS[:, 2], ALU.mult)
                dve.tensor_tensor(TOK[:, :, 3, :], K2, EXPS[:, 2], ALU.mult).then_inc(w_tok, 1)
                split(5)
                split(6)
                for t in range(TT):
                    dve.wait_ge(w_gram, i * 4 + (2 * p + t + 1))
                    dve.tensor_tensor(GR[:, 2 * t:2 * t + 2].rearrange("p u g n -> p u (g n)"), ps[:, 4:6, :],
                                      bc(MASKS[:, 0:4, :].rearrange("p g n -> p (g n)"), 2), ALU.mult)
                    dve.tensor_tensor(MM[:, 2 * t:2 * t + 2, :], ps[:, 6:8, t * P:(t + 1) * P], bc(MASKS[:, 4, :], 2),
                                      ALU.mult).then_inc(w_mask, 1)
                    split(7 + t)
                dve.drain()
                dve.tensor_tensor(TM, MM, bc(MASKS[:, 10, :], 4), ALU.mult)
                dve.tensor_tensor(TMT, GR[:, :, 0, :], bc(MASKS[:, 11, :], 4), ALU.mult)
                dve.drain()
                dve.tensor_tensor(TM, TM, bc(ident[:, :], 4), ALU.add)
                dve.tensor_tensor(TMT, TMT, bc(ident[:, :], 4), ALU.add).then_inc(w_t0, 1)
                for lv in range(5):
                    dve.wait_ge(w_dt, i * 10 + (5 * p + lv + 1))
                    if lv < 4:
                        dve.tensor_tensor(TM, TM, tp(1).rearrange("p (u n) -> p u n", u=4), ALU.add)
                    dve.tensor_tensor(TMT, TMT, tp(2).rearrange("p (u n) -> p u n", u=4), ALU.add).then_inc(w_tn, 1)
                    split(9 + lv)
                dve.wait_ge(w_sa0, i * 2 + (p + 1))
                dve.tensor_copy(SA, tp(2)[:, 0:T].rearrange("p (u n) -> p u n", u=4)).then_inc(w_sae, 1)
                for c in range(NCH - 1):
                    decay = WST[:, 20 + c:21 + c]
                    if c:
                        dve.tensor_scalar(SPC, ST[:, c, :], decay, None, ALU.mult)
                        dve.drain()
                    dve.wait_ge(w_delta, i * 6 + (3 * p + c + 1))
                    delta = tp(3)[:, c * 64:(c + 1) * 64]
                    if c:
                        dve.scalar_tensor_tensor(ST[:, c + 1, :], delta, decay, SPC, ALU.mult, ALU.add)\
                           .then_inc(w_state, 1)
                    else:
                        dve.tensor_scalar(ST[:, 1, :], delta, decay, None, ALU.mult).then_inc(w_state, 1)
                    t, rs = (c + 1) // 2, slice(CH * ((c + 1) % 2), CH * ((c + 1) % 2) + CH)
                    dve.wait_ge(w_sap, i * 6 + (3 * p + c + 1))
                    dve.tensor_tensor(SA[rs, 2 * t:2 * t + 2, :], SA[rs, 2 * t:2 * t + 2, :], ps[rs, 4:6, 0:64],
                                      ALU.add).then_inc(w_sae, 1)
                    if c < 2:
                        split(14 + c)
                if more:
                    split(16)
                if more:
                    norm_keys(i, p + 1)
                dve.wait_ge(w_ye, i * 2 + (p + 1))
                dve.tensor_reduce(WST[:, 24:28], YS, AX.X, ALU.add)
                dve.drain()
                dve.tensor_scalar(WST[:, 24:28], WST[:, 24:28], -1.0 / 64, None, ALU.mult)
                dve.drain()
                dve.tensor_tensor(YS, YS, bcl(WST[:, 24:28], 64), ALU.add)
                dve.drain()
                dve.tensor_tensor(YQ, YS, YS, ALU.mult)
                dve.drain()
                dve.tensor_reduce(WST[:, 28:32], YQ, AX.X, ALU.add)
                dve.drain()
                dve.tensor_scalar(WST[:, 12:16], WST[:, 28:32], 1.0 / 64, GN_EPS, ALU.mult, ALU.add)
                dve.drain()
                if more:
                    split(17)
                rsqrt(WST[:, 16:20], WST[:, 12:16], small[:, 68:72])
                dve.tensor_tensor(YS, YS, bcl(WST[:, 16:20], 64), ALU.mult)
                dve.drain()
                ys = YS.rearrange("p (t h) n -> p t (h n)", t=TT)
                dve.tensor_tensor(ys, ys, bc(prm[:, 6, :], TT), ALU.mult)
                dve.drain()
                dve.tensor_tensor(ys, ys, bc(prm[:, 7, :], TT), ALU.add)
                dve.drain()
                dve.tensor_tensor(ys, ys, BV, ALU.add).then_inc(w_yo, 1)

            norm_keys(0, 0)
            with dve.Fori(0, HP // 2 - 1) as i:
                for p in range(2):
                    pair(i, p, True)
            for p in range(2):
                pair(HP // 2 - 1, p, p == 0)

            for c in range(2):
                dve.wait_ge(y_sig, c + 1)
                dve.tensor_tensor(YW, YW, ZA, ALU.mult)
                dve.tensor_tensor(ZB, ZB, BG, ALU.mult)
                dve.drain()
                dve.tensor_tensor(SRC[:, :, c * NB:(c + 1) * NB], YW, SZ[:, 0], ALU.mult)
                dve.tensor_tensor(ZB, ZB, SZ[:, 1], ALU.mult)
                dve.wait_ge(y_u, c + 1)
                for n in range(3):
                    dve.tensor_tensor(CG[:, n], CG[:, n], bc(CW[:, 2 - n, c * NB:(c + 1) * NB], TT), ALU.mult)
                dve.drain()
                dve.tensor_tensor(YT, CG[:, 0], CG[:, 1], ALU.add)
                dve.drain()
                dve.tensor_tensor(YT, YT, CG[:, 2], ALU.add)
                dve.drain()
                dve.tensor_tensor(SRC[:, :, DA + c * NB:DA + (c + 1) * NB], YT, ZB, ALU.mult).then_inc(y_src, 1)
            for g in range(8):
                take_lo(dve, G_Y + g, 2 * g)
            with dve.Fori(0, 4) as i:
                for q in range(4):
                    split_lo(dve, i, 8, H_PAB + q + 2)
                dve.wait_ge(half_done, i * 8 + (H_PAB + 4))
                dve.wait_ge(ga_sig, i + 1)
                dve.tensor_tensor(MT, acc(B_PAB), GA[:, 0], ALU.mult).then_inc(acc_free[B_PAB % 2], 1)
                for q in range(4, 8):
                    split_lo(dve, i, 8, H_PAB + q + 2)
                dve.wait_ge(half_done, i * 8 + (H_PAB + 8))
                dve.tensor_tensor(MU, acc(B_PAB + 1), GA[:, 1], ALU.mult).then_inc(acc_free[(B_PAB + 1) % 2], 1)
                dve.drain()
                dve.tensor_tensor(SRC[:, :, ds(i * NB, NB)], MT, MU, ALU.add).then_inc(m_done, 1)
                dve.drain()
            for g in range(8):
                take_lo(dve, G_M + g, 2 * g)
            with dve.Fori(0, 2) as i:
                for b in range(2):
                    split_lo_block(i, 16, H_OUT + 8 * b)
            dve.wait_ge(o_bc, 64)
            dve.tensor_tensor(GB[:, 0], GB[:, 0], GB[:, 1], ALU.add)
            dve.drain()
            dve.tensor_tensor(GB[:, 0], GB[:, 0], GB[:, 2], ALU.mult)
            dve.drain()
            dve.wait_ge(o_sq, 2)
            dve.tensor_scalar(MSQ, MSQ, 1.0 / D, RMS_EPS, ALU.mult, ALU.add)
            dve.drain()
            rsqrt(RSTD, MSQ, RTMP)
            for t in range(TT):
                dve.scalar_tensor_tensor(SUM[:, t, :], SUM[:, t, :], RSTD[:, t:t + 1], GB[:, 0], ALU.mult, ALU.mult)
                dve.drain()
                dve.tensor_tensor(XRES[:, t, :], XRES[:, t, :], SUM[:, t, :], ALU.add).then_inc(x1_done, 1)
            for g in range(8):
                take_lo(dve, G_X1 + g, 2 * g)

            def ffn(h0, blk, g0, n0, zeroed):
                def gate_up(i, per, h, b, n):
                    split_lo_block(i, per, h)
                    dve.wait_ge(ff_sig, i + n)
                    dve.tensor_tensor(GS, acc(b), SIG, ALU.mult).then_inc(acc_free[b % 2], 1)
                    split_lo_block(i, per, h + 8)
                    dve.wait_ge(half_done, i * per + (h + 16))
                    dve.tensor_tensor(HID, acc(b + 1), GS, ALU.mult).then_inc(acc_free[(b + 1) % 2], 1)

                def hidden_lo(i, g):
                    for j in range(2):
                        dve.wait_ge(tp_hi, i * 2 + (g + j + 1))
                        dve.tensor_tensor(glo[:, 2 * j:2 * j + 2, :], tp(j).rearrange("p (k t) -> p k t", k=2),
                                          ghi[:, 2 * j:2 * j + 2, :].bitcast(F32), ALU.subtract).then_inc(tp_lo, 1)

                def down(i, per, h, b):
                    for n in range(4):
                        split_lo(dve, i, per, h + 2 * n + 2)
                        split_lo(dve, i, per, h + 2 * n + 3)
                        dve.wait_ge(half_done, i * per + (h + 2 * n + 2))
                        part = SUM[:, :, n * NB:(n + 1) * NB]
                        dve.tensor_tensor(part, part, acc(b + n), ALU.add).then_inc(acc_free[(b + n) % 2], 1)

                gate_up(0, 0, h0, blk, n0 + 1)
                hidden_lo(0, g0)
                dve.wait_ge(ff_zero, zeroed)
                with dve.Fori(0, FB - 1) as i:
                    gate_up(i, 24, h0 + 16, blk + 2, n0 + 2)
                    down(i, 24, h0 + 32, blk + 4)
                    hidden_lo(i, g0 + 2)
                down(0, 0, h0 + 24 * FB - 8, blk + 6 * FB - 4)
                dve.drain()

            def layer_norm(n, scale):
                for t in range(TT):
                    dve.tensor_scalar(XRES[:, t, :], XRES[:, t, :], ALPHA, None, ALU.mult)
                    dve.drain()
                    dve.scalar_tensor_tensor(SUM[:, t, :], SUM[:, t, :], scale, XRES[:, t, :], ALU.mult, ALU.add)
                    dve.drain()
                    stats(SUM, t)
                dve.drain()
                dve.tensor_scalar(MSQ, MV[:, :, 1], LN_EPS, None, ALU.add)
                dve.drain()
                rsqrt(RSTD, MSQ, RTMP)
                dve.wait_ge(n_bc, 32 * (n + 1))
                for t in range(TT):
                    dve.tensor_scalar(XRES[:, t, :], SUM[:, t, :], MV[:, t, 0:1], RSTD[:, t:t + 1], ALU.subtract,
                                      ALU.mult)
                    dve.drain()
                    dve.tensor_tensor(XRES[:, t, :], XRES[:, t, :], NG[:, 0], ALU.mult)
                    dve.drain()
                    dve.tensor_tensor(XRES[:, t, :], XRES[:, t, :], NG[:, 1], ALU.add).then_inc(x_done, 1)

            ffn(H_FFN1, B_FFN1, G_FFN1, 0, 1)
            layer_norm(0, 0.5)
            for g in range(8):
                take_lo(dve, G_X2 + g, 2 * g)
            with dve.Fori(0, 2) as i:
                for b in range(2):
                    split_lo_block(i, 16, H_IN2 + 8 * b)

            def splits(m, end):
                for h in range(m, end):
                    split_lo(dve, 0, 0, H_HY + h + 2)

            def hyena_input(u, m0):
                m1 = HY_PARTS[u]
                splits(m0, m1)
                dve.wait_ge(hy_in, 64 * (u + 1))
                for s in range(3):
                    dve.tensor_tensor(HL[:, s], HL[:, s], bc(HW[:, s, :], TT), ALU.mult)
                dve.drain()
                splits(m1, m1 + 1)
                z = HZ[:, u % 3]
                dve.tensor_tensor(z, HL[:, 0], HL[:, 1], ALU.add)
                dve.tensor_tensor(HL[:, 2], HL[:, 2], bc(HW[:, 3, :], TT), ALU.add)
                dve.drain()
                dve.tensor_tensor(z, z, HL[:, 2], ALU.add).then_inc(hy_z, 1)
                return m1 + 1

            def hyena_unit(u, m0):
                m1 = HY_UNITS[u]
                splits(m0, m1)
                dve.wait_ge(hy_f, u + 1)
                dve.wait_ge(hy_kin, 32 * (u + 1))
                re, im = ps[:, 4:6, :], ps[:, 6:8, :]
                dve.tensor_tensor(HY_[:, 0:2], re, HK[0], ALU.mult)
                splits(m1, m1 + 1)
                dve.tensor_tensor(HT[:, 0], im, HK[1], ALU.mult)
                dve.tensor_tensor(HY_[:, 2:4], re, HK[1], ALU.mult)
                splits(m1 + 1, m1 + 2)
                dve.tensor_tensor(HT[:, 1], im, HK[0], ALU.mult)
                dve.drain()
                dve.tensor_tensor(HY_[:, 0:2], HY_[:, 0:2], HT[:, 0], ALU.subtract)
                dve.tensor_tensor(HY_[:, 2:4], HY_[:, 2:4], HT[:, 1], ALU.add).then_inc(hy_m, 1)
                splits(m1 + 2, m1 + 4)
                dve.wait_ge(hy_i, u + 1)
                dst = HZ[:, 0] if u % 2 == 0 else SRC[:, :, u // 2 * NB:(u // 2 + 1) * NB]
                dve.tensor_tensor(dst, ps[:, 4:6, :], HZ[:, 1 + u % 2], ALU.mult).then_inc(hy_y, 1)
                dve.drain()
                return m1 + 4

            m = 0
            for cb in range(2):
                for part in range(3):
                    m = hyena_input(3 * cb + part, m)
                for n in range(2):
                    m = hyena_unit(2 * cb + n, m)
            splits(m, 64)
            for t in range(TT):
                for s in range(2):
                    dve.bn_stats(STATS[:, t, s, :], SRC[:, t, s * NB:(s + 1) * NB])
                dve.drain()
                dve.bn_aggr(MV[:, t, :], STATS[:, t, 0:2])
            dve.drain()
            dve.tensor_tensor(MSQ, MV[:, :, 0], MV[:, :, 0], ALU.mult)
            dve.drain()
            dve.tensor_tensor(MSQ, MSQ, MV[:, :, 1], ALU.add)
            dve.drain()
            dve.tensor_scalar(MSQ, MSQ, LN_EPS, None, ALU.add)
            dve.drain()
            rsqrt(RSTD, MSQ, RTMP)
            dve.wait_ge(hy_tab, 80)
            for t in range(TT):
                dve.scalar_tensor_tensor(SRC[:, t, 0:DA], SRC[:, t, 0:DA], RSTD[:, t:t + 1], HG, ALU.mult, ALU.mult)\
                   .then_inc(hy_g, 1)

            for g in range(4):
                take_lo(dve, G_Y2 + g, 2 * g)

            def splits(m, end):
                for h in range(m, end):
                    split_lo(dve, 0, 0, H_OUT2 + h + 2)

            splits(0, 2)
            for n in range(2):
                dve.wait_ge(acc_free[n], (B_OUT2 - n + 1) // 2)
            dve.wait_ge(at_in, 48)
            for n, x in enumerate((AQ, AK)):
                g = x.rearrange("p t (g e) -> p t g e", e=64)
                a, b = g[:, :, :, 0:8], g[:, :, :, 8:16]
                cos, sin = (ROPE[:, s].unsqueeze(2).to_broadcast([P, TT, 16, 8]) for s in range(2))
                tmp = [RT[:, s].rearrange("p t (g e) -> p t g e", e=8) for s in range(4)]
                for dst, src, tab in ((tmp[0], a, cos), (tmp[1], b, sin), (tmp[2], b, cos), (tmp[3], a, sin)):
                    dve.tensor_tensor(dst, src, tab, ALU.mult)
                dve.drain()
                dve.tensor_tensor(a, tmp[0], tmp[1], ALU.subtract)
                dve.tensor_tensor(b, tmp[2], tmp[3], ALU.add).then_inc(at_rope, 1)
                dve.drain()
                splits(2 + n, 3 + n)
            for n in range(2):
                dve.tensor_tensor(RT[:, n, 0, 0:64], LAM[:, 2 * n], LAM[:, 2 * n + 1], ALU.mult)
            dve.drain()
            dve.tensor_reduce(AST[:, 0:2], RT[:, 0:2, 0, 0:64], AX.X, ALU.add).then_inc(at_lam, 1)
            dve.wait_ge(at_le, 1)
            dve.scalar_tensor_tensor(AST[:, 4:5], AST[:, 2:3], LAMBDA_INIT, AST[:, 3:4], ALU.add, ALU.subtract)
            dve.tensor_scalar(SUBG, SUBG, 1.0 - LAMBDA_INIT, None, ALU.mult)
            dve.drain()

            def maxima(h):
                dve.wait_ge(at_s, h + 1)
                n = 8 + 4 * h
                dve.tensor_reduce(AST[:, n:n + 4], ps[:, 4:6, :]
                                  .rearrange("p m (t k) -> p (m t) k", t=TT), AX.X, ALU.max)
                dve.drain()
                dve.tensor_scalar(AST[:, n:n + 4], AST[:, n:n + 4], -0.125, None, ALU.mult).then_inc(at_max, 1)

            maxima(0)
            for h in range(8):
                dve.wait_ge(at_e, h + 1)
                n = 40 + 4 * h
                dve.reciprocal(AST[:, 72:76], AST[:, n:n + 4])
                dve.drain()
                dve.tensor_scalar(AST[:, 76:78], AST[:, 74:76], AST[:, 4:5], None, ALU.mult)
                dve.drain()
                if h:
                    dve.wait_ge(at_wt, h)
                for t in range(TT):
                    dve.tensor_scalar(EE[:, 1, t, :], EE[:, 1, t, :], AST[:, 76 + t:77 + t], None, ALU.mult)
                dve.drain()
                for t in range(TT):
                    ins = dve.scalar_tensor_tensor(WW[:, t, :], EE[:, 0, t, :], AST[:, 72 + t:73 + t], EE[:, 1, t, :],
                                                   ALU.mult, ALU.subtract)
                ins.then_inc(at_w, 1)
                if h < 7:
                    maxima(h + 1)
                splits(4 + h, 5 + h)
            splits(12, 13)
            dve.wait_ge(at_oe, 8)
            dve.tensor_tensor(AO2, AO, AO, ALU.mult)
            dve.drain()
            dve.tensor_reduce(AMS, AO2.rearrange("p t (h n) -> p (t h) n", n=P), AX.X, ALU.add)
            dve.drain()
            dve.tensor_scalar(AMS, AMS, 1.0 / P, LN_EPS, ALU.mult, ALU.add)
            dve.drain()
            splits(13, 14)
            rsqrt(ARS, AMS, AST[:, 80:96])
            splits(14, 15)
            for t in range(TT):
                ao = AO[:, t, :].rearrange("p (h n) -> p h n", n=P)
                dve.tensor_tensor(ao, ao, bcl(ARS[:, 8 * t:8 * t + 8], P), ALU.mult)
                dve.drain()
                dve.tensor_tensor(ao, ao, bc(SUBG, 8), ALU.mult).then_inc(at_g, 1)
            splits(15, 16)
            for g in range(4, 8):
                take_lo(dve, G_Y2 + g, 2 * g)
            with dve.Fori(0, 2) as i:
                for b in range(2):
                    h0 = H_OUT2 + 16 + 4 * b
                    for q in range(4):
                        split_lo(dve, i, 8, h0 + q + 2)
                    dve.wait_ge(half_done, i * 8 + (h0 + 4))
                    part = SUM[:, :, ds(i * (2 * NB) + b * NB, NB)]
                    dve.tensor_tensor(part, part, acc(B_OUT2 + 4 + b), ALU.add)\
                       .then_inc(acc_free[(B_OUT2 + b) % 2], 1)
            dve.drain()
            layer_norm(1, 1.0)
            for g in range(8):
                take_lo(dve, G_X3 + g, 2 * g)
            ffn(H_FFN2, B_FFN2, G_FFN2, FB, 2)
            layer_norm(2, 0.5)



def constants():
    t = np.arange(T)
    theta = 2.0 * np.pi * (np.arange(T) + 0.5) / (2 * T)
    ang = np.outer(t, theta)
    dft = np.stack([np.cos(ang), -np.sin(ang), np.cos(ang).T / T, -np.sin(ang).T / T])
    bands = 16
    lin = np.linspace(0.0, 1.0, T, dtype=np.float32)[:, None]
    w = (2.0 * np.pi * np.arange(T)[:, None] / T).astype(np.float32)
    f = np.linspace(1e-4, bands - 1, bands, dtype=np.float32)[None, :]
    fw = (f * w).astype(np.float64)
    z = np.concatenate([lin, np.cos(fw), -np.sin(fw)], axis=-1)
    lo, hi = math.log(1e-2) / 1.5, math.log(1e-2) / 0.3
    deltas = np.abs(np.linspace(lo, hi, DA))
    decay = np.exp(-lin.astype(np.float64) * deltas)
    back = decay.copy()
    back[0] = 0.0
    inv = 500000.0 ** (-np.arange(0, 16, 2) / 16.0)
    pos = np.outer(t, inv.astype(np.float32))
    p = np.arange(P)
    same = p[:, None] // CH == p[None, :] // CH
    before = same & (p[:, None] < p[None, :])
    upto = same & (p[:, None] <= p[None, :])
    levels = []
    for s in (1, 2, 4, 8, 16, 32):
        pair = p[:, None] // (2 * s) == p[None, :] // (2 * s)
        levels.append(pair & (p[:, None] // s % 2 == 0) & (p[None, :] // s % 2 == 1))
    steps = np.zeros((P, P))
    steps[p, p // CH] = 1.0
    masks = [before, upto, before, upto, before.T] + levels[1:] + [levels[0].T, levels[0], steps]
    return {
        "ident": np.eye(P), "dft": dft, "hy_zt": z.T, "hy_decay": np.stack([decay, back]),
        "rope": np.stack([np.cos(pos), np.sin(pos)]), "masks": np.stack(masks, axis=1),
        "zeros": np.zeros((1, N_IN)),
    }


def kernel(**inputs):
    import concourse.bacc as _bacc
    from concourse.bass_utils import run_bass_kernel_spmd as _run

    g = {n: np.asarray(a) for n, a in inputs.items()}
    arrays = {}
    for n in ("x", "c", "ada_b", "pre_gain", "post_gain", "ln1_g_2", "ln1_b_2", "ln2_g_2", "ln2_b_2", "ln3_g_2",
              "ln3_b_2", "hyena_norm_g_2", "subln_g_2"):
        arrays[n] = g[n]
    for n in ("ada_w", "w_in", "p_a", "p_b", "w_out", "ffn1_w_gate_2", "ffn1_w_up_2", "ffn1_w_down_2", "w_in_2",
              "w_out_2", "ffn2_w_gate_2", "ffn2_w_up_2", "ffn2_w_down_2", "conv_w", "filt_w1_2", "filt_w2_2",
              "filt_w3_2", "filt_w_out_2", "hyena_bias_2"):
        arrays[n] = g[n][0]
    mu = g["mu_shift"][0]
    arrays["mu_lora"] = mu[None, 3 * DA:]
    arrays["wkv_rows"] = np.stack([mu[0:DA], mu[DA:2 * DA], mu[2 * DA:3 * DA], g["k_k"][0], g["k_a"][0],
                                   g["r_k"][0].reshape(DA), g["lnx_gain"][0], g["lnx_bias"][0]])
    arrays["lora_w"] = np.stack([np.concatenate([g["w2"][0], g["w0"]]), np.concatenate([g["a2"][0], g["a0"]])])
    arrays["filt_cols"] = np.stack([g["filt_b1_2"][0], g["filt_b2_2"][0], g["filt_b3_2"][0], g["filt_freq_2"][0]],
                                   axis=1)
    arrays["hyena_rows"] = np.concatenate([g["hyena_conv_w_2"][0], g["hyena_conv_b_2"]])
    arrays["lambdas"] = np.concatenate([g["lambda_q1_2"], g["lambda_k1_2"], g["lambda_q2_2"], g["lambda_k2_2"]])
    for n, a in constants().items():
        arrays[n] = a.astype(np.float32)
    arrays = {f"in_{n}": np.ascontiguousarray(a) for n, a in arrays.items()}

    nc = _bacc.Bacc("TRN2", target_bir_lowering=False, num_devices=1)
    aps = {n[3:]: nc.dram_tensor(n, a.shape, F32, kind="ExternalInput").ap() for n, a in arrays.items()}
    out = nc.dram_tensor("out", (1, T, D), F32, kind="ExternalOutput").ap()
    with nc.allow_non_contiguous_dma(reason="short rows of parameters"):
        build(nc, aps, out)
    r = _run(nc, [arrays], core_ids=[0])
    return r.results[0]["out"]
```

```python
from contextlib import ExitStack
import math

import numpy as np
import concourse.bass as bass
from concourse import mybir

F32 = mybir.dt.float32
F32R = mybir.dt.float32r
ALU = mybir.AluOpType
ACT = mybir.ActivationFunctionType
AX = mybir.AxisListType
ds = bass.ds

P = 128
T = 256
TT = T // P
D = 2048
KT = D // P
NB = 512
DA = 1024
HP = DA // P
LORA = 64
COLS_A = 3 * DA + 2 * LORA
OFF_ZA = COLS_A
OFF_B = OFF_ZA + DA
OFF_ZB = OFF_B + 3 * DA
OFF_GATE = OFF_B + 4 * DA
N_IN = OFF_GATE + 2 * D
F = 5632
FB = F // NB
D_IN = 6144
RMS_EPS = 1e-6
GN_EPS = 64e-5
LN_EPS = 1e-5
ALPHA = 2.0 ** 0.25
LAMBDA_INIT = 0.8 - 0.6 * math.exp(0.0)
CH = 64
NCH = T // CH
PARAM_ROWS = 8
TWO_PI_HI = 6.28125
TWO_PI_LO = 2.0 * math.pi - TWO_PI_HI
ROUND = 1.5 * 2.0 ** 23
PI_IN = 3.1415925

H_LORA = 0
H_FIRST = H_LORA + 2
H_IN = H_FIRST + 16
IN_BLOCKS = (N_IN - 2 * LORA) // NB
H_PAB = H_IN + 8 * (IN_BLOCKS - 2)
H_OUT = H_PAB + 4 * 8
H_FFN1 = H_OUT + 4 * 8
FFN_HALVES = 8 + 8 + 4 * 2
H_IN2 = H_FFN1 + FB * FFN_HALVES
H_HY = H_IN2 + 4 * 8
H_OUT2 = H_IN2 + 8 * (D_IN // NB)
H_FFN2 = H_OUT2 + 4 * 8
H_END = H_FFN2 + FB * FFN_HALVES

B_LORA = 0
B_FIRST = 1
B_IN = B_FIRST + 2
B_PAB = B_IN + IN_BLOCKS - 2
B_OUT = B_PAB + 8
B_FFN1 = B_OUT + 4
B_IN2 = B_FFN1 + FB * 6
B_HY = B_IN2 + 4
FILTERS_AFTER = 10, 14, 20, 24
GATE_TILES = (0, 1), (2, 3), (4, 5, 6), (7, 8, 9), (10, 11, 12), (13, 14, 15)
GATE_AFTER = (3, 7), (2, 6), (1, 4, 7), (1, 4, 7), (1, 4, 7), (1, 4, 7)
HY_PARTS = 8, 14, 20, 33, 40, 47
HY_UNITS = 23, 28, 50, 55
B_OUT2 = B_IN2 + D_IN // NB
B_FFN2 = B_OUT2 + 8


def build(nc, A, out):
    ctx = ExitStack()
    with ctx:
        def sb(name, shape, dt=F32):
            return ctx.enter_context(nc.sbuf_tensor(name, shape, dt))

        def sem(name):
            return ctx.enter_context(nc.semaphore(name))

        raw = sb("w_raw", [P, 4, 4 * NB])
        whi = sb("w_hi", [P, 4, 2 * NB], F32R)
        wlo = sb("w_lo", [P, 4, 2 * NB], F32R)
        ahi = sb("act_hi", [P, KT, T], F32R)
        alo = sb("act_lo", [P, KT, T], F32R)
        ghi = sb("hid_hi", [P, 4, T], F32R)
        glo = sb("hid_lo", [P, 4, T], F32R)
        ident = sb("ident", [P, P])
        ones = sb("ones", [P, P])
        small = sb("small", [P, 128])
        arena = sb("arena", [P, 25600])
        ps = ctx.enter_context(nc.psum_tensor("ps", [P, 8, NB], F32))

        def at(off, *dims):
            v = arena[:, off:off + math.prod(dims)]
            if len(dims) == 1:
                return v
            names = " ".join("abcd"[:len(dims)])
            return v.rearrange(f"p ({names}) -> p {names}", **dict(zip("abcd", dims)))

        def acc(block):
            b = 2 * (block % 2)
            return ps[:, b:b + 2, :]

        def tp(n):
            return ps[:, 4 + n, :]

        XRES = at(0, TT, D)
        SRC = at(4096, TT, D)
        SUM = at(8192, TT, D)
        STG = at(12288, 2, TT, NB)
        R5 = 14336

        proj1 = nc.dram_tensor("proj1", [T + 2, N_IN], F32).ap()
        proj2 = nc.dram_tensor("proj2", [T + 2, D_IN], F32).ap()
        y_cat = nc.dram_tensor("y_cat", [T, D], F32).ap()
        filt = nc.dram_tensor("filt", [2, 2, P, 4 * NB], F32).ap()
        mod_gate = nc.dram_tensor("mod_gate", [1, D], F32).ap()
        hy_out = nc.dram_tensor("hy_out", [T, DA], F32).ap()

        def wait_alone(eng, semaphore, value):
            eng.wait_ge(semaphore, value)
            eng.sem_inc(waits_done, 1)

        def level(ap, lv, sides=2):
            return ap.rearrange("p (g s b) -> p g s b", s=sides, b=2 << lv)

        def quarter(ap, q):
            return ap[..., q * NB:(q + 1) * NB]

        def tokens(ap):
            return ap.rearrange("(t p) n -> p t n", p=P)

        def bc(ap, n):
            return ap.unsqueeze(1).to_broadcast([ap.shape[0], n, ap.shape[-1]])

        def rows(ap, n):
            return ap.partition_broadcast(n)

        raw_in = [sem(f"raw_in{n}") for n in range(4)]
        hi_ready = sem("hi_ready")
        lo_ready = sem("lo_ready")
        half_done = sem("half_done")
        acc_free = [sem(f"acc_free{n}") for n in range(2)]
        tp_ready = sem("tp_ready")
        tp_hi = sem("tp_hi")
        tp_lo = sem("tp_lo")
        stg_out = [sem(f"stg_out{n}") for n in range(2)]
        s_const = sem("s_const")
        s_rows = sem("s_rows")
        s_ones = sem("s_ones")
        waits_done = sem("waits_done")
        x_done = sem("x_done")
        x_own = sem("x_done_dve")
        x_out = sem("x_out")
        ada_in = [sem(f"ada_in{n}") for n in range(4)]
        ada_done = sem("ada_done")
        gate_w_in = [sem(f"gate_w_in{n}") for n in range(2)]
        gate_done = sem("gate_done")
        rows_t = sem("rows_t")
        c_sig = sem("c_sig")
        c_act = sem("c_act")
        mod_cols = sem("mod_cols")
        mod_row = sem("mod_row")
        mod_row_sb = sem("mod_row_sb")
        mod_stored = sem("mod_stored")
        mod_scale = sem("mod_scale")
        x_in = sem("x_in")
        x_norm = sem("x_norm")
        f_in = sem("f_in")
        f_mlp = sem("f_mlp")
        f_arg = sem("f_arg")
        f_sin = sem("f_sin")
        f_h = sem("f_h")
        f_sd = sem("f_sd")
        f_sd0 = sem("f_sd0")
        f_hb = sem("f_hb")
        x_sq = sem("x_sq")
        f_k = sem("f_k")
        f_ke = sem("f_ke")
        f_dec = sem("f_dec")
        f_st = sem("f_st")
        zero_rows = sem("zero_rows")


        def load_chunk(sp, i, per, h, src):
            slot = h // 2 % 4
            if h >= 8:
                sp.wait_ge(lo_ready, i * per + (h - 8 + 2))
            else:
                sp.wait_ge(ada_done, 28 + h // 2 + 1)
            dst = raw[:, slot, :].rearrange("p (k n) -> p k n", n=src.shape[-1])
            sp.dma_start(dst, src).then_inc(raw_in[slot], 16)

        def split_hi(act, i, per, h):
            if h >= H_END:
                return
            slot = h // 2 % 4
            if h % 2 == 0:
                act.wait_ge(raw_in[slot], i * (per * 2) + 16 * (h // 8 + 1))
            if h >= 4:
                act.wait_ge(half_done, i * per + (h - 4 + 1))
            act.activation(whi[:, h % 4, :], raw[:, slot, h % 2 * 2 * NB:(h % 2 + 1) * 2 * NB], ACT.Copy)\
               .then_inc(hi_ready, 1)

        def split_lo(dve, i, per, h):
            if h >= H_END:
                return
            dve.wait_ge(hi_ready, i * per + (h + 1))
            dve.tensor_tensor(wlo[:, h % 4, :], raw[:, h // 2 % 4, h % 2 * 2 * NB:(h % 2 + 1) * 2 * NB],
                              whi[:, h % 4, :].bitcast(F32), ALU.subtract).then_inc(lo_ready, 1)

        def products(pe, i, per, h, xh, xl, banks, first, last, cols=NB, part=None):
            nk = 2 * NB // cols
            ks = range(nk) if part is None else (part,)
            if 0 in ks:
                pe.wait_ge(lo_ready, i * per + (h + 1))
            hi = whi[:, h % 4, :].rearrange("p (k n) -> p k n", k=nk)
            lo = wlo[:, h % 4, :].rearrange("p (k n) -> p k n", k=nk)
            for k in ks:
                for t in range(TT):
                    ts = slice(t * P, (t + 1) * P)
                    dst = banks[:, t, 0:cols]
                    pe.matmul(dst, xh[:, k, ts], hi[:, k, :], start=first and k == 0, stop=False)
                    pe.matmul(dst, xh[:, k, ts], lo[:, k, :], start=False, stop=False)
                    mm = pe.matmul(dst, xl[:, k, ts], hi[:, k, :], start=False, stop=last and k == nk - 1)
            if part != 0:
                mm.then_inc(half_done, 1)

        def block_2048(pe, i, per, h, blk_per, blk, group=None):
            if blk >= 2:
                pe.wait_ge(acc_free[blk % 2], i * (blk_per // 2) + blk // 2)
            for q in range(8):
                if group is not None:
                    pe.wait_ge(tp_lo, group + q + 1)
                products(pe, i, per, h + q, ahi[:, 2 * q:2 * q + 2, :], alo[:, 2 * q:2 * q + 2, :],
                         acc(blk), q == 0, q == 7)

        def transpose_group(pe, n, src, k):
            if n >= 4:
                pe.wait_ge(tp_lo, n - 3)
            for j in range(2):
                for t in range(TT):
                    mm = pe.transpose(tp(n % 4)[:, j * T + t * P:j * T + (t + 1) * P],
                                      src[:, t, (k + j) * P:(k + j + 1) * P], ident[:, :])
            mm.then_inc(tp_ready, 1)

        def take_hi(act, n, k):
            act.wait_ge(tp_ready, n + 1)
            act.activation(ahi[:, k:k + 2, :], tp(n % 4).rearrange("p (k t) -> p k t", k=2), ACT.Copy)\
               .then_inc(tp_hi, 1)

        def take_lo(dve, n, k):
            dve.wait_ge(tp_hi, n + 1)
            dve.tensor_tensor(alo[:, k:k + 2, :], tp(n % 4).rearrange("p (k t) -> p k t", k=2),
                              ahi[:, k:k + 2, :].bitcast(F32), ALU.subtract).then_inc(tp_lo, 1)

        G_H, G_Y, G_M, G_X1 = 0, 8, 16, 24
        G_FFN1 = 32
        G_X2 = G_FFN1 + 2 * FB
        G_Y2 = G_X2 + 8
        G_X3 = G_Y2 + 8
        G_FFN2 = G_X3 + 8

        ADA = at(0, 2 * D)
        WOF = at(4096, 4 * DA)
        DEC = at(22728, 2, TT, NB)
        ADAG = at(19456, D)
        GW = [at(n * D, D) for n in range(2)]
        BROW = at(12288, 2, DA)
        FC = at(14336, TT, T)
        FS = at(14848, TT, T)
        HFB = at(15360, 2, TT, NB)
        SD = at(17408, 2, TT, NB)
        KST = at(19456, 4, NB)
        ZT = at(21504, T)
        FW = at(21760, 3, 64)
        FCOL = at(21952, 4)
        H1 = at(21960, T)
        H2 = at(22216, T)
        ROWS = at(22472, P)
        COLS = at(22600, 64)
        CACT = at(22664, 32)
        MODC = at(22696, 32)
        GROW = at(22728, 2048)
        HTMP = at(24776, 2, T)
        COEF = small[:, 0:32]
        STATS = small[:, 64:112].rearrange("p (t s v) -> p t s v", t=TT, s=4)
        MV = small[:, 112:116].rearrange("p (t v) -> p t v", t=TT)
        MSQ = small[:, 116:118]
        RSTD = small[:, 118:120]
        RTMP = small[:, 120:122]
        NMR = small[:, 122:124]
        SQ = small[:, 64:72].rearrange("p (t s) -> p t s", t=TT)

        ada_w = A["ada_w"].rearrange("(k p) n -> p k n", p=P)
        w_in = A["w_in"].rearrange("(k p) n -> p k n", p=P)
        wk = {n: A[n].rearrange("(k p) n -> p k n", p=P) for n in
              ("p_a", "p_b", "w_out", "ffn1_w_gate_2", "ffn1_w_up_2", "ffn1_w_down_2", "w_in_2", "w_out_2",
               "ffn2_w_gate_2", "ffn2_w_up_2", "ffn2_w_down_2")}

        HY = 3 * DA

        block = ctx.enter_context(nc.Block())

        @block.sync
        def _(sp):
            sp.dma_start(ident[:, :], A["ident"]).then_inc(s_const, 16)
            sp.dma_start(ROWS[0:16, :], A["c"].rearrange("a (k p) -> (a k) p", p=P)).then_inc(s_rows, 16)
            sp.dma_start(ROWS[16:32, :], A["pre_gain"].rearrange("a (k p) -> (a k) p", p=P)).then_inc(s_rows, 16)
            sp.dma_start(ROWS[32:64, :], A["ada_b"][:, 0:2 * D].rearrange("a (k p) -> (a k) p", p=P))\
              .then_inc(s_rows, 16)
            for n in range(32):
                if n >= 4:
                    sp.wait_ge(ada_done, n - 3)
                sp.dma_start(raw[:, n % 4, :], ada_w[:, n % 16, n // 16 * D:(n // 16 + 1) * D])\
                  .then_inc(ada_in[n % 4], 16)

            load_chunk(sp, 0, 0, H_LORA, w_in[:, :, 3 * DA:3 * DA + P])

            def load_block(i, per, h, w, col):
                for q in range(4):
                    load_chunk(sp, i, per, h + 2 * q, w[:, 4 * q:4 * q + 4, ds(col, NB)])

            for b in range(2):
                load_block(0, 0, H_FIRST + 8 * b, w_in, b * NB)
            with sp.Fori(0, 2) as i:
                for b in range(2):
                    load_block(i, 16, H_IN + 8 * b, w_in, i * (2 * NB) + (2 + b) * NB)
            with sp.Fori(0, 9) as i:
                for b in range(2):
                    load_block(i, 16, H_IN + 32 + 8 * b, w_in, i * (2 * NB) + (OFF_ZA + b * NB))
            with sp.Fori(0, 4) as i:
                for n, w in enumerate(("p_b", "p_a")):
                    for q in range(2):
                        load_chunk(sp, i, 8, H_PAB + 4 * n + 2 * q, wk[w][:, 4 * q:4 * q + 4, ds(i * NB, NB)])
            with sp.Fori(0, 2) as i:
                for b in range(2):
                    load_block(i, 16, H_OUT + 8 * b, wk["w_out"], i * (2 * NB) + b * NB)

            def load_ffn(h0, gate, up, down):
                load_block(0, 0, h0, wk[gate], 0)
                load_block(0, 0, h0 + 8, wk[up], 0)
                with sp.Fori(0, FB - 1) as i:
                    load_block(i, 24, h0 + 16, wk[gate], i * NB + NB)
                    load_block(i, 24, h0 + 24, wk[up], i * NB + NB)
                    for n in range(4):
                        load_chunk(sp, i, 24, h0 + 32 + 2 * n, wk[down][:, ds(i * 4, 4), n * NB:(n + 1) * NB])
                for n in range(4):
                    load_chunk(sp, 0, 0, h0 + 24 * FB - 8 + 2 * n,
                               wk[down][:, 4 * FB - 4:4 * FB, n * NB:(n + 1) * NB])

            load_ffn(H_FFN1, "ffn1_w_gate_2", "ffn1_w_up_2", "ffn1_w_down_2")
            with sp.Fori(0, 2) as i:
                for b in range(2):
                    load_block(i, 16, H_IN2 + 8 * b, wk["w_in_2"], i * (2 * NB) + b * NB)
            for b, col in enumerate((4, 5, 10, 11, 6, 7, 8, 9)):
                load_block(0, 0, H_HY + 8 * b, wk["w_in_2"], col * NB)
            for part in range(2):
                with sp.Fori(0, 2) as i:
                    for b in range(2):
                        for q in range(2):
                            k = 8 * part + 4 * q
                            load_chunk(sp, i, 8, H_OUT2 + 16 * part + 4 * b + 2 * q,
                                       wk["w_out_2"][:, k:k + 4, ds(i * (2 * NB) + b * NB, NB)])
            load_ffn(H_FFN2, "ffn2_w_gate_2", "ffn2_w_up_2", "ffn2_w_down_2")
            for q in range(4):
                if q < 2:
                    sp.wait_ge(x_done, 7 + q)
                else:
                    sp.wait_ge(x_own, 7 + q - 2)
                sp.dma_start(quarter(tokens(out[0]), q), quarter(XRES, q)).then_inc(x_out, 16)
            sp.wait_ge(x_out, 64)

        (w_mix, w_z, w_tanh, w_ld, w_cum, w_exp, w_tok, w_t4p, w_t4, w_gram, w_mask, w_t0,
         w_ms, w_u, w_ue, w_dt, w_tn, w_w1, w_w1e, w_sa0, w_sae, w_sap, w_delta, w_state, w_y, w_ye,
         w_yo, w_st, w_prep, w_lora, w_lorat, w_loras, w_kin) = [sem("wkv_" + n) for n in (
             "mix z tanh logdecay cumulated exp tok t4 t4_sb gram masked t0 "
             "m u u_sb dt tn w1 w1_sb sa0 sa sa_state delta state y y_sb out stored prep lora lora_t "
             "lora_sb const").split()]
        w_in_s = [sem(f"wkv_in{n}") for n in range(2)]
        w_za = sem("wkv_za")
        w_zag = sem("wkv_za_gate")
        cv_in = sem("conv_in")
        cv_sig = sem("conv_gate")
        cv_out = sem("conv_out")
        yb_in = sem("yb_in")
        ya_in = sem("ya_in")
        ga_in = sem("ga_in")
        ga_sig = sem("ga_sig")
        m_done = sem("m_done")
        o_bc = sem("o_bc")
        o_sq = sem("o_sq")
        x_stat = sem("x_stat")
        x_norm_act = sem("x_normed")
        x_gain = sem("x_gained")
        x_scaled = sem("x_scaled")
        n_bc = sem("n_bc")
        ff_sig = sem("ff_sig")
        ff_zero = sem("ff_zero")
        hy_tab = sem("hy_tab")
        hy_in = sem("hy_in")
        hy_z = sem("hy_z")
        hy_kin = sem("hy_kin")
        hy_f = sem("hy_f")
        hy_m = sem("hy_m")
        hy_i = sem("hy_i")
        hy_y = sem("hy_y")
        hy_g = sem("hy_g")
        at_in = sem("at_in")
        at_lam = sem("at_lam")
        at_le = sem("at_le")
        at_rope = sem("at_rope")
        at_tp = sem("at_tp")
        at_tps = sem("at_tps")
        at_s = sem("at_s")
        at_max = sem("at_max")
        at_e = sem("at_e")
        at_w = sem("at_w")
        at_wt = sem("at_wt")
        at_wts = sem("at_wts")
        at_o = sem("at_o")
        at_oe = sem("at_oe")
        at_g = sem("at_g")

        CUR = at(0, TT, 3, P), at(18816, TT, 3, P)
        PRV = at(768, TT, 3, P), at(19584, TT, 3, P)
        PRM = at(1536, PARAM_ROWS, P), at(20352, PARAM_ROWS, P)
        WA = at(2560, 2, P), at(21376, 2, P)
        TOK = at(2816, TT, 4, P)
        T4 = at(3840, TT, 4, P)
        GR = at(4864, 4, 4, P)
        TM = at(6912, 4, P)
        TMT = at(7424, 4, P)
        MM = at(7936, 4, P)
        MS = at(8448, 4, P)
        UU = at(8960, 4, P)
        SG = at(9472, 2, TT, P)
        LD = at(9984, TT, P)
        KK = at(10240, TT, P)
        K2 = at(10496, TT, P)
        BB = at(10752, TT, P)
        RK = at(11008, TT, P)
        BV = at(11264, TT, P)
        EXPS = at(11520, 3, TT, P)
        W1S = at(14336, 4, 64)
        AEF = at(14592, TT, P)
        SA = at(14848, 4, 64)
        ST = at(15104, NCH, 64)
        SPC = at(15360, 64)
        YS = at(15424, 4, 64)
        YQ = at(15680, 4, 64)
        MASKS = at(15936, 13, P)
        ZA = at(21632, TT, P)
        ZAG = at(21888, TT, P)
        CG = at(22144, 3, TT, P)
        HB = at(22912, 3, TT, P)
        ZB = at(23680, TT, P)
        BG = at(23936, TT, P)
        CW = at(24192, 3, P)
        ZBG = at(24576, TT, P)
        CY = at(24832, TT, P)
        LORAW = at(17600, T)
        LORAA = at(17856, T)
        LIN = at(18112, 2, TT, P)
        MUL = at(18624, P)
        WST = small[:, 32:64]

        YB = at(22144, TT, DA)
        YA = at(4096, TT, DA)
        GA = at(R5, 2, TT, NB)
        MT = at(R5 + 2048, TT, NB)
        MU = at(R5 + 3072, TT, NB)
        GB = at(R5, 3, D)
        SIG = at(R5, TT, NB)
        GS = at(R5 + 1024, TT, NB)
        HID = at(R5 + 2048, TT, NB)
        NG = at(R5 + 4096, 2, D)
        AQ = at(8192, TT, DA)
        AK = at(10240, TT, DA)
        AV = SRC[:, :, DA:D]
        TAB = at(12288, 4, TT, T)
        HL = at(R5, 3, TT, NB)
        HT = at(10240, 2, 2, NB)
        HW = at(17408, 4, NB)
        HK = [g.bitcast(F32).rearrange("p k t -> p (k t)").rearrange("p (m n) -> p m n", n=NB) for g in (ghi, glo)]
        HZ = at(19456, 3, TT, NB)
        HY_ = at(22528, 4, NB)
        HG = at(24576, DA)
        QT = at(14336, 8, T)
        KTT = at(16384, 8, T)
        EE = at(18432, 2, TT, T)
        WW = at(19456, TT, T)
        WT2 = at(19968, 2, T)
        ROPE = at(20480, 2, TT, 8)
        LAM = at(20512, 4, 64)
        SUBG = at(20768, P)
        AO = AV
        AO2 = at(22528, TT, DA)
        RT = at(20896, 4, TT, 128)
        AST = at(21920, 128)
        AMS = at(22048, 16)
        ARS = at(22064, 16)

        @block.gpsimd
        def _(pool):
            pool.memset(ones[:, :], 1.0).then_inc(s_ones, 1)
            for dst, src in ((ZT[0:33, :], A["hy_zt"]), (FW[0:33, 0, :], A["filt_w1_2"]),
                             (FW[0:64, 1, :], A["filt_w2_2"]), (FW[0:64, 2, :], A["filt_w3_2"]),
                             (FCOL[0:64, 0:4], A["filt_cols"]), (WOF[0:64, :], A["filt_w_out_2"]),
                             (FC, A["dft"][0].rearrange("(t p) f -> p t f", p=P)),
                             (FS, A["dft"][1].rearrange("(t p) f -> p t f", p=P)),
                             (BROW[0:1, :, :], A["hyena_bias_2"].rearrange("(a n) c -> a n c", a=1))):
                pool.dma_start(dst, src).then_inc(f_in, 16)
            for r in range(2):
                pool.dma_start(proj1[r:r + 1, 0:OFF_ZB], A["zeros"][:, 0:OFF_ZB]).then_inc(zero_rows, 16)
            for r in (0, T + 1):
                pool.dma_start(proj2[r:r + 1, 0:HY], A["zeros"][:, 0:HY]).then_inc(zero_rows, 16)
            def load_decay(cb):
                for d in range(2):
                    pool.dma_start(DEC[:, d], A["hy_decay"][d].rearrange("(t p) n -> p t n", p=P)
                                   [:, :, cb * NB:(cb + 1) * NB]).then_inc(f_dec, 16)

            load_decay(0)
            for t in range(TT):
                pool.dma_start(SUM[:, t, :], A["x"][0, t * P:(t + 1) * P, :]).then_inc(x_in, 16)
            for u in range(4):
                if u == 1:
                    pool.wait_ge(f_sd0, 2)
                    load_decay(1)
                pool.wait_ge(f_hb, u + 1)
                if u:
                    pool.wait_ge(f_k, u)
                pool.tensor_tensor(SD[:, 0], HFB[:, 0], HFB[:, 1], ALU.add).then_inc(f_sd, 1)
                pool.tensor_tensor(SD[:, 1], HFB[:, 0], HFB[:, 1], ALU.subtract).then_inc(f_sd, 1)
                pool.wait_ge(f_ke, u + 1)
                pool.dma_start(filt[u % 2, u // 2], KST).then_inc(f_st, 16)

            def store_block(i, per2, s, blk, dst):
                wait_alone(pool, acc_free[blk % 2], i * per2 + (blk // 2 + 1))
                pool.dma_start(dst, STG[:, s % 2, :, 0:dst.shape[-1]]).then_inc(stg_out[s % 2], 16)

            p1 = tokens(proj1[2:T + 2, :])
            store_block(0, 0, 0, B_LORA, p1[:, :, 3 * DA:3 * DA + P])
            pool.wait_ge(f_st, 64)
            pool.wait_ge(mod_cols, 2)
            for b in range(6):
                for k in GATE_TILES[b]:
                    if k >= 2:
                        pool.wait_ge(gate_done, k - 1)
                    pool.dma_start(GW[k % 2], ada_w[:, k, 2 * D:3 * D]).then_inc(gate_w_in[k % 2], 16)
                store_block(0, 0, 1 + b, B_FIRST + b, p1[:, :, b * NB:(b + 1) * NB])

            pool.sem_inc(w_yo, 1)
            pool.wait_ge(gate_done, 16)
            pool.wait_ge(stg_out[0], 16 * 4)
            pool.wait_ge(stg_out[1], 16 * 3)
            pool.wait_ge(zero_rows, 64)
            for a, w in enumerate((LIN[:, 0], LIN[:, 1])):
                pool.dma_start(w, tokens(proj1[2 - a:T + 2 - a, 3 * DA:3 * DA + P])).then_inc(w_lora, 16)
            pool.dma_start(MUL, A["mu_lora"].rearrange("a n -> (a n)").partition_broadcast(P)).then_inc(w_lora, 16)
            pool.dma_start(MASKS, A["masks"]).then_inc(w_kin, 16)

            def load_pair(i, p):
                for a, w in enumerate((CUR[p % 2], PRV[p % 2])):
                    for t in range(TT):
                        pool.dma_start(w[:, t], proj1[2 - a + t * P:2 - a + (t + 1) * P, 0:3 * DA]
                                       .rearrange("r (q n) -> r q n", q=3)[:, :, ds(i * (2 * P) + p * P, P)])\
                            .then_inc(w_in_s[p % 2], 16)
                pool.dma_start(PRM[p % 2], A["wkv_rows"][:, ds(i * (2 * P) + p * P, P)].partition_broadcast(P))\
                    .then_inc(w_in_s[p % 2], 16)
                pool.dma_start(WA[p % 2][0:LORA + 1], A["lora_w"].rearrange("a k n -> k a n")
                               [:, :, ds(i * (2 * P) + p * P, P)]).then_inc(w_in_s[p % 2], 16)

            def mix_pair(i, p):
                pool.wait_ge(w_in_s[p % 2], i * 96 + (96 * (p // 2) + 96))
                cur, prv = (a.rearrange("p t q n -> p t (q n)") for a in (CUR[p % 2], PRV[p % 2]))
                pool.tensor_tensor(prv, prv, cur, ALU.subtract)
                pool.drain()
                pool.tensor_tensor(prv, prv, bc(PRM[p % 2][:, 0:3, :].rearrange("p q n -> p (q n)"), TT), ALU.mult)
                pool.drain()
                pool.tensor_tensor(cur, cur, prv, ALU.add).then_inc(w_mix, 1)

            def load_conv(c, ns):
                def cols(back, off):
                    return tokens(proj1[2 - back:T + 2 - back, off + c * P:off + (c + 1) * P])

                for n in ns:
                    if n < 3:
                        pool.dma_start(CG[:, n], cols(n, OFF_B + DA)).then_inc(cv_in, 16)
                        pool.dma_start(HB[:, n], cols(n, OFF_B + 2 * DA)).then_inc(cv_in, 16)
                    else:
                        pool.dma_start(ZB, cols(0, OFF_ZB)).then_inc(cv_in, 16)
                        pool.dma_start(BG, cols(0, OFF_B)).then_inc(cv_in, 16)
                        pool.dma_start(CW, A["conv_w"][:, c * P:(c + 1) * P].partition_broadcast(P))\
                            .then_inc(cv_in, 16)

            def conv(c, step):
                if step == 0:
                    pool.wait_ge(cv_sig, c + 1)
                    pool.tensor_tensor(CG, CG, HB, ALU.mult)
                    pool.tensor_tensor(ZB, ZB, BG, ALU.mult)
                    pool.drain()
                elif step == 1:
                    for n in range(3):
                        pool.tensor_tensor(CG[:, n], CG[:, n], bc(CW[:, 2 - n, :], TT), ALU.mult)
                    pool.tensor_tensor(ZB, ZB, ZBG, ALU.mult)
                    pool.drain()
                elif step == 2:
                    pool.tensor_tensor(CG[:, 0], CG[:, 0], CG[:, 1], ALU.add)
                    pool.drain()
                    pool.tensor_tensor(CG[:, 0], CG[:, 0], CG[:, 2], ALU.add)
                    pool.drain()
                else:
                    if c:
                        pool.wait_ge(cv_out, 16 * c)
                    pool.tensor_tensor(CY, CG[:, 0], ZB, ALU.mult)
                    pool.drain()
                    pool.dma_start(tokens(y_cat)[:, :, DA + c * P:DA + (c + 1) * P], CY).then_inc(cv_out, 16)

            def pair(i, p, c=None):
                more = c is None or c < 6
                wait_alone(pool, w_yo, i * 2 + (p + 1))
                if more:
                    load_pair(i, p + 1)
                pool.dma_start(ZA, p1[:, :, ds(i * (2 * P) + (OFF_ZA + p * P), P)]).then_inc(w_za, 16)
                for lv in range(5):
                    if lv == 0:
                        pool.wait_ge(w_mask, i * 4 + (2 * p + 2))
                    else:
                        pool.wait_ge(w_u, i * 10 + (5 * p + lv))
                    mt = GR.rearrange("p u g n -> p g u n")[:, 0]
                    pool.tensor_tensor(MS, mt, MASKS[:, 5 + lv, :].unsqueeze(1).to_broadcast([P, 4, P]), ALU.mult)\
                        .then_inc(w_ms, 1)
                    if lv == 2:
                        store_block(i, 2, 9 + 2 * p, B_IN + 6 + 2 * p,
                                    p1[:, :, ds(i * (4 * NB) + (OFF_ZA + (2 + 2 * p) * NB), NB)])
                    if c is not None:
                        if lv < 4:
                            conv(c, lv)
                        if lv >= 3:
                            load_conv(c + 1, ((0,), (1, 2, 3))[lv - 3])
                if more:
                    mix_pair(i, p + 1)
                if c is not None:
                    for step in range(4):
                        conv(c + 1, step)
                if not more:
                    pool.wait_ge(cv_out, 16 * 8)
                    pool.dma_start(YB, tokens(y_cat)[:, :, DA:D]).then_inc(yb_in, 16)
                wait_alone(pool, w_yo, i * 2 + (p + 2))
                pool.dma_start(tokens(y_cat)[:, :, ds(i * (2 * P) + p * P, P)],
                               YS.rearrange("p (t h) n -> p t (h n)", t=TT)).then_inc(w_st, 16)
                if c is not None and more:
                    load_conv(c + 2, range(4))
                store_block(i, 2, 10 + 2 * p, B_IN + 7 + 2 * p,
                            p1[:, :, ds(i * (4 * NB) + (OFF_ZA + (3 + 2 * p) * NB), NB)])
                wait_alone(pool, w_st, i * 32 + (16 * p + 16))

            load_pair(0, 0)
            mix_pair(0, 0)
            pool.wait_ge(mod_row_sb, 1)
            pool.dma_start(mod_gate, GROW[0:1, :]).then_inc(mod_stored, 16)
            for b in range(2):
                store_block(0, 0, 7 + b, B_IN + 4 + b, p1[:, :, OFF_ZA + b * NB:OFF_ZA + (b + 1) * NB])
            pool.wait_ge(stg_out[1], 16 * 4)
            pool.wait_ge(stg_out[0], 16 * 5)
            pool.wait_ge(mod_stored, 16)
            with pool.Fori(0, HP // 4) as i:
                for p in range(2):
                    pair(i, p)
            pool.wait_ge(stg_out[1], 16 * 8)
            pool.wait_ge(stg_out[0], 16 * 9)
            load_conv(0, range(4))
            for j in range(HP // 2, HP):
                pair(j // 2, j % 2, 2 * j - HP)
            pool.wait_ge(w_st, 16 * HP)
            pool.dma_start(YA, tokens(y_cat)[:, :, 0:DA]).then_inc(ya_in, 16)
            pool.wait_ge(stg_out[0], 16 * 13)
            pool.wait_ge(stg_out[1], 16 * 12)
            pool.sem_inc(m_done, 1)
            with pool.Fori(0, 4) as i:
                wait_alone(pool, m_done, i + 1)
                for n in range(2):
                    pool.dma_start(GA[:, n], p1[:, :, ds(i * NB + (OFF_GATE + n * D), NB)]).then_inc(ga_in, 16)
            pool.wait_ge(m_done, 5)
            for n, src in enumerate((mod_gate[0], A["ada_b"][0, 2 * D:3 * D], A["post_gain"][0])):
                pool.dma_start(GB[:, n], rows(src, P)).then_inc(o_bc, 16)
            pool.dma_start(XRES, tokens(A["x"][0])).then_inc(o_bc, 16)

            def add_quarters(stage, rows_b):
                for q in range(2):
                    pool.wait_ge(x_gain, 2 * stage + q + 1)
                    pool.tensor_tensor(quarter(XRES, q), quarter(XRES, q), rows_b(q), ALU.add).then_inc(x_done, 1)
                pool.drain()

            def norm_rows(n, g, b):
                pool.wait_ge(x_done, 2 * n + 2)
                pool.wait_ge(x_own, 2 * n + 2)
                for j, name in enumerate((g, b)):
                    pool.dma_start(NG[:, j], rows(A[name][0], P)).then_inc(n_bc, 16)

            def norm_bias(q):
                return bc(quarter(NG[:, 1], q), TT)

            add_quarters(0, lambda q: quarter(SUM, q))
            pool.wait_ge(x_own, 2)
            pool.tensor_scalar(SUM, XRES, 2.0 * ALPHA, None, ALU.mult).then_inc(ff_zero, 1)
            norm_rows(0, "ln1_g_2", "ln1_b_2")
            add_quarters(1, norm_bias)

            p2 = tokens(proj2[1:T + 1, :])
            pool.wait_ge(tp_lo, G_X2 + 8)
            pool.tensor_scalar(XRES, XRES, ALPHA, None, ALU.mult).then_inc(x_scaled, 1)
            with pool.Fori(0, 2) as i:
                for b in range(2):
                    store_block(i, 1, 25 + b, B_IN2 + b, p2[:, :, ds(i * (2 * NB) + b * NB, NB)])

            def load_input(u):
                if u:
                    pool.wait_ge(hy_z, u)
                off = u % 3 * DA + u // 3 * NB
                pool.dma_start(HW, A["hyena_rows"][:, off:off + NB].partition_broadcast(P)).then_inc(hy_in, 16)
                for s in range(3):
                    pool.dma_start(HL[:, s], tokens(proj2[s:T + s, off:off + NB])).then_inc(hy_in, 16)

            def load_spectrum(u):
                if u:
                    pool.wait_ge(hy_m, u)
                for part in range(2):
                    pool.dma_start(HK[part], filt[u % 2, u // 2].rearrange("p (m n) -> p m n", n=NB)
                                   [:, 2 * part:2 * part + 2, :]).then_inc(hy_kin, 16)

            pool.wait_ge(stg_out[1], 16 * (12 + 2))
            pool.wait_ge(stg_out[0], 16 * (13 + 2))
            load_input(0)
            load_input(1)
            store_block(0, 0, 29, B_HY, p2[:, :, 4 * NB:5 * NB])
            pool.wait_ge(stg_out[1], 16 * (12 + 3))
            load_input(2)
            store_block(0, 0, 30, B_HY + 1, p2[:, :, 5 * NB:6 * NB])
            load_spectrum(0)
            pool.wait_ge(stg_out[0], 16 * (13 + 3))
            for n in range(4):
                pool.dma_start(TAB[:, n], A["dft"][n].rearrange("(t p) f -> p t f", p=P)).then_inc(hy_tab, 16)
            pool.dma_start(HG, rows(A["hyena_norm_g_2"][0], P)).then_inc(hy_tab, 16)
            load_input(3)
            load_spectrum(1)
            load_spectrum(2)
            load_input(4)
            load_input(5)
            load_spectrum(3)
            pool.wait_ge(hy_y, 4)
            pool.dma_start(ROPE, A["rope"].rearrange("a (t p) f -> p a t f", p=P)).then_inc(at_in, 16)
            pool.dma_start(LAM, A["lambdas"].partition_broadcast(P)).then_inc(at_in, 16)
            pool.dma_start(SUBG, rows(A["subln_g_2"][0], P)).then_inc(at_in, 16)
            pool.wait_ge(at_g, 2)
            norm_rows(1, "ln2_g_2", "ln2_b_2")
            add_quarters(2, norm_bias)
            pool.wait_ge(x_own, 6)
            pool.tensor_scalar(SUM, XRES, 2.0 * ALPHA, None, ALU.mult).then_inc(ff_zero, 1)
            norm_rows(2, "ln3_g_2", "ln3_b_2")
            add_quarters(3, norm_bias)
            for st, n in ((f_st, 64), (zero_rows, 64), (mod_stored, 16)):
                pool.wait_ge(st, n)

        @block.scalar
        def _(act):
            act.wait_ge(rows_t, 1)
            act.activation(CACT[:, 16:32], tp(0)[:, 0:16], ACT.Sigmoid).then_inc(c_sig, 1)
            for n in range(3):
                act.wait_ge(f_arg, n + 1)
                act.activation((H1, H2, H1)[n][0:64, :], KST[0:64, 0, 0:T], ACT.Sin).then_inc(f_sin, 1)
            act.wait_ge(x_in, 32)
            for t in range(TT):
                squares = (whi, wlo)[t][:, 2:4, :].rearrange("p a n -> p (a n)")
                act.activation(squares, SUM[:, t, :], ACT.Square, accum_out=MSQ[:, t:t + 1]).then_inc(x_sq, 1)
            for u in range(4):
                act.wait_ge(f_k, u + 1)
                if u:
                    act.wait_ge(f_st, 16 * u)
                act.activation(KST, ps[:, 4:8, :], ACT.Copy).then_inc(f_ke, 1)
            for h in range(3):
                split_hi(act, 0, 0, h)
            for g in range(8):
                act.wait_ge(tp_ready, G_H + g + 1)
                for j in range(2):
                    k = 2 * g + j
                    ins = act.activation(ahi[:, k, :], tp(g % 4)[:, j * T:(j + 1) * T], ACT.Identity,
                                         scale=COEF[:, k:k + 1], bias=COEF[:, 16 + k:17 + k])
                ins.then_inc(tp_hi, 1)

            def stage(i, per, h_end, s, blk, cols=NB):
                act.wait_ge(half_done, i * per + h_end)
                if s >= 2:
                    act.wait_ge(stg_out[s % 2], i * per + 16 * (s // 2))
                act.activation(STG[:, s % 2, :, 0:cols], acc(blk)[:, :, 0:cols], ACT.Copy)\
                   .then_inc(acc_free[blk % 2], 1)

            def split_hi_block(i, per, h):
                for q in range(8):
                    split_hi(act, i, per, h + q + 3)

            split_hi(act, 0, 0, 3)
            split_hi(act, 0, 0, 4)
            stage(0, 0, 2, 0, B_LORA, P)
            for b in range(2):
                split_hi_block(0, 0, H_FIRST + 8 * b)
                stage(0, 0, H_FIRST + 8 * b + 8, 1 + b, B_FIRST + b)
            with act.Fori(0, 2) as i:
                for b in range(2):
                    split_hi_block(i, 16, H_IN + 8 * b)
                    stage(i, 16, H_IN + 8 * b + 8, 3 + b, B_IN + b)
            for b in range(2):
                for q in range(8):
                    split_hi(act, 0, 0, H_IN + 32 + 8 * b + q + 3)
                    if b == 0 and q == 4:
                        act.wait_ge(mod_row, 1)
                        act.activation(GROW[0:1, :].rearrange("p (a n) -> p a n", a=4), ps[0:1, 4:8, :], ACT.Copy)\
                           .then_inc(mod_row_sb, 1)
                    if b and q == 0:
                        act.wait_ge(w_prep, 1)
                        act.activation(LIN[:, 0, :, 0:LORA], LIN[:, 0, :, 0:LORA], ACT.Tanh).then_inc(w_prep, 1)
                    if b and q == 2:
                        act.wait_ge(w_lorat, 1)
                        act.activation(LORAW[0:LORA, :], tp(0)[0:LORA, 0:T], ACT.Copy).then_inc(w_loras, 1)
                        act.activation(LORAA[0:LORA, :], tp(1)[0:LORA, 0:T], ACT.Copy).then_inc(w_loras, 1)
                stage(0, 0, H_IN + 32 + 8 * b + 8, 7 + b, B_IN + 4 + b)
            def gate_conv(i, p, n):
                c = 2 * p + n - HP
                act.wait_ge(cv_in, i * (4 * 144) + (144 * c + 144))
                act.activation(ZBG, ZB, ACT.Sigmoid).then_inc(cv_sig, 1)

            def pair(i, p, conv):
                h0, s0, blk = H_IN + 48 + 16 * p, 9 + 2 * p, B_IN + 6 + 2 * p

                def split(q):
                    split_hi(act, i, 32, h0 + q + 3)

                act.wait_ge(w_z, i * 2 + (p + 1))
                act.activation(SG.rearrange("p a t n -> p (a t n)"), tp(2), ACT.Tanh, scale=0.5)\
                   .then_inc(w_tanh, 1)
                for q in range(5):
                    split(q)
                act.wait_ge(w_cum, i * 2 + (p + 1))
                act.activation(EXPS[:, 0:2].rearrange("p a t n -> p (a t n)"), tp(1), ACT.Exp)
                act.activation(EXPS[:, 2].rearrange("p t n -> p (t n)"), tp(1)[:, 0:T], ACT.Exp, scale=-1.0)
                act.activation(WST[:, 20:24], tp(2)[:, 0:4], ACT.Exp).then_inc(w_exp, 1)
                split(5)
                for t in range(TT):
                    act.wait_ge(w_t4p, i * 4 + (2 * p + t + 1))
                    act.activation(T4[:, t].rearrange("p a n -> p (a n)"), tp(2 + t), ACT.Copy).then_inc(w_t4, 1)
                split(6)
                if conv:
                    gate_conv(i, p, 0)
                split(7)
                for lv in range(5):
                    if lv == 1:
                        stage(i, 32, h0 + 8, s0, blk)
                    act.wait_ge(w_u, i * 10 + (5 * p + lv + 1))
                    act.activation(UU.rearrange("p u n -> p (u n)"), tp(0), ACT.Copy).then_inc(w_ue, 1)
                    split(8 + lv)
                act.wait_ge(w_w1, i * 2 + (p + 1))
                act.activation(W1S.rearrange("p u n -> p (u n)"), tp(0)[:, 0:T], ACT.Copy)
                act.activation(AEF.rearrange("p t n -> p (t n)"), tp(1)[:, 0:T], ACT.Copy).then_inc(w_w1e, 1)
                act.wait_ge(w_za, i * 32 + (16 * p + 16))
                act.activation(ZAG, ZA, ACT.Sigmoid).then_inc(w_zag, 1)
                split(13)
                split(14)
                if conv:
                    gate_conv(i, p, 1)
                split(15)
                act.wait_ge(w_y, i * 2 + (p + 1))
                act.activation(YS.rearrange("p (t h) n -> p t h n", t=TT),
                               ps[:, 4:6, 0:P].rearrange("p h (t n) -> p t h n", t=TT), ACT.Copy)\
                   .then_inc(w_ye, 1)
                stage(i, 32, h0 + 16, s0 + 1, blk + 1)

            with act.Fori(0, HP // 4) as i:
                for p in range(2):
                    pair(i, p, False)
            with act.Fori(0, HP // 4) as i:
                for p in range(HP // 2, HP // 2 + 2):
                    pair(i, p, True)

            for g in range(4):
                take_hi(act, G_Y + g, 8 + 2 * g)

            def gate_columns(i, first):
                for q in range(4):
                    split_hi(act, i, 8, H_PAB + q + 3)
                if first:
                    for g in range(4):
                        take_hi(act, G_Y + 4 + g, 2 * g)
                act.wait_ge(ga_in, i * 32 + 32)
                act.activation(GA, GA, ACT.Sigmoid).then_inc(ga_sig, 1)
                for q in range(4, 8):
                    split_hi(act, i, 8, H_PAB + q + 3)

            gate_columns(0, True)
            with act.Fori(1, 4) as i:
                gate_columns(i, False)
            for g in range(8):
                take_hi(act, G_M + g, 2 * g)

            for n in range(4):
                split_hi_block(0, 0, H_OUT + 8 * n)
                act.wait_ge(half_done, H_OUT + 8 * n + 8)
                for t in range(TT):
                    act.activation(quarter(SRC[:, t], n), acc(B_OUT + n)[:, t], ACT.Square, accum_out=SQ[:, t, n:n + 1])
                ins = act.activation(quarter(SUM, n), acc(B_OUT + n), ACT.Copy).then_inc(acc_free[(B_OUT + n) % 2], 1)
            act.drain().then_inc(o_sq, 1)

            def scale_quarters(stage):
                act.wait_ge(x_stat, stage + 1)
                for q in range(4):
                    for t in range(TT):
                        src = quarter(SUM[:, t], q)
                        if stage == 0:
                            ins = act.activation(src, src, ACT.Copy, scale=RSTD[:, t:t + 1])
                        else:
                            ins = act.activation(quarter(XRES[:, t], q), src, ACT.Identity, scale=RSTD[:, t:t + 1],
                                                 bias=NMR[:, t:t + 1])
                    ins.then_inc(x_norm_act, 1)

            scale_quarters(0)
            for g in range(8):
                take_hi(act, G_X1 + g, 2 * g)

            def hidden_hi(i, g):
                for j in range(2):
                    act.wait_ge(tp_ready, i * 2 + (g + j + 1))
                    act.activation(ghi[:, 2 * j:2 * j + 2, :], tp(j).rearrange("p (k t) -> p k t", k=2), ACT.Copy)\
                       .then_inc(tp_hi, 1)

            def ffn(h0, blk, g0):
                def gate_up(i, per, h, b):
                    split_hi_block(i, per, h)
                    act.wait_ge(half_done, i * per + (h + 8))
                    act.activation(SIG, acc(b), ACT.Sigmoid).then_inc(ff_sig, 1)
                    split_hi_block(i, per, h + 8)

                gate_up(0, 0, h0, blk)
                hidden_hi(0, g0)
                with act.Fori(0, FB - 1) as i:
                    gate_up(i, 24, h0 + 16, blk + 2)
                    split_hi_block(i, 24, h0 + 32)
                    hidden_hi(i, g0 + 2)
                split_hi_block(0, 0, h0 + 24 * FB - 8)

            ffn(H_FFN1, B_FFN1, G_FFN1)
            scale_quarters(1)
            for g in range(8):
                take_hi(act, G_X2 + g, 2 * g)
            with act.Fori(0, 2) as i:
                for b in range(2):
                    split_hi_block(i, 16, H_IN2 + 8 * b)
                    stage(i, 16, H_IN2 + 8 * b + 8, 25 + b, B_IN2 + b)
            for b in range(2):
                split_hi_block(0, 0, H_HY + 8 * b)
                stage(0, 0, H_HY + 8 * b + 8, 29 + b, B_HY + b)
            for b in range(2, 8):
                split_hi_block(0, 0, H_HY + 8 * b)
                act.wait_ge(half_done, H_HY + 8 * b + 8)
                if b >= 6:
                    act.wait_ge(hy_m, 4)
                act.activation((AV, AQ, AK)[b // 2 - 1][:, :, b % 2 * NB:(b % 2 + 1) * NB], acc(B_HY + b), ACT.Copy)\
                   .then_inc(acc_free[(B_HY + b) % 2], 1)
            for g in range(4):
                take_hi(act, G_Y2 + g, 2 * g)

            def splits(m, end):
                for h in range(m, end):
                    split_hi(act, 0, 0, H_OUT2 + h + 3)

            def upper_sum(n):
                act.wait_ge(half_done, H_OUT2 + 4 * n + 4)
                act.activation(SUM[:, :, n * NB:(n + 1) * NB], acc(B_OUT2 + n), ACT.Copy)\
                   .then_inc(acc_free[(B_OUT2 + n) % 2], 1)

            splits(0, 3)
            act.wait_ge(at_lam, 1)
            act.activation(AST[:, 2:4], AST[:, 0:2], ACT.Exp).then_inc(at_le, 1)
            for h in range(8):
                act.wait_ge(at_tp, h + 1)
                act.activation(QT[:, h, :], tp(h % 4)[:, 0:T], ACT.Copy)
                act.activation(KTT[:, h, :], tp(h % 4)[:, T:2 * T], ACT.Copy).then_inc(at_tps, 1)

            def exps(h):
                act.wait_ge(at_max, h + 1)
                if h:
                    act.wait_ge(at_w, h)
                for m in range(2):
                    for t in range(TT):
                        n = 4 * h + 2 * m + t
                        ins = act.activation(EE[:, m, t, :], tp(m)[:, t * T:(t + 1) * T], ACT.Exp,
                                             scale=0.125, bias=AST[:, 8 + n:9 + n],
                                             accum_out=AST[:, 40 + n:41 + n])
                ins.then_inc(at_e, 1)

            splits(3, 4)
            exps(0)
            splits(4, 5)
            upper_sum(0)
            for h in range(8):
                act.wait_ge(at_wt, h + 1)
                act.activation(WT2, tp(2).rearrange("p (k q) -> p k q", k=2), ACT.Copy).then_inc(at_wts, 1)
                if h < 7:
                    exps(h + 1)
                splits(5 + h, 6 + h)
                act.wait_ge(at_o, h + 1)
                act.activation(AO[:, :, h * P:(h + 1) * P], tp(3)[:, 0:T].rearrange("p (t n) -> p t n", t=TT),
                               ACT.Copy).then_inc(at_oe, 1)
                if h % 4 == 3:
                    upper_sum(1 + h // 4)
            splits(13, 16)
            upper_sum(3)
            for g in range(4, 8):
                take_hi(act, G_Y2 + g, 2 * g)
            with act.Fori(0, 2) as i:
                for q in range(8):
                    split_hi(act, i, 8, H_OUT2 + 16 + q + 3)
            scale_quarters(2)
            for g in range(8):
                take_hi(act, G_X3 + g, 2 * g)
            ffn(H_FFN2, B_FFN2, G_FFN2)
            scale_quarters(3)

        @block.tensor
        def _(pe):
            pe.wait_ge(s_const, 16)
            pe.wait_ge(s_rows, 48)
            pe.transpose(tp(0)[:, 0:64], ROWS[0:64, :], ident[0:64, 0:64]).then_inc(rows_t, 1)
            pe.wait_ge(f_in, 9 * 16)
            pe.matmul(tp(1)[0:64, 0:T], FW[0:33, 0, :], ZT[0:33, :], start=True, stop=True).then_inc(f_mlp, 1)
            for n, src in ((1, H1), (2, H2)):
                pe.wait_ge(f_sin, n)
                pe.matmul(tp(1)[0:64, 0:T], FW[0:64, n, :], src[0:64, :], start=True, stop=True).then_inc(f_mlp, 1)
            pe.wait_ge(f_sin, 3)
            pe.wait_ge(c_act, 1)

            def filters(u):
                cb, n = u // 2, u % 2
                if u:
                    pe.wait_ge(f_sd0, u)
                for d in range(2):
                    for t in range(TT):
                        col = n * 2 * DA + d * DA + cb * NB
                        mm = pe.matmul(ps[:, 2 * d + t, :], H1[0:64, t * P:(t + 1) * P], WOF[0:64, col:col + NB],
                                       start=True, stop=True)
                mm.then_inc(f_h, 1)

            def sums(first, end):
                pe.wait_ge(ada_done, end)
                for j in range(first, end):
                    mm = pe.matmul(ps[:, 0, j:j + 1], ADA[:, j * P:(j + 1) * P], ones[:, 0:1], start=True, stop=True)
                mm.then_inc(mod_cols, 1)

            filters(0)
            for u in range(4):
                if u < 3:
                    filters(u + 1)
                else:
                    pe.wait_ge(s_ones, 1)
                    pe.wait_ge(f_sd0, 4)
                    sums(0, 16)
                pe.wait_ge(f_sd, 2 * u + 2)
                if u:
                    pe.wait_ge(f_ke, u)
                for part, tab in enumerate((FC, FS)):
                    for m in range(2):
                        for t in range(TT):
                            mm = pe.matmul(tp(2 * part + m), tab[:, t, m * P:(m + 1) * P], SD[:, part, t, :],
                                           start=t == 0, stop=t == 1)
                mm.then_inc(f_k, 1)
            sums(16, 32)
            pe.wait_ge(f_ke, 4)
            pe.wait_ge(x_norm, 2)
            for g in range(8):
                transpose_group(pe, G_H + g, SRC, 2 * g)
            pe.wait_ge(tp_lo, G_H + 4)
            pe.wait_ge(mod_scale, 1)
            products(pe, 0, 0, 0, ahi[:, 0:8, :], alo[:, 0:8, :], acc(B_LORA), True, False, P)
            pe.wait_ge(tp_lo, G_H + 8)
            products(pe, 0, 0, 1, ahi[:, 8:16, :], alo[:, 8:16, :], acc(B_LORA), False, True, P)
            for b in range(2):
                block_2048(pe, 0, 0, H_FIRST + 8 * b, 0, B_FIRST + b)
            with pe.Fori(0, 2) as i:
                for b in range(2):
                    block_2048(pe, i, 16, H_IN + 8 * b, 2, B_IN + b)
            for b in range(2):
                pe.wait_ge(acc_free[(B_IN + b) % 2], (B_IN + 4 + b) // 2)
                for q in range(8):
                    products(pe, 0, 0, H_IN + 32 + 8 * b + q, ahi[:, 2 * q:2 * q + 2, :], alo[:, 2 * q:2 * q + 2, :],
                             acc(B_IN + b), q == 0, q == 7)
                    if b == 0 and q == 3:
                        pe.wait_ge(gate_done, 16)
                        for n in range(4):
                            mm = pe.matmul(ps[0:1, 4 + n, :], ones[:, 0:1], ADAG[:, n * NB:(n + 1) * NB],
                                           start=True, stop=True)
                        mm.then_inc(mod_row, 1)
                    if b and q == 1:
                        pe.wait_ge(mod_row_sb, 1)
                        pe.wait_ge(w_prep, 2)
                        for t in range(TT):
                            pe.transpose(tp(0)[0:LORA, t * P:(t + 1) * P], LIN[:, 0, t, 0:LORA], ident[:, :])
                            mm = pe.transpose(tp(1)[0:LORA, t * P:(t + 1) * P], LIN[:, 0, t, LORA:P], ident[:, :])
                        mm.then_inc(w_lorat, 1)
            pe.wait_ge(w_loras, 3)
            pe.wait_ge(w_kin, 16)
            with pe.Fori(0, HP // 2) as i:
                for p in range(2):
                    h0, blk, V = H_IN + 48 + 16 * p, B_IN + 6 + 2 * p, CUR[p][:, :, 2, :]

                    def part(n):
                        q, b = n // 2 % 8, n // 16
                        if n % 16 == 0:
                            pe.wait_ge(acc_free[(blk + b) % 2], i * 2 + (blk + b) // 2)
                        products(pe, i, 32, h0 + n // 2, ahi[:, 2 * q:2 * q + 2, :], alo[:, 2 * q:2 * q + 2, :],
                                 acc(blk + b), q == 0, q == 7, part=n % 2)

                    def parts(n, end):
                        for m in range(n, end):
                            part(m)

                    pe.wait_ge(w_in_s[p], i * 96 + 96)
                    for a, lora in enumerate((LORAW, LORAA)):
                        for t in range(TT):
                            mm = pe.matmul(tp(2)[:, (2 * a + t) * P:(2 * a + t + 1) * P],
                                           lora[0:LORA + 1, t * P:(t + 1) * P], WA[p][0:LORA + 1, a, :],
                                           start=True, stop=True)
                    mm.then_inc(w_z, 1)
                    parts(0, 9)
                    pe.wait_ge(w_ld, i * 2 + (p + 1))
                    for t in range(TT):
                        pe.matmul(tp(1)[:, t * P:(t + 1) * P], MASKS[:, 1, :], LD[:, t, :], start=True, stop=True)
                        pe.matmul(tp(1)[:, T + t * P:T + (t + 1) * P], MASKS[:, 0, :], LD[:, t, :],
                                  start=True, stop=True)
                        mm = pe.matmul(tp(2)[:, 2 * t:2 * t + 2], LD[:, t, :], MASKS[:, 12, 0:2], start=True, stop=True)
                    mm.then_inc(w_cum, 1)
                    parts(9, 12)
                    pe.wait_ge(w_tok, i * 2 + (p + 1))
                    for t in range(TT):
                        for n in range(4):
                            mm = pe.transpose(tp(2 + t)[:, n * P:(n + 1) * P], TOK[:, t, n, :], ident[:, :])
                        mm.then_inc(w_t4p, 1)
                    part(12)
                    for t in range(TT):
                        pe.wait_ge(w_t4, i * 4 + (2 * p + 2))
                        if t:
                            pe.wait_ge(w_mask, i * 4 + (2 * p + t))
                        for h in range(2):
                            hs = slice(64 * h, 64 * h + 64)
                            ar = T4[hs, t, 0:2, :].rearrange("p a n -> p (a n)")
                            pe.matmul(tp(h)[:, 0:T], T4[hs, t, 2, :], ar, start=True, stop=True)
                            pe.matmul(tp(h)[:, T:2 * T], T4[hs, t, 3, :], ar, start=True, stop=True)
                            mm = pe.matmul(tp(2 + h)[:, t * P:(t + 1) * P],
                                           T4[hs, t, 0, :], T4[hs, t, 2, :], start=True, stop=True)
                        mm.then_inc(w_gram, 1)
                        part(13 + t)
                    part(15)
                    pe.wait_ge(w_t0, i * 2 + (p + 1))
                    for lv in range(5):
                        if lv:
                            pe.wait_ge(w_tn, i * 10 + (5 * p + lv))
                        pe.wait_ge(w_ms, i * 10 + (5 * p + lv + 1))
                        for u in range(4):
                            mm = pe.matmul(tp(0)[:, u * P:(u + 1) * P], MS[:, u, :], TM[:, u, :], start=True, stop=True)
                        mm.then_inc(w_u, 1)
                        part(16 + 2 * lv)
                        pe.wait_ge(w_ue, i * 10 + (5 * p + lv + 1))
                        for u in range(4):
                            if lv < 4:
                                pe.matmul(level(tp(1)[:, u * 64:(u + 1) * 64], lv, 1)[:, :, 0, :], TMT[:, u, :],
                                          level(UU[:, u, :], lv)[:, :, 0, :], start=True, stop=True)
                            mm = pe.matmul(level(tp(2)[:, u * 64:(u + 1) * 64], lv, 1)[:, :, 0, :], UU[:, u, :],
                                           level(TMT[:, u, :], lv)[:, :, 1, :], start=True, stop=True)
                        mm.then_inc(w_dt, 1)
                        part(17 + 2 * lv)
                    pe.wait_ge(w_tn, i * 10 + (5 * p + 5))
                    for t in range(TT):
                        for h in range(2):
                            u = 2 * t + h
                            hs = slice(64 * h, 64 * h + 64)
                            pe.matmul(tp(0)[:, u * 64:(u + 1) * 64], GR[:, u, 2, :], V[:, t, hs], start=True, stop=True)
                            mm = pe.matmul(tp(1)[hs, t * P:(t + 1) * P], TOK[:, t, 0, hs], TMT[:, u, :],
                                           start=True, stop=True)
                    mm.then_inc(w_w1, 1)
                    part(26)
                    pe.wait_ge(w_w1e, i * 2 + (p + 1))
                    for u in range(4):
                        mm = pe.matmul(tp(2)[:, u * 64:(u + 1) * 64], TMT[:, u, :], W1S[:, u, :], start=True, stop=True)
                    mm.then_inc(w_sa0, 1)
                    part(27)
                    for c in range(NCH):
                        t, rs = c // 2, slice(CH * (c % 2), CH * (c % 2) + CH)
                        cs = slice(CH * (c % 2), CH * (c % 2) + CH)
                        if c:
                            wait_alone(pe, w_state, i * 6 + (3 * p + c))
                            for h in range(2):
                                hs = slice(64 * h, 64 * h + 64)
                                mm = pe.matmul(tp(h)[rs, 0:64], AEF[hs, t, cs], ST[hs, c, :], start=True, stop=True)
                            mm.then_inc(w_sap, 1)
                            if c < 3:
                                part(27 + 2 * c)
                        if c == NCH - 1:
                            break
                        wait_alone(pe, w_sae, i * 8 + (4 * p + c + 1))
                        for h in range(2):
                            hs = slice(64 * h, 64 * h + 64)
                            pe.matmul(tp(3)[hs, c * 64:(c + 1) * 64], TOK[rs, t, 2, hs], SA[rs, 2 * t + h, :],
                                      start=True, stop=False)
                            mm = pe.matmul(tp(3)[hs, c * 64:(c + 1) * 64], TOK[rs, t, 3, hs], V[rs, t, hs],
                                           start=False, stop=True)
                        mm.then_inc(w_delta, 1)
                        if c < 2:
                            part(28 + 2 * c)
                    wait_alone(pe, w_sae, i * 8 + (4 * p + NCH))
                    for t in range(TT):
                        for h in range(2):
                            u = 2 * t + h
                            hs = slice(64 * h, 64 * h + 64)
                            dst = tp(h)[:, t * 64:(t + 1) * 64]
                            pe.matmul(dst, GR[:, u, 1, :], SA[:, u, :], start=True, stop=False)
                            pe.matmul(dst, GR[:, u, 3, :], V[:, t, hs], start=False, stop=False)
                            for c in (2 * t, 2 * t + 1):
                                rs = slice(CH * (c % 2), CH * (c % 2) + CH)
                                mm = pe.matmul(tp(h)[rs, t * 64:(t + 1) * 64], T4[hs, t, 1, rs], ST[hs, c, :],
                                               start=False, stop=True)
                    mm.then_inc(w_y, 1)
            def transpose_residual(stage, n):
                for g in range(8):
                    if g % 2 == 0:
                        pe.wait_ge((x_done, x_own)[g // 4], 2 * stage + g // 2 % 2 + 1)
                    transpose_group(pe, n + g, XRES, 2 * g)

            pe.wait_ge(yb_in, 16)
            pe.wait_ge(w_ye, HP)
            for g in range(4):
                transpose_group(pe, G_Y + g, YB, 2 * g)
            pe.wait_ge(tp_lo, G_Y + 4)

            def branch(i, n):
                blk = B_PAB + n
                pe.wait_ge(acc_free[blk % 2], i + blk // 2)
                for q in range(4):
                    k = 8 * (1 - n) + 2 * q
                    products(pe, i, 8, H_PAB + 4 * n + q, ahi[:, k:k + 2, :], alo[:, k:k + 2, :], acc(blk),
                             q == 0, q == 3)

            branch(0, 0)
            pe.wait_ge(ya_in, 16)
            for g in range(4):
                transpose_group(pe, G_Y + 4 + g, YA, 2 * g)
            pe.wait_ge(tp_lo, G_Y + 8)
            branch(0, 1)
            with pe.Fori(1, 4) as i:
                for n in range(2):
                    branch(i, n)
            pe.wait_ge(m_done, 5)
            for g in range(8):
                transpose_group(pe, G_M + g, SRC, 2 * g)
            pe.wait_ge(tp_lo, G_M + 8)
            with pe.Fori(0, 2) as i:
                for b in range(2):
                    block_2048(pe, i, 16, H_OUT + 8 * b, 2, B_OUT + b)
            transpose_residual(0, G_X1)

            def ffn(h0, blk, g0):
                def hidden(i, g, up):
                    pe.wait_ge(acc_free[up % 2], i * 3 + (up // 2 + 1))
                    pe.wait_ge(tp_lo, i * 2 + g)
                    for j in range(2):
                        for k in range(2):
                            for t in range(TT):
                                col = (2 * j + k) * P
                                mm = pe.transpose(tp(j)[:, k * T + t * P:k * T + (t + 1) * P],
                                                  HID[:, t, col:col + P], ident[:, :])
                        mm.then_inc(tp_ready, 1)

                def down(i, per, h, blk_per, b, g):
                    pe.wait_ge(tp_lo, i * 2 + g)
                    for n in range(4):
                        pe.wait_ge(acc_free[(b + n) % 2], i * (blk_per // 2) + (b + n) // 2)
                        for q in range(2):
                            products(pe, i, per, h + 2 * n + q, ghi[:, 2 * q:2 * q + 2, :], glo[:, 2 * q:2 * q + 2, :],
                                     acc(b + n), q == 0, q == 1)

                block_2048(pe, 0, 0, h0, 0, blk, g0 - 8)
                block_2048(pe, 0, 0, h0 + 8, 0, blk + 1)
                hidden(0, g0, blk + 1)
                with pe.Fori(0, FB - 1) as i:
                    block_2048(pe, i, 24, h0 + 16, 6, blk + 2)
                    block_2048(pe, i, 24, h0 + 24, 6, blk + 3)
                    down(i, 24, h0 + 32, 6, blk + 4, g0 + 2)
                    hidden(i, g0 + 2, blk + 3)
                down(0, 0, h0 + 24 * FB - 8, 0, blk + 6 * FB - 4, g0 + 2 * FB)

            ffn(H_FFN1, B_FFN1, G_FFN1)
            transpose_residual(1, G_X2)
            pe.wait_ge(tp_lo, G_X2 + 8)
            with pe.Fori(0, 2) as i:
                for b in range(2):
                    block_2048(pe, i, 16, H_IN2 + 8 * b, 2, B_IN2 + b)

            def halves(n, end):
                for m in range(n, end):
                    blk, q = B_HY + m // 8, m % 8
                    if q == 0:
                        pe.wait_ge(acc_free[blk % 2], blk // 2)
                    products(pe, 0, 0, H_HY + m, ahi[:, 2 * q:2 * q + 2, :], alo[:, 2 * q:2 * q + 2, :],
                             acc(blk), q == 0, q == 7)

            halves(0, HY_UNITS[0])
            pe.wait_ge(hy_tab, 80)
            for u in range(4):
                if u % 2 == 0:
                    pe.wait_ge(hy_z, 3 * (u // 2) + 3)
                else:
                    pe.wait_ge(hy_y, u)
                for part in range(2):
                    for m in range(2):
                        for t in range(TT):
                            mm = pe.matmul(tp(2 * part + m), TAB[:, part, t, m * P:(m + 1) * P], HZ[:, 0, t, :],
                                           start=t == 0, stop=t == 1)
                mm.then_inc(hy_f, 1)
                m0 = HY_UNITS[u]
                halves(m0, m0 + 3)
                pe.wait_ge(hy_m, u + 1)
                for t in range(TT):
                    for part in range(2):
                        for m in range(2):
                            mm = pe.matmul(tp(t), TAB[:, 2 + part, m, t * P:(t + 1) * P],
                                           HY_[:, 2 * part + m, :], start=part == 0 and m == 0,
                                           stop=part == 1 and m == 1)
                mm.then_inc(hy_i, 1)
                halves(m0 + 3, HY_UNITS[u + 1] if u < 3 else 64)

            pe.wait_ge(hy_g, 2)
            for g in range(4):
                transpose_group(pe, G_Y2 + g, SRC, 2 * g)
            pe.wait_ge(tp_lo, G_Y2 + 4)

            def upper(n, end):
                for m in range(n, end):
                    blk, q = B_OUT2 + m // 4, m % 4
                    if q == 0:
                        pe.wait_ge(acc_free[blk % 2], blk // 2)
                    products(pe, 0, 0, H_OUT2 + m, ahi[:, 2 * q:2 * q + 2, :], alo[:, 2 * q:2 * q + 2, :],
                             acc(blk), q == 0, q == 3)

            upper(0, 3)
            pe.wait_ge(at_rope, 2)
            for h in range(8):
                if h >= 4:
                    pe.wait_ge(at_tps, h - 3)
                for n, src in enumerate((AQ, AK)):
                    for t in range(TT):
                        mm = pe.transpose(tp(h % 4)[:, n * T + t * P:n * T + (t + 1) * P],
                                          src[:, t, h * P:(h + 1) * P], ident[:, :])
                mm.then_inc(at_tp, 1)
            pe.wait_ge(at_tps, 8)

            def scores(h):
                if h:
                    pe.wait_ge(at_e, h)
                for m in range(2):
                    rs = slice(64 * m, 64 * m + 64)
                    for t in range(TT):
                        mm = pe.matmul(tp(m)[:, t * T:(t + 1) * T], QT[rs, h, t * P:(t + 1) * P],
                                       KTT[rs, h, :], start=True, stop=True)
                mm.then_inc(at_s, 1)

            scores(0)
            upper(3, 4)
            for h in range(8):
                pe.wait_ge(at_w, h + 1)
                for k in range(2):
                    for t in range(TT):
                        mm = pe.transpose(tp(2)[:, k * T + t * P:k * T + (t + 1) * P],
                                          WW[:, t, k * P:(k + 1) * P], ident[:, :])
                mm.then_inc(at_wt, 1)
                if h < 7:
                    scores(h + 1)
                upper(4 + h, 5 + h)
                pe.wait_ge(at_wts, h + 1)
                if h:
                    pe.wait_ge(at_oe, h)
                for t in range(TT):
                    for k in range(2):
                        mm = pe.matmul(tp(3)[:, t * P:(t + 1) * P], WT2[:, k, t * P:(t + 1) * P],
                                       AV[:, k, h * P:(h + 1) * P], start=k == 0, stop=k == 1)
                mm.then_inc(at_o, 1)
            upper(12, 16)
            pe.wait_ge(at_g, 2)
            for g in range(4, 8):
                transpose_group(pe, G_Y2 + g, SRC, 2 * g)
            pe.wait_ge(tp_lo, G_Y2 + 8)
            with pe.Fori(0, 2) as i:
                for b in range(2):
                    blk = B_OUT2 + 4 + b
                    pe.wait_ge(acc_free[blk % 2], i + blk // 2)
                    for q in range(4):
                        products(pe, i, 8, H_OUT2 + 16 + 4 * b + q, ahi[:, 8 + 2 * q:10 + 2 * q, :],
                                 alo[:, 8 + 2 * q:10 + 2 * q, :], acc(blk), q == 0, q == 3)
            transpose_residual(2, G_X3)
            ffn(H_FFN2, B_FFN2, G_FFN2)

        @block.vector
        def _(dve):
            def bcl(ap, n):
                return ap.unsqueeze(2).to_broadcast([ap.shape[0], ap.shape[1], n])

            def rsqrt(dst, src, tmp):
                dve.tensor_scalar(tmp.bitcast(mybir.dt.int32), src.bitcast(mybir.dt.int32), 1, None,
                                  ALU.logical_shift_right)
                dve.drain()
                dve.tensor_scalar(dst.bitcast(mybir.dt.int32), tmp.bitcast(mybir.dt.int32), -1.0, 1597463007.0,
                                  ALU.mult, ALU.add)
                dve.drain()
                for _ in range(3):
                    dve.scalar_tensor_tensor(tmp, dst, -0.5, dst, ALU.mult, ALU.mult)
                    dve.drain()
                    dve.tensor_tensor(tmp, tmp, src, ALU.mult)
                    dve.drain()
                    dve.scalar_tensor_tensor(dst, tmp, 1.5, dst, ALU.add, ALU.mult)
                    dve.drain()

            dve.wait_ge(rows_t, 1)
            dve.wait_ge(c_sig, 1)
            dve.tensor_copy(COLS[:, 0:64], tp(0)[:, 0:64])
            dve.drain()
            dve.tensor_tensor(CACT[:, 0:16], COLS[:, 0:16], CACT[:, 16:32], ALU.mult).then_inc(c_act, 1)
            dve.drain()

            def ada(n):
                k, part = n % 16, ADA[:, n // 16 * D:(n // 16 + 1) * D]
                dve.wait_ge(ada_in[n % 4], 16 * (n // 4 + 1))
                if k == 0:
                    dve.tensor_scalar(part, raw[:, n % 4, :], CACT[:, 0:1], None, ALU.mult).then_inc(ada_done, 1)
                else:
                    dve.scalar_tensor_tensor(part, raw[:, n % 4, :], CACT[:, k:k + 1], part, ALU.mult, ALU.add)\
                       .then_inc(ada_done, 1)
                dve.drain()

            def sine_argument(n):
                arg, turns = KST[0:64, 0, 0:T], KST[0:64, 1, 0:T]
                dve.wait_ge(f_mlp, n + 1)
                if n == 0:
                    dve.wait_ge(f_in, 9 * 16)
                dve.tensor_scalar(arg, tp(1)[0:64, 0:T], FCOL[0:64, n:n + 1], FCOL[0:64, 3:4], ALU.add, ALU.mult)
                dve.drain()
                dve.tensor_scalar(turns, arg, 1.0 / (2.0 * math.pi), ROUND, ALU.mult, ALU.add)
                dve.drain()
                dve.tensor_scalar(turns, turns, ROUND, None, ALU.subtract)
                dve.drain()
                for part in (TWO_PI_HI, TWO_PI_LO):
                    dve.scalar_tensor_tensor(arg, turns, -part, arg, ALU.mult, ALU.add)
                    dve.drain()
                dve.tensor_scalar(arg, arg, PI_IN, -PI_IN, ALU.min, ALU.max).then_inc(f_arg, 1)

            def filter_unit(u):
                cb, n = u // 2, u % 2
                if u:
                    dve.wait_ge(f_sd, 2 * u)
                dve.wait_ge(f_h, u + 1)
                dve.wait_ge(f_dec, 32 * (cb + 1))
                dve.tensor_tensor(HFB, ps[:, 0:4, :].rearrange("p (d t) n -> p d t n", d=2), DEC, ALU.mult)\
                   .then_inc(f_sd0, 1)
                dve.drain()
                row = HFB[0:1, 0, 0, :]
                dve.tensor_tensor(row, row, BROW[0:1, n, cb * NB:(cb + 1) * NB], ALU.add).then_inc(f_hb, 1)

            def x_statistics():
                dve.wait_ge(x_sq, 2)
                dve.tensor_scalar(MSQ, MSQ, 1.0 / D, RMS_EPS, ALU.mult, ALU.add)
                dve.drain()
                rsqrt(RSTD, MSQ, RTMP)

            def gate_tile(k):
                dve.wait_ge(gate_w_in[k % 2], 16 * (k // 2 + 1))
                if k == 0:
                    dve.tensor_scalar(ADAG, GW[0], CACT[:, 0:1], None, ALU.mult).then_inc(gate_done, 1)
                else:
                    dve.scalar_tensor_tensor(ADAG, GW[k % 2], CACT[:, k:k + 1], ADAG, ALU.mult, ALU.add)\
                       .then_inc(gate_done, 1)
                dve.drain()

            for n in range(32):
                ada(n)
                if n in (2, 5, 8):
                    sine_argument((n - 2) // 3)
                if n in FILTERS_AFTER:
                    filter_unit(FILTERS_AFTER.index(n))
                if n == 26:
                    x_statistics()
            dve.wait_ge(mod_cols, 2)
            dve.tensor_tensor(MODC, ps[:, 0, 0:32], COLS[:, 32:64], ALU.add)
            dve.drain()
            dve.scalar_tensor_tensor(COEF[:, 0:16], MODC[:, 16:32], 1.0, COLS[:, 16:32], ALU.add, ALU.mult)
            dve.tensor_copy(COEF[:, 16:32], MODC[:, 0:16]).then_inc(mod_scale, 1)
            for t in range(TT):
                dve.tensor_scalar(SRC[:, t, :], SUM[:, t, :], RSTD[:, t:t + 1], None, ALU.mult).then_inc(x_norm, 1)
            for h in range(2):
                split_lo(dve, 0, 0, h)
            for g in range(8):
                dve.wait_ge(tp_hi, G_H + g + 1)
                for j in range(2):
                    k = 2 * g + j
                    dve.tensor_scalar(HTMP[:, j, :], tp(g % 4)[:, j * T:(j + 1) * T], COEF[:, k:k + 1],
                                      COEF[:, 16 + k:17 + k], ALU.mult, ALU.add)
                dve.drain()
                dve.tensor_tensor(alo[:, 2 * g:2 * g + 2, :], HTMP, ahi[:, 2 * g:2 * g + 2, :].bitcast(F32),
                                  ALU.subtract).then_inc(tp_lo, 1)
                dve.drain()

            def split_lo_block(i, per, h):
                for q in range(8):
                    split_lo(dve, i, per, h + q + 2)

            split_lo(dve, 0, 0, 2)
            split_lo(dve, 0, 0, 3)
            for b in range(6):
                for q in range(8):
                    split_lo(dve, 0, 0, H_FIRST + 8 * b + q + 2)
                    if q in GATE_AFTER[b]:
                        gate_tile(GATE_TILES[b][GATE_AFTER[b].index(q)])
            split_lo_block(0, 0, H_IN + 32)
            split_lo(dve, 0, 0, H_IN + 42)
            dve.wait_ge(w_lora, 48)
            dve.tensor_tensor(LIN[:, 1], LIN[:, 1], LIN[:, 0], ALU.subtract)
            dve.memset(ST[:, 0, :], 0.0)
            dve.memset(LORAW[LORA:LORA + 1, :], 1.0)
            dve.memset(LORAA[LORA:LORA + 1, :], 1.0).then_inc(w_loras, 1)
            dve.drain()
            dve.tensor_tensor(LIN[:, 1], LIN[:, 1], bc(MUL, TT), ALU.mult)
            dve.drain()
            dve.tensor_tensor(LIN[:, 0], LIN[:, 0], LIN[:, 1], ALU.add).then_inc(w_prep, 1)
            for q in range(11, 21):
                split_lo(dve, 0, 0, H_IN + 32 + q)

            def heads(ap):
                return ap.rearrange("p t (h n) -> p t h n", h=2)

            def per_head(ap):
                return ap.rearrange("p (t h) -> p t h", t=TT).unsqueeze(3).to_broadcast([P, TT, 2, 64])

            def th(ap):
                return ap.rearrange("p (t h) -> p t h", t=TT)

            dve.wait_ge(w_kin, 16)
            def norm_keys(i, p):
                dve.wait_ge(w_mix, i * 2 + (p + 1))
                dve.tensor_tensor(KK, CUR[p % 2][:, :, 1, :], bc(PRM[p % 2][:, 3, :], TT), ALU.mult)
                dve.drain()
                dve.tensor_tensor(RK, KK, KK, ALU.mult)
                dve.drain()
                dve.tensor_reduce(th(WST[:, 0:4]), heads(RK), AX.X, ALU.add)
                dve.drain()
                dve.tensor_scalar(WST[:, 0:4], WST[:, 0:4], 1e-24, None, ALU.max)
                dve.drain()
                rsqrt(WST[:, 4:8], WST[:, 0:4], small[:, 64:68])

            def pair(i, p, more):
                h0 = H_IN + 48 + 16 * p
                R, K, V = (CUR[p][:, :, n, :] for n in range(3))
                prm = PRM[p]

                def split(q):
                    split_lo(dve, i, 32, h0 + q + 2)

                dve.wait_ge(w_tanh, i * 2 + (p + 1))
                sg = SG.rearrange("p a t n -> p (a t n)")
                dve.tensor_scalar(sg, sg, 0.5, 0.5, ALU.mult, ALU.add)
                dve.drain()
                dve.tensor_scalar(LD, SG[:, 0], -math.exp(-0.5), None, ALU.mult).then_inc(w_ld, 1)
                split(3)
                dve.scalar_tensor_tensor(K2, SG[:, 1], -1.0, bc(prm[:, 4, :], TT), ALU.add, ALU.mult)
                dve.drain()
                dve.scalar_tensor_tensor(K2, K2, 1.0, K, ALU.add, ALU.mult)
                dve.drain()
                dve.tensor_tensor(RK, R, K2, ALU.mult)
                dve.drain()
                dve.tensor_tensor(RK, RK, bc(prm[:, 5, :], TT), ALU.mult)
                dve.drain()
                dve.tensor_reduce(th(WST[:, 8:12]), heads(RK), AX.X, ALU.add)
                dve.drain()
                dve.tensor_tensor(heads(BV), heads(V), per_head(WST[:, 8:12]), ALU.mult)
                dve.tensor_tensor(heads(KK), heads(KK), per_head(WST[:, 4:8]), ALU.mult)
                dve.drain()
                dve.tensor_tensor(BB, KK, SG[:, 1], ALU.mult)
                dve.drain()
                split(4)
                dve.wait_ge(w_exp, i * 2 + (p + 1))
                dve.scalar_tensor_tensor(TOK[:, :, 0, :], KK, -1.0, EXPS[:, 1], ALU.mult, ALU.mult)
                dve.tensor_tensor(TOK[:, :, 1, :], R, EXPS[:, 0], ALU.mult)
                dve.tensor_tensor(TOK[:, :, 2, :], BB, EXPS[:, 2], ALU.mult)
                dve.tensor_tensor(TOK[:, :, 3, :], K2, EXPS[:, 2], ALU.mult).then_inc(w_tok, 1)
                split(5)
                split(6)
                for t in range(TT):
                    dve.wait_ge(w_gram, i * 4 + (2 * p + t + 1))
                    dve.tensor_tensor(GR[:, 2 * t:2 * t + 2].rearrange("p u g n -> p u (g n)"), ps[:, 4:6, :],
                                      bc(MASKS[:, 0:4, :].rearrange("p g n -> p (g n)"), 2), ALU.mult)
                    dve.tensor_tensor(MM[:, 2 * t:2 * t + 2, :], ps[:, 6:8, t * P:(t + 1) * P], bc(MASKS[:, 4, :], 2),
                                      ALU.mult).then_inc(w_mask, 1)
                    split(7 + t)
                dve.drain()
                dve.tensor_tensor(TM, MM, bc(MASKS[:, 10, :], 4), ALU.mult)
                dve.tensor_tensor(TMT, GR[:, :, 0, :], bc(MASKS[:, 11, :], 4), ALU.mult)
                dve.drain()
                dve.tensor_tensor(TM, TM, bc(ident[:, :], 4), ALU.add)
                dve.tensor_tensor(TMT, TMT, bc(ident[:, :], 4), ALU.add).then_inc(w_t0, 1)
                for lv in range(5):
                    dve.wait_ge(w_dt, i * 10 + (5 * p + lv + 1))
                    tm, tmt = (level(m.rearrange("p u n -> p (u n)"), lv) for m in (TM, TMT))
                    if lv < 4:
                        left = tm[:, :, 0, :]
                        dve.tensor_tensor(left, left, level(tp(1)[:, 0:T], lv, 1)[:, :, 0, :], ALU.add)
                    right = tmt[:, :, 1, :]
                    dve.tensor_tensor(right, right, level(tp(2)[:, 0:T], lv, 1)[:, :, 0, :], ALU.add)\
                       .then_inc(w_tn, 1)
                    split(9 + lv)
                dve.wait_ge(w_sa0, i * 2 + (p + 1))
                dve.tensor_copy(SA, tp(2)[:, 0:T].rearrange("p (u n) -> p u n", u=4)).then_inc(w_sae, 1)
                for c in range(NCH - 1):
                    decay = WST[:, 20 + c:21 + c]
                    if c:
                        dve.tensor_scalar(SPC, ST[:, c, :], decay, None, ALU.mult)
                        dve.drain()
                    dve.wait_ge(w_delta, i * 6 + (3 * p + c + 1))
                    delta = tp(3)[:, c * 64:(c + 1) * 64]
                    if c:
                        dve.scalar_tensor_tensor(ST[:, c + 1, :], delta, decay, SPC, ALU.mult, ALU.add)\
                           .then_inc(w_state, 1)
                    else:
                        dve.tensor_scalar(ST[:, 1, :], delta, decay, None, ALU.mult).then_inc(w_state, 1)
                    t, rs = (c + 1) // 2, slice(CH * ((c + 1) % 2), CH * ((c + 1) % 2) + CH)
                    dve.wait_ge(w_sap, i * 6 + (3 * p + c + 1))
                    dve.tensor_tensor(SA[rs, 2 * t:2 * t + 2, :], SA[rs, 2 * t:2 * t + 2, :], ps[rs, 4:6, 0:64],
                                      ALU.add).then_inc(w_sae, 1)
                    if c < 2:
                        split(14 + c)
                split(16)
                if more:
                    norm_keys(i, p + 1)
                else:
                    split(17)
                    for g in range(4):
                        take_lo(dve, G_Y + g, 8 + 2 * g)
                dve.wait_ge(w_ye, i * 2 + (p + 1))
                dve.tensor_reduce(WST[:, 24:28], YS, AX.X, ALU.add)
                dve.drain()
                dve.tensor_scalar(WST[:, 24:28], WST[:, 24:28], -1.0 / 64, None, ALU.mult)
                dve.drain()
                dve.tensor_tensor(YS, YS, bcl(WST[:, 24:28], 64), ALU.add)
                dve.drain()
                dve.tensor_tensor(YQ, YS, YS, ALU.mult)
                dve.drain()
                dve.tensor_reduce(WST[:, 28:32], YQ, AX.X, ALU.add)
                dve.drain()
                dve.tensor_scalar(WST[:, 12:16], WST[:, 28:32], 1.0 / 64, GN_EPS, ALU.mult, ALU.add)
                dve.drain()
                if more:
                    split(17)
                rsqrt(WST[:, 16:20], WST[:, 12:16], small[:, 68:72])
                if more:
                    split(18)
                dve.tensor_tensor(YS, YS, bcl(WST[:, 16:20], 64), ALU.mult)
                dve.drain()
                ys = YS.rearrange("p (t h) n -> p t (h n)", t=TT)
                dve.tensor_tensor(ys, ys, bc(prm[:, 6, :], TT), ALU.mult)
                dve.drain()
                dve.tensor_tensor(ys, ys, bc(prm[:, 7, :], TT), ALU.add)
                dve.drain()
                dve.tensor_tensor(ys, ys, BV, ALU.add)
                dve.drain()
                dve.wait_ge(w_zag, i * 2 + (p + 1))
                dve.tensor_tensor(ys, ys, ZA, ALU.mult)
                dve.drain()
                dve.tensor_tensor(ys, ys, ZAG, ALU.mult).then_inc(w_yo, 1)

            norm_keys(0, 0)
            with dve.Fori(0, HP // 2 - 1) as i:
                for p in range(2):
                    pair(i, p, True)
            for p in range(2):
                pair(HP // 2 - 1, p, p == 0)

            def gated(i, first):
                for q in range(2 if first else 0, 4):
                    split_lo(dve, i, 8, H_PAB + q + 2)
                if first:
                    for g in range(4):
                        take_lo(dve, G_Y + 4 + g, 2 * g)
                dve.wait_ge(half_done, i * 8 + (H_PAB + 4))
                dve.wait_ge(ga_sig, i + 1)
                dve.tensor_tensor(MT, acc(B_PAB), GA[:, 1], ALU.mult).then_inc(acc_free[B_PAB % 2], 1)
                for q in range(4, 8):
                    split_lo(dve, i, 8, H_PAB + q + 2)
                dve.wait_ge(half_done, i * 8 + (H_PAB + 8))
                dve.tensor_tensor(MU, acc(B_PAB + 1), GA[:, 0], ALU.mult).then_inc(acc_free[(B_PAB + 1) % 2], 1)
                dve.drain()
                dve.tensor_tensor(SRC[:, :, ds(i * NB, NB)], MT, MU, ALU.add).then_inc(m_done, 1)
                dve.drain()

            gated(0, True)
            with dve.Fori(1, 4) as i:
                gated(i, False)
            for g in range(8):
                take_lo(dve, G_M + g, 2 * g)
            with dve.Fori(0, 2) as i:
                for b in range(2):
                    split_lo_block(i, 16, H_OUT + 8 * b)
            dve.wait_ge(o_bc, 64)
            dve.tensor_tensor(GB[:, 0], GB[:, 0], GB[:, 1], ALU.add)
            dve.drain()
            dve.tensor_tensor(GB[:, 0], GB[:, 0], GB[:, 2], ALU.mult)
            dve.drain()
            dve.wait_ge(o_sq, 1)
            dve.tensor_reduce(MSQ, SQ, AX.X, ALU.add)
            dve.drain()
            dve.tensor_scalar(MSQ, MSQ, 1.0 / D, RMS_EPS, ALU.mult, ALU.add)
            dve.drain()
            rsqrt(RSTD, MSQ, RTMP)
            dve.tensor_copy(NMR, RSTD).then_inc(x_stat, 1)

            def gain_quarters(stage, dst, gain, bias):
                for q in range(4):
                    dve.wait_ge(x_norm_act, 4 * stage + q + 1)
                    ins = dve.tensor_tensor(quarter(dst, q), quarter(dst, q), bc(quarter(gain, q), TT), ALU.mult)
                    if q < 2:
                        ins.then_inc(x_gain, 1)
                    else:
                        dve.drain()
                        dve.tensor_tensor(quarter(XRES, q), quarter(XRES, q), bias(q), ALU.add).then_inc(x_own, 1)

            gain_quarters(0, SUM, GB[:, 0], lambda q: quarter(SUM, q))
            for g in range(8):
                take_lo(dve, G_X1 + g, 2 * g)

            def quarter_stats(n):
                for t in range(TT):
                    dve.bn_stats(STATS[:, t, n, :], quarter(SUM[:, t], n))

            def ffn(h0, blk, g0, n0, zeroed):
                def gate_up(i, per, h, b, n):
                    split_lo_block(i, per, h)
                    dve.wait_ge(ff_sig, i + n)
                    dve.tensor_tensor(GS, acc(b), SIG, ALU.mult).then_inc(acc_free[b % 2], 1)
                    split_lo_block(i, per, h + 8)
                    dve.wait_ge(half_done, i * per + (h + 16))
                    dve.tensor_tensor(HID, acc(b + 1), GS, ALU.mult).then_inc(acc_free[(b + 1) % 2], 1)

                def hidden_lo(i, g):
                    for j in range(2):
                        dve.wait_ge(tp_hi, i * 2 + (g + j + 1))
                        dve.tensor_tensor(glo[:, 2 * j:2 * j + 2, :], tp(j).rearrange("p (k t) -> p k t", k=2),
                                          ghi[:, 2 * j:2 * j + 2, :].bitcast(F32), ALU.subtract).then_inc(tp_lo, 1)

                def down(i, per, h, b, last=False):
                    for n in range(4):
                        split_lo(dve, i, per, h + 2 * n + 2)
                        split_lo(dve, i, per, h + 2 * n + 3)
                        dve.wait_ge(half_done, i * per + (h + 2 * n + 2))
                        part = SUM[:, :, n * NB:(n + 1) * NB]
                        dve.tensor_tensor(part, part, acc(b + n), ALU.add).then_inc(acc_free[(b + n) % 2], 1)
                        if last:
                            dve.drain()
                            quarter_stats(n)

                gate_up(0, 0, h0, blk, n0 + 1)
                hidden_lo(0, g0)
                dve.wait_ge(ff_zero, zeroed)
                with dve.Fori(0, FB - 1) as i:
                    gate_up(i, 24, h0 + 16, blk + 2, n0 + 2)
                    down(i, 24, h0 + 32, blk + 4)
                    hidden_lo(i, g0 + 2)
                down(0, 0, h0 + 24 * FB - 8, blk + 6 * FB - 4, True)

            def layer_norm(stage, eps):
                dve.drain()
                for t in range(TT):
                    dve.bn_aggr(MV[:, t, :], STATS[:, t])
                dve.drain()
                dve.tensor_scalar(MSQ, MV[:, :, 1], eps, None, ALU.add)
                dve.drain()
                rsqrt(RSTD, MSQ, RTMP)
                dve.scalar_tensor_tensor(NMR, MV[:, :, 0], -1.0, RSTD, ALU.mult, ALU.mult).then_inc(x_stat, 1)
                dve.wait_ge(n_bc, 32 * stage)
                gain_quarters(stage, XRES, NG[:, 0], lambda q: bc(quarter(NG[:, 1], q), TT))

            ffn(H_FFN1, B_FFN1, G_FFN1, 0, 1)
            layer_norm(1, 4.0 * LN_EPS)
            for g in range(8):
                take_lo(dve, G_X2 + g, 2 * g)
            with dve.Fori(0, 2) as i:
                for b in range(2):
                    split_lo_block(i, 16, H_IN2 + 8 * b)

            def splits(m, end):
                for h in range(m, end):
                    split_lo(dve, 0, 0, H_HY + h + 2)

            def hyena_input(u, m0):
                m1 = HY_PARTS[u]
                splits(m0, m1)
                dve.wait_ge(hy_in, 64 * (u + 1))
                for s in range(3):
                    dve.tensor_tensor(HL[:, s], HL[:, s], bc(HW[:, s, :], TT), ALU.mult)
                dve.drain()
                splits(m1, m1 + 1)
                z = HZ[:, u % 3]
                dve.tensor_tensor(z, HL[:, 0], HL[:, 1], ALU.add)
                dve.tensor_tensor(HL[:, 2], HL[:, 2], bc(HW[:, 3, :], TT), ALU.add)
                dve.drain()
                dve.tensor_tensor(z, z, HL[:, 2], ALU.add).then_inc(hy_z, 1)
                return m1 + 1

            def hyena_unit(u, m0):
                m1 = HY_UNITS[u]
                splits(m0, m1)
                dve.wait_ge(hy_f, u + 1)
                dve.wait_ge(hy_kin, 32 * (u + 1))
                re, im = ps[:, 4:6, :], ps[:, 6:8, :]
                dve.tensor_tensor(HY_[:, 0:2], re, HK[0], ALU.mult)
                splits(m1, m1 + 1)
                dve.tensor_tensor(HT[:, 0], im, HK[1], ALU.mult)
                dve.tensor_tensor(HY_[:, 2:4], re, HK[1], ALU.mult)
                splits(m1 + 1, m1 + 2)
                dve.tensor_tensor(HT[:, 1], im, HK[0], ALU.mult)
                dve.drain()
                dve.tensor_tensor(HY_[:, 0:2], HY_[:, 0:2], HT[:, 0], ALU.subtract)
                dve.tensor_tensor(HY_[:, 2:4], HY_[:, 2:4], HT[:, 1], ALU.add).then_inc(hy_m, 1)
                splits(m1 + 2, m1 + 4)
                dve.wait_ge(hy_i, u + 1)
                dst = HZ[:, 0] if u % 2 == 0 else SRC[:, :, u // 2 * NB:(u // 2 + 1) * NB]
                dve.tensor_tensor(dst, ps[:, 4:6, :], HZ[:, 1 + u % 2], ALU.mult).then_inc(hy_y, 1)
                dve.drain()
                return m1 + 4

            m = 0
            for cb in range(2):
                for part in range(3):
                    m = hyena_input(3 * cb + part, m)
                for n in range(2):
                    m = hyena_unit(2 * cb + n, m)
            splits(m, 64)
            for t in range(TT):
                for s in range(2):
                    dve.bn_stats(STATS[:, t, s, :], SRC[:, t, s * NB:(s + 1) * NB])
                dve.drain()
                dve.bn_aggr(MV[:, t, :], STATS[:, t, 0:2])
            dve.drain()
            dve.tensor_tensor(MSQ, MV[:, :, 0], MV[:, :, 0], ALU.mult)
            dve.drain()
            dve.tensor_tensor(MSQ, MSQ, MV[:, :, 1], ALU.add)
            dve.drain()
            dve.tensor_scalar(MSQ, MSQ, LN_EPS, None, ALU.add)
            dve.drain()
            rsqrt(RSTD, MSQ, RTMP)
            dve.wait_ge(hy_tab, 80)
            for t in range(TT):
                dve.scalar_tensor_tensor(SRC[:, t, 0:DA], SRC[:, t, 0:DA], RSTD[:, t:t + 1], HG, ALU.mult, ALU.mult)\
                   .then_inc(hy_g, 1)

            for g in range(4):
                take_lo(dve, G_Y2 + g, 2 * g)

            def splits(m, end):
                for h in range(m, end):
                    split_lo(dve, 0, 0, H_OUT2 + h + 2)

            splits(0, 2)
            for n in range(2):
                dve.wait_ge(acc_free[n], (B_OUT2 - n + 1) // 2)
            dve.wait_ge(at_in, 48)
            for n, x in enumerate((AQ, AK)):
                g = x.rearrange("p t (g e) -> p t g e", e=64)
                a, b = g[:, :, :, 0:8], g[:, :, :, 8:16]
                cos, sin = (ROPE[:, s].unsqueeze(2).to_broadcast([P, TT, 16, 8]) for s in range(2))
                tmp = [RT[:, s].rearrange("p t (g e) -> p t g e", e=8) for s in range(4)]
                for dst, src, tab in ((tmp[0], a, cos), (tmp[1], b, sin), (tmp[2], b, cos), (tmp[3], a, sin)):
                    dve.tensor_tensor(dst, src, tab, ALU.mult)
                dve.drain()
                dve.tensor_tensor(a, tmp[0], tmp[1], ALU.subtract)
                dve.tensor_tensor(b, tmp[2], tmp[3], ALU.add).then_inc(at_rope, 1)
                dve.drain()
                splits(2 + n, 3 + n)
            for n in range(2):
                dve.tensor_tensor(RT[:, n, 0, 0:64], LAM[:, 2 * n], LAM[:, 2 * n + 1], ALU.mult)
            dve.drain()
            dve.tensor_reduce(AST[:, 0:2], RT[:, 0:2, 0, 0:64], AX.X, ALU.add).then_inc(at_lam, 1)
            dve.wait_ge(at_le, 1)
            dve.scalar_tensor_tensor(AST[:, 4:5], AST[:, 2:3], LAMBDA_INIT, AST[:, 3:4], ALU.add, ALU.subtract)
            dve.tensor_scalar(SUBG, SUBG, 1.0 - LAMBDA_INIT, None, ALU.mult)
            dve.drain()

            def maxima(h):
                dve.wait_ge(at_s, h + 1)
                n = 8 + 4 * h
                dve.tensor_reduce(AST[:, n:n + 4], ps[:, 4:6, :]
                                  .rearrange("p m (t k) -> p (m t) k", t=TT), AX.X, ALU.max)
                dve.drain()
                dve.tensor_scalar(AST[:, n:n + 4], AST[:, n:n + 4], -0.125, None, ALU.mult).then_inc(at_max, 1)

            maxima(0)
            for h in range(8):
                dve.wait_ge(at_e, h + 1)
                n = 40 + 4 * h
                dve.reciprocal(AST[:, 72:76], AST[:, n:n + 4])
                dve.drain()
                dve.tensor_scalar(AST[:, 76:78], AST[:, 74:76], AST[:, 4:5], None, ALU.mult)
                dve.drain()
                if h:
                    dve.wait_ge(at_wt, h)
                for t in range(TT):
                    dve.tensor_scalar(EE[:, 1, t, :], EE[:, 1, t, :], AST[:, 76 + t:77 + t], None, ALU.mult)
                dve.drain()
                for t in range(TT):
                    ins = dve.scalar_tensor_tensor(WW[:, t, :], EE[:, 0, t, :], AST[:, 72 + t:73 + t], EE[:, 1, t, :],
                                                   ALU.mult, ALU.subtract)
                ins.then_inc(at_w, 1)
                if h < 7:
                    maxima(h + 1)
                splits(4 + h, 5 + h)
            splits(12, 13)
            dve.wait_ge(at_oe, 8)
            dve.tensor_tensor(AO2, AO, AO, ALU.mult)
            dve.drain()
            dve.tensor_reduce(AMS, AO2.rearrange("p t (h n) -> p (t h) n", n=P), AX.X, ALU.add)
            dve.drain()
            dve.tensor_scalar(AMS, AMS, 1.0 / P, LN_EPS, ALU.mult, ALU.add)
            dve.drain()
            splits(13, 14)
            rsqrt(ARS, AMS, AST[:, 80:96])
            splits(14, 15)
            for t in range(TT):
                ao = AO[:, t, :].rearrange("p (h n) -> p h n", n=P)
                dve.tensor_tensor(ao, ao, bcl(ARS[:, 8 * t:8 * t + 8], P), ALU.mult)
                dve.drain()
                dve.tensor_tensor(ao, ao, bc(SUBG, 8), ALU.mult).then_inc(at_g, 1)
            splits(15, 16)
            for g in range(4, 8):
                take_lo(dve, G_Y2 + g, 2 * g)
            dve.wait_ge(x_scaled, 1)
            for n in range(4):
                h0 = H_OUT2 + 16 + 4 * n
                for q in range(4):
                    split_lo(dve, 0, 0, h0 + q + 2)
                    if q == 2 and n:
                        quarter_stats(n - 1)
                dve.wait_ge(half_done, h0 + 4)
                part = quarter(SUM, n)
                dve.tensor_tensor(part, part, acc(B_OUT2 + 4 + n), ALU.add).then_inc(acc_free[(B_OUT2 + n) % 2], 1)
                dve.drain()
                dve.tensor_tensor(part, part, quarter(XRES, n), ALU.add)
                dve.drain()
            quarter_stats(3)
            layer_norm(2, LN_EPS)
            for g in range(8):
                take_lo(dve, G_X3 + g, 2 * g)
            ffn(H_FFN2, B_FFN2, G_FFN2, FB, 2)
            layer_norm(3, 4.0 * LN_EPS)



def constants():
    t = np.arange(T)
    theta = 2.0 * np.pi * (np.arange(T) + 0.5) / (2 * T)
    ang = np.outer(t, theta)
    dft = np.stack([np.cos(ang), -np.sin(ang), np.cos(ang).T / T, -np.sin(ang).T / T])
    bands = 16
    lin = np.linspace(0.0, 1.0, T, dtype=np.float32)[:, None]
    w = (2.0 * np.pi * np.arange(T)[:, None] / T).astype(np.float32)
    f = np.linspace(1e-4, bands - 1, bands, dtype=np.float32)[None, :]
    fw = (f * w).astype(np.float64)
    z = np.concatenate([lin, np.cos(fw), -np.sin(fw)], axis=-1)
    lo, hi = math.log(1e-2) / 1.5, math.log(1e-2) / 0.3
    deltas = np.abs(np.linspace(lo, hi, DA))
    decay = np.exp(-lin.astype(np.float64) * deltas)
    back = decay.copy()
    back[0] = 0.0
    inv = 500000.0 ** (-np.arange(0, 16, 2) / 16.0)
    pos = np.outer(t, inv.astype(np.float32))
    p = np.arange(P)
    same = p[:, None] // CH == p[None, :] // CH
    before = same & (p[:, None] < p[None, :])
    upto = same & (p[:, None] <= p[None, :])
    levels = []
    for s in (1, 2, 4, 8, 16, 32):
        pair = p[:, None] // (2 * s) == p[None, :] // (2 * s)
        levels.append(pair & (p[:, None] // s % 2 == 0) & (p[None, :] // s % 2 == 1))
    steps = np.zeros((P, P))
    steps[p, p // CH] = 1.0
    masks = [before, upto, before, upto, before.T] + levels[1:] + [levels[0].T, levels[0], steps]
    return {
        "ident": np.eye(P), "dft": dft, "hy_zt": z.T, "hy_decay": np.stack([decay, back]),
        "rope": np.stack([np.cos(pos), np.sin(pos)]), "masks": np.stack(masks, axis=1),
        "zeros": np.zeros((1, N_IN)),
    }


def kernel(**inputs):
    import concourse.bacc as _bacc
    from concourse.bass_utils import run_bass_kernel_spmd as _run

    g = {n: np.asarray(a) for n, a in inputs.items()}
    arrays = {}
    for n in ("x", "c", "ada_b", "pre_gain", "post_gain", "ln1_g_2", "ln1_b_2", "ln2_g_2", "ln2_b_2", "ln3_g_2",
              "ln3_b_2", "hyena_norm_g_2", "subln_g_2"):
        arrays[n] = g[n]
    for n in ("ada_w", "w_in", "p_a", "p_b", "w_out", "ffn1_w_gate_2", "ffn1_w_up_2", "ffn1_w_down_2", "w_in_2",
              "w_out_2", "ffn2_w_gate_2", "ffn2_w_up_2", "ffn2_w_down_2", "conv_w", "filt_w1_2", "filt_w2_2",
              "filt_w3_2", "filt_w_out_2", "hyena_bias_2"):
        arrays[n] = g[n][0]
    mu = g["mu_shift"][0]
    arrays["mu_lora"] = mu[None, 3 * DA:]
    arrays["wkv_rows"] = np.stack([mu[0:DA], mu[DA:2 * DA], mu[2 * DA:3 * DA], g["k_k"][0], g["k_a"][0],
                                   g["r_k"][0].reshape(DA), g["lnx_gain"][0], g["lnx_bias"][0]])
    arrays["lora_w"] = np.stack([np.concatenate([g["w2"][0], g["w0"]]), np.concatenate([g["a2"][0], g["a0"]])])
    arrays["filt_cols"] = np.stack([g["filt_b1_2"][0], g["filt_b2_2"][0], g["filt_b3_2"][0], g["filt_freq_2"][0]],
                                   axis=1)
    arrays["hyena_rows"] = np.concatenate([g["hyena_conv_w_2"][0], g["hyena_conv_b_2"]])
    arrays["lambdas"] = np.concatenate([g["lambda_q1_2"], g["lambda_k1_2"], g["lambda_q2_2"], g["lambda_k2_2"]])
    for n, a in constants().items():
        arrays[n] = a.astype(np.float32)
    arrays = {f"in_{n}": np.ascontiguousarray(a) for n, a in arrays.items()}

    nc = _bacc.Bacc("TRN2", target_bir_lowering=False, num_devices=1)
    aps = {n[3:]: nc.dram_tensor(n, a.shape, F32, kind="ExternalInput").ap() for n, a in arrays.items()}
    out = nc.dram_tensor("out", (1, T, D), F32, kind="ExternalOutput").ap()
    with nc.allow_non_contiguous_dma(reason="short rows of parameters"):
        build(nc, aps, out)
    r = _run(nc, [arrays], core_ids=[0])
    return r.results[0]["out"]
```
